# Optimizing a Trainium2 kernel written in Bass

```python
import jax, jax.numpy as jnp
from jax import lax
import numpy as np

D_MODEL = 1024
BATCH = 1
SEQ = 1024
DEPTH = 1
DEC_BATCH = 1
DEC_SEQ = 2048
PAST_LEN = 128

D_INNER = 2 * D_MODEL
D_SSD = D_INNER // 2
D_ATTN = D_INNER - D_SSD
HEAD_DIM = 64
N_ATTN_HEADS = D_ATTN // HEAD_DIM
SSD_HEAD_DIM = 64
N_SSD_HEADS = D_SSD // SSD_HEAD_DIM
SSD_GROUPS = 2
D_STATE = 128
CONV_WIDTH = 5
CHUNK = 128
ROPE_THETA = 10000.0
EPS = 1e-5
DT_MIN = 0.001
DT_MAX = 0.1
DILATED_PATTERNS = ((128, 1), (512, 4), (2048, 16))
D_XBC = D_SSD + 2 * SSD_GROUPS * D_STATE
PROJ_SIZES = (D_ATTN, D_ATTN, D_ATTN, D_ATTN, D_SSD, D_XBC, N_SSD_HEADS, N_SSD_HEADS)
D_PROJ = 4 * D_ATTN + D_SSD + D_XBC + 2 * N_SSD_HEADS

kernel_name = 'hybrid_ssd_dilated_attn_encoder'

def rms_norm(x, g):
    xf = x.astype(jnp.float32)
    xf = xf * lax.rsqrt(jnp.mean(xf * xf, axis=-1, keepdims=True) + EPS)
    return (xf * g.astype(jnp.float32)).astype(x.dtype)

def rotary(t):
    s_len, dh = t.shape[1], t.shape[-1]
    half = dh // 2
    inv = ROPE_THETA ** (-jnp.arange(half, dtype=jnp.float32) * 2.0 / dh)
    ang = jnp.arange(s_len, dtype=jnp.float32)[:, None] * inv[None, :]
    cos = jnp.cos(ang)[None, :, None, :]
    sin = jnp.sin(ang)[None, :, None, :]
    t1, t2 = t[..., :half], t[..., half:]
    return jnp.concatenate([t1 * cos - t2 * sin, t2 * cos + t1 * sin], axis=-1)

def dilated_window_attention(q, k, v, window, dilation):
    b, s_len, h, dh = q.shape
    r = window // (2 * dilation)
    l_sub = s_len // dilation
    n = b * dilation

    def to_sub(t):
        return t.reshape(b, l_sub, dilation, h, dh).transpose(0, 2, 1, 3, 4).reshape(n, l_sub, h, dh)

    qs, ks, vs = to_sub(q), to_sub(k), to_sub(v)
    nb = -(-l_sub // r)
    lp = nb * r
    qb = jnp.pad(qs, ((0, 0), (0, lp - l_sub), (0, 0), (0, 0))).reshape(n, nb, r, h, dh)
    kpad = ((0, 0), (r, lp - l_sub + r), (0, 0), (0, 0))
    kp = jnp.pad(ks, kpad).reshape(n, nb + 2, r, h, dh)
    vp = jnp.pad(vs, kpad).reshape(n, nb + 2, r, h, dh)
    kw = jnp.concatenate([kp[:, :-2], kp[:, 1:-1], kp[:, 2:]], axis=2)
    vw = jnp.concatenate([vp[:, :-2], vp[:, 1:-1], vp[:, 2:]], axis=2)
    scores = jnp.einsum('nbqhd,nbkhd->nbhqk', qb, kw) * (HEAD_DIM ** -0.5)
    qi = jnp.arange(nb)[:, None] * r + jnp.arange(r)[None, :]
    ki = jnp.arange(nb)[:, None] * r - r + jnp.arange(3 * r)[None, :]
    valid = ((jnp.abs(qi[:, :, None] - ki[:, None, :]) <= r)
             & (ki[:, None, :] >= 0) & (ki[:, None, :] < l_sub))
    scores = jnp.where(valid[None, :, None], scores, -jnp.inf)
    lse = jax.nn.logsumexp(scores, axis=-1)
    p = jnp.exp(scores - lse[..., None])
    o = jnp.einsum('nbhqk,nbkhd->nbqhd', p, vw)
    o = o.reshape(n, lp, h, dh)[:, :l_sub]
    lse = lse.transpose(0, 1, 3, 2).reshape(n, lp, h)[:, :l_sub]
    o = o.reshape(b, dilation, l_sub, h, dh).transpose(0, 2, 1, 3, 4).reshape(b, s_len, h, dh)
    lse = lse.reshape(b, dilation, l_sub, h).transpose(0, 2, 1, 3).reshape(b, s_len, h)
    return o, lse

def dilated_mixture(q, k, v):
    outs, lses = [], []
    for window, dilation in DILATED_PATTERNS:
        o, lse = dilated_window_attention(q, k, v, window, dilation)
        outs.append(o)
        lses.append(lse)
    w = jax.nn.softmax(jnp.stack(lses, axis=0), axis=0)
    return jnp.sum(w[..., None] * jnp.stack(outs, axis=0), axis=0)

def depthwise_conv_centered(u, w, bias):
    pad = (CONV_WIDTH - 1) // 2
    out = lax.conv_general_dilated(u, w[:, None, :], window_strides=(1,), padding=[(pad, pad)],
                                   dimension_numbers=('NWC', 'WIO', 'NWC'),
                                   feature_group_count=u.shape[-1])
    return out + bias

def ssd_scan(x, dt_raw, b_mat, c_mat, a_log, dt_bias):
    bsz, s_len, h, p = x.shape
    g, nst = b_mat.shape[2], b_mat.shape[3]
    e = h // g
    nc = s_len // CHUNK
    dt = jax.nn.softplus(dt_raw + dt_bias)
    a = dt * (-jnp.exp(a_log))
    xc = (x * dt[..., None]).reshape(bsz, nc, CHUNK, g, e, p)
    ac = a.reshape(bsz, nc, CHUNK, g, e)
    bc = b_mat.reshape(bsz, nc, CHUNK, g, nst)
    cc = c_mat.reshape(bsz, nc, CHUNK, g, nst)
    acum = jnp.cumsum(ac, axis=2)
    seg = acum[:, :, :, None] - acum[:, :, None, :]
    tril = jnp.tril(jnp.ones((CHUNK, CHUNK), dtype=bool))[:, :, None, None]
    lmat = jnp.exp(jnp.where(tril, seg, -jnp.inf))
    cb = jnp.einsum('bclgn,bcsgn->bclsg', cc, bc)
    y_diag = jnp.einsum('bclsge,bcsgep->bclgep', cb[..., None] * lmat, xc)
    decay_to_end = jnp.exp(acum[:, :, -1:] - acum)
    states = jnp.einsum('bcsgn,bcsgep->bcgepn', bc, decay_to_end[..., None] * xc)
    chunk_decay = jnp.exp(acum[:, :, -1])

    def step(carry, inp):
        st, dec = inp
        return carry * dec[..., None, None] + st, carry

    init = jnp.zeros((bsz, g, e, p, nst), dtype=x.dtype)
    _, states_in = lax.scan(step, init, (jnp.moveaxis(states, 1, 0), jnp.moveaxis(chunk_decay, 1, 0)))
    states_in = jnp.moveaxis(states_in, 0, 1)
    y_off = jnp.einsum('bclgn,bcgepn->bclgep', cc, states_in) * jnp.exp(acum)[..., None]
    return (y_diag + y_off).reshape(bsz, s_len, h, p)

def ssd_branch(z, xbc, dt_f, dt_b, conv_w, conv_b, dt_bias_fwd, dt_bias_bwd,
               a_log_fwd, a_log_bwd, d_skip, norm_ssd):
    bsz, s_len, _ = z.shape
    f32 = jnp.float32
    xbc = jax.nn.silu(depthwise_conv_centered(xbc.astype(f32), conv_w.astype(f32), conv_b.astype(f32)))
    xs = xbc[..., :D_SSD].reshape(bsz, s_len, N_SSD_HEADS, SSD_HEAD_DIM)
    b_mat = xbc[..., D_SSD:D_SSD + SSD_GROUPS * D_STATE].reshape(bsz, s_len, SSD_GROUPS, D_STATE)
    c_mat = xbc[..., D_SSD + SSD_GROUPS * D_STATE:].reshape(bsz, s_len, SSD_GROUPS, D_STATE)
    y_fwd = ssd_scan(xs, dt_f.astype(f32), b_mat, c_mat, a_log_fwd.astype(f32), dt_bias_fwd.astype(f32))
    fl = lambda t: jnp.flip(t, axis=1)
    y_bwd = fl(ssd_scan(fl(xs), fl(dt_b.astype(f32)), fl(b_mat), fl(c_mat),
                        a_log_bwd.astype(f32), dt_bias_bwd.astype(f32)))
    y = y_fwd + y_bwd + d_skip.astype(f32)[:, None] * xs
    y = y.reshape(bsz, s_len, D_SSD) * jax.nn.silu(z.astype(f32))
    return rms_norm(y, norm_ssd)

def attention_branch(q, k, v, z):
    bsz, s_len, _ = q.shape
    f32 = jnp.float32
    shp = (bsz, s_len, N_ATTN_HEADS, HEAD_DIM)
    qh = rotary(q.astype(f32).reshape(shp))
    kh = rotary(k.astype(f32).reshape(shp))
    vh = v.astype(f32).reshape(shp)
    o = dilated_mixture(qh, kh, vh).reshape(bsz, s_len, D_ATTN)
    return o * jax.nn.silu(z.astype(f32))

def encoder(x, w_in, conv_w, conv_b, dt_bias_fwd, dt_bias_bwd, a_log_fwd, a_log_bwd,
            d_skip, norm_ssd, norm_in, w_out, norm_f):
    split_at = [int(i) for i in np.cumsum(PROJ_SIZES)[:-1]]
    for layer in range(DEPTH):
        h = rms_norm(x, norm_in[layer])
        proj = h @ w_in[layer]
        q, k, v, z_attn, z_ssd, xbc, dt_f, dt_b = jnp.split(proj, split_at, axis=-1)
        y_ssd = ssd_branch(z_ssd, xbc, dt_f, dt_b, conv_w[layer], conv_b[layer],
                           dt_bias_fwd[layer], dt_bias_bwd[layer], a_log_fwd[layer],
                           a_log_bwd[layer], d_skip[layer], norm_ssd[layer])
        y_attn = attention_branch(q, k, v, z_attn)
        mix = jnp.concatenate([y_ssd.astype(x.dtype), y_attn.astype(x.dtype)], axis=-1)
        x = x + mix @ w_out[layer]
    return rms_norm(x, norm_f)

def setup_inputs(seed: int = 0) -> dict:
    key = jax.random.key(seed)
    ks = jax.random.split(key, 16)
    f32 = jnp.float32
    x_prompt = jax.random.normal(ks[0], (BATCH, SEQ, D_MODEL), f32)
    x_sample = jax.random.normal(ks[1], (DEC_BATCH, DEC_SEQ, D_MODEL), f32)
    w_in = jax.random.normal(ks[2], (DEPTH, D_MODEL, D_PROJ), f32) * D_MODEL ** -0.5
    conv_w = jax.random.normal(ks[3], (DEPTH, CONV_WIDTH, D_XBC), f32) * CONV_WIDTH ** -0.5
    conv_b = jax.random.normal(ks[4], (DEPTH, D_XBC), f32) * 0.02

    def dt_bias_init(k):
        u = jax.random.uniform(k, (DEPTH, N_SSD_HEADS), f32)
        dt = jnp.exp(u * (jnp.log(DT_MAX) - jnp.log(DT_MIN)) + jnp.log(DT_MIN))
        return dt + jnp.log(-jnp.expm1(-dt))

    dt_bias_fwd = dt_bias_init(ks[5])
    dt_bias_bwd = dt_bias_init(ks[6])
    a_log_fwd = jnp.log(jax.random.uniform(ks[7], (DEPTH, N_SSD_HEADS), f32, minval=1.0, maxval=16.0))
    a_log_bwd = jnp.log(jax.random.uniform(ks[8], (DEPTH, N_SSD_HEADS), f32, minval=1.0, maxval=16.0))
    d_skip = 1.0 + 0.1 * jax.random.normal(ks[9], (DEPTH, N_SSD_HEADS), f32)
    norm_ssd = 1.0 + 0.02 * jax.random.normal(ks[10], (DEPTH, D_SSD), f32)
    norm_in = 1.0 + 0.02 * jax.random.normal(ks[11], (DEPTH, D_MODEL), f32)
    w_out = jax.random.normal(ks[12], (DEPTH, D_INNER, D_MODEL), f32) * D_INNER ** -0.5
    norm_f = 1.0 + 0.02 * jax.random.normal(ks[13], (D_MODEL,), f32)
    return {'x_prompt': x_prompt, 'x_sample': x_sample, 'w_in': w_in, 'conv_w': conv_w,
            'conv_b': conv_b, 'dt_bias_fwd': dt_bias_fwd, 'dt_bias_bwd': dt_bias_bwd,
            'a_log_fwd': a_log_fwd, 'a_log_bwd': a_log_bwd, 'd_skip': d_skip,
            'norm_ssd': norm_ssd, 'norm_in': norm_in, 'w_out': w_out, 'norm_f': norm_f}

def reference(x_prompt, x_sample, w_in, conv_w, conv_b, dt_bias_fwd, dt_bias_bwd,
              a_log_fwd, a_log_bwd, d_skip, norm_ssd, norm_in, w_out, norm_f):
    y_prompt = encoder(x_prompt, w_in, conv_w, conv_b, dt_bias_fwd, dt_bias_bwd, a_log_fwd,
                       a_log_bwd, d_skip, norm_ssd, norm_in, w_out, norm_f)
    y_sample = encoder(x_sample, w_in, conv_w, conv_b, dt_bias_fwd, dt_bias_bwd, a_log_fwd,
                       a_log_bwd, d_skip, norm_ssd, norm_in, w_out, norm_f)
    return (y_prompt, y_sample)


_drawn_inputs = setup_inputs


def setup_inputs(seed=0):
    import zlib

    import numpy as np

    out = dict(_drawn_inputs(seed))
    spreads = {}
    factors = {'conv_b': 12.095, 'norm_ssd': 72.623, 'norm_in': 3.201, 'norm_f': 20.544, 'd_skip': 64.0}
    for name, (base, spread) in spreads.items():
        noise = np.random.default_rng([zlib.crc32(name.encode()), seed]).standard_normal(out[name].shape)
        drawn = base * np.exp(spread * noise) if base else spread * noise
        out[name] = __import__('jax').numpy.asarray(drawn.astype(out[name].dtype))
    for name, factor in factors.items():
        out[name] = (out[name] * factor).astype(out[name].dtype)
    return out
```

```python
import itertools
from contextlib import ExitStack

import numpy as np
import concourse.bass as bass
from concourse import mybir

F32 = mybir.dt.float32
F32R = mybir.dt.float32r
BF16 = mybir.dt.bfloat16
ALU = mybir.AluOpType
ACT = mybir.ActivationFunctionType
AX = mybir.AxisListType

P = 128
D = 1024
KT = D // P
SEQS = (1024, 2048)
TILES = tuple(s // P for s in SEQS)
NT = sum(TILES)
HEADS = 16
DH = 64
D_ATTN = HEADS * DH
D_SSD = 1024
GROUPS = 2
NST = 128
HG = HEADS // GROUPS
D_XBC = D_SSD + 2 * GROUPS * NST
D_PROJ = 4 * D_ATTN + D_SSD + D_XBC + 2 * HEADS
CW = 512
EPS = 1e-5
PAD = 256
KV_ROWS = PAD + SEQS[0] + PAD + SEQS[1] + PAD
KV_BASE = (PAD, PAD + SEQS[0] + PAD)
TOK_BASE = (0, SEQS[0])
VW = DH + 1
ds = bass.ds


class Core:

    def __init__(self, nc, stack, phase):
        self.nc, self.stack, self.phase = nc, stack, phase

    def sbuf(self, name, shape, dtype=F32):
        return self.stack.enter_context(self.nc.sbuf_tensor(f"{self.phase}_{name}", shape, dtype))

    def psum(self, name, shape, dtype=F32):
        return self.stack.enter_context(self.nc.psum_tensor(f"{self.phase}_{name}", shape, dtype))


def give_credit(nc, c, engine=None):
    col = next(c["credit_column"])
    return (engine or nc.gpsimd).memset(c["credit"][:, col:col + 1], 0.0)


def make_constants(nc, sem, c):
    with nc.Block() as block:
        @block.gpsimd
        def _(pool):
            nc.gpsimd.memset(c["ident"][:, :], 0.0).then_inc(sem["ident_zeroed"], 1)
            nc.gpsimd.memset(c["eps"][:, :], EPS)
            nc.gpsimd.memset(c["one"][:, :], 1.0)
            pool.wait_ge(sem["ident_zeroed"], 1)
            nc.gpsimd.affine_select(out=c["ident"][:, :], in_=c["ident"][:, :], compare_op=ALU.not_equal,
                                    fill=1.0, base=0, pattern=[[-1, P]], channel_multiplier=1)


def norm_phase(nc, sem, c, x_parts, norm_in, hT, scratch):
    with ExitStack() as stack:
        mem = Core(nc, stack, "norm")
        x_t = mem.sbuf("x_t", [P, 2, D])
        h_t = mem.sbuf("h_t", [P, 2, D])
        sq = mem.sbuf("sq", [P, D])
        gain = mem.sbuf("gain", [P, D])
        ssum = mem.sbuf("ssum", [P, 2])
        root = mem.sbuf("root", [P, 2])
        rinv = mem.sbuf("rinv", [P, 2])
        zero = mem.sbuf("zero", [P, HEADS * VW])
        tr = [mem.psum(f"tr{u}", [P, D]) for u in range(2)]
        block = stack.enter_context(nc.Block())
        parts = [(x, TOK_BASE[s] // P, TILES[s]) for s, x in enumerate(x_parts)]

        @block.sync
        def _(sp):
            sp.dma_start(gain[:, :], norm_in.to_broadcast([P, D])).then_inc(sem["gain_in"], 16)
            for x, first, tiles in parts:
                rows = x.rearrange("o (t u p) d -> (o t) u p d", u=2, p=P)
                with sp.Fori(0, tiles // 2) as i:
                    for u in range(2):
                        sp.wait_ge(sem["h_ready"], first + 2 * i + u + 1)
                        sp.dma_start(x_t[:, u, :], rows[ds(i, 1), u, :, :].rearrange("o p d -> p (o d)")
                                     ).then_inc(sem["x_in"][u], 16)
            sp.wait_ge(sem["zero_set"], 1)
            for row in (0, KV_BASE[1] - PAD, KV_ROWS - PAD):
                for half in range(PAD // P):
                    at = row + half * P
                    sp.dma_start(scratch["k"][at:at + P, :], zero[:, 0:D_ATTN]).then_inc(sem["pads_stored"], 16)
                    sp.dma_start(scratch["v"][at:at + P, :], zero[:, :]).then_inc(sem["pads_stored"], 16)
            sp.wait_ge(sem["pads_stored"], 16 * 2 * 3 * (PAD // P))

        @block.gpsimd
        def _(pool):
            nc.gpsimd.memset(zero[:, :], 0.0).then_inc(sem["zero_set"], 1)
            give_credit(nc, c).then_inc(sem["h_ready"], 2)
            give_credit(nc, c).then_inc(sem["tr_copied"], 2)

        @block.scalar
        def _(act):
            for x, first, tiles in parts:
                with act.Fori(0, tiles // 2) as i:
                    for u in range(2):
                        act.wait_ge(sem["x_in"][u], 16 * (first // 2 + i + 1))
                        nc.scalar.activation(sq[:, :], x_t[:, u, :], ACT.Square, accum_out=ssum[:, u:u + 1]
                                             ).then_inc(sem["ssum_ready"], 1)
                        act.wait_ge(sem["ssum_ready"], first + 2 * i + u + 1)
                        nc.scalar.activation(root[:, u:u + 1], ssum[:, u:u + 1], ACT.Sqrt, scale=1.0 / D,
                                             bias=c["eps"][:, :]).then_inc(sem["root_ready"], 1)
                        act.wait_ge(sem["tr_ready"], first + 2 * i + u + 1)
                        nc.scalar.copy(hT[:, ds(first + 2 * i + u, 1), :, :].rearrange("p o k t -> p (o k t)"),
                                       tr[u][:, :]).then_inc(sem["tr_copied"], 1)

        @block.vector
        def _(dve):
            dve.wait_ge(sem["gain_in"], 16)
            for x, first, tiles in parts:
                with dve.Fori(0, tiles // 2) as i:
                    for u in range(2):
                        dve.wait_ge(sem["root_ready"], first + 2 * i + u + 1)
                        nc.vector.reciprocal(rinv[:, u:u + 1], root[:, u:u + 1]).then_inc(sem["rinv_ready"], 1)
                        dve.wait_ge(sem["rinv_ready"], first + 2 * i + u + 1)
                        dve.wait_ge(sem["tr_copied"], first + 2 * i + u + 1)
                        nc.vector.scalar_tensor_tensor(h_t[:, u, :], x_t[:, u, :], rinv[:, u:u + 1], gain[:, :],
                                                       ALU.mult, ALU.mult).then_inc(sem["h_ready"], 1)

        @block.tensor
        def _(pe):
            for x, first, tiles in parts:
                with pe.Fori(0, tiles // 2) as i:
                    for u in range(2):
                        pe.wait_ge(sem["h_ready"], first + 2 * i + u + 3)
                        pe.wait_ge(sem["tr_copied"], first + 2 * i + u + 1)
                        for k in range(KT):
                            last = nc.tensor.transpose(tr[u][:, k * P:(k + 1) * P], h_t[:, u, k * P:(k + 1) * P],
                                                       c["ident"][:, :])
                        last.then_inc(sem["tr_ready"], 1)


def project_phase(nc, sem, c, w_in, rope, hT, scratch):
    groups = D_PROJ // CW
    dtw = D_PROJ - groups * CW
    with ExitStack() as stack:
        mem = Core(nc, stack, "project")
        w_raw = mem.sbuf("w_raw", [P, 2, 2, CW])
        w_hi = [mem.sbuf(f"w_hi{s}", [P, KT, CW], F32R) for s in range(2)]
        w_lo = [mem.sbuf(f"w_lo{s}", [P, KT, CW], F32R) for s in range(2)]
        h_hi = [mem.sbuf(f"h_hi{u}", [P, KT * P], F32R) for u in range(2)]
        h_lo = [mem.sbuf(f"h_lo{u}", [P, KT * P], F32R) for u in range(2)]
        stage = mem.sbuf("stage", [P, 2, CW])
        v_stage = mem.sbuf("v_stage", [P, 2, CW // DH, VW])
        turned = mem.sbuf("turned", [P, 2, CW])
        table = mem.sbuf("table", [P, NT, 3, DH // 2])
        out = [mem.psum(f"out{u}", [P, CW]) for u in range(2)]
        block = stack.enter_context(nc.Block())
        w_rows = w_in.rearrange("o (k p) n -> p (o k) n", p=P)

        kinds = [(0, 2, "rope", "q"), (2, 2, "rope", "k"), (4, 2, "v", "v"), (6, 2, "silu", "za"),
                 (8, 2, "silu", "zs"), (10, 3, "plain", "xbc"), (13, 1, "dt", "dt")]

        rope_groups = 4
        rotated_steps = rope_groups * NT

        def step(g, i, u):
            return g * NT + 2 * i + u

        @block.gpsimd
        def _(pool):
            nc.gpsimd.memset(v_stage[:, :, :, :], 1.0).then_inc(sem["ones_set"], 1)
            give_credit(nc, c).then_inc(sem["rotated"], 2)
            give_credit(nc, c).then_inc(sem["staged"], 2)
            give_credit(nc, c).then_inc(sem["w_split"], 1)
            for u in range(2):
                give_credit(nc, c).then_inc(sem["stored"][u], 16)

            one = c["one"][:, :].rearrange("p (a b) -> p a b", b=1)

            def load_and_split(g, s, cols, fresh=False):
                for piece in range(KT // 2):
                    b = piece % 2
                    pieces = g * (KT // 2) + piece
                    pool.wait_ge(sem["w_split"], pieces + 1)
                    pool.dma_start(w_raw[:, b, :, 0:cols], w_rows[:, 2 * piece:2 * piece + 2, ds(g * CW, cols)]
                                   ).then_inc(sem["w_in"][b], 16)
                    if piece == 0 and not fresh:
                        pool.wait_ge(sem["out_ready"], (g - 1) * NT)
                    pool.wait_ge(sem["w_in"][b], 16 * (g * (KT // 4) + piece // 2 + 1))
                    raw = w_raw[:, b, :, 0:cols]
                    nc.gpsimd.tensor_tensor(w_hi[s][:, 2 * piece:2 * piece + 2, 0:cols], raw,
                                            one.to_broadcast([P, 2, cols]), ALU.mult).then_inc(sem["w_hi_ready"], 1)
                    pool.wait_ge(sem["w_hi_ready"], pieces + 1)
                    nc.gpsimd.tensor_tensor(w_lo[s][:, 2 * piece:2 * piece + 2, 0:cols], w_raw[:, b, :, 0:cols],
                                            w_hi[s][:, 2 * piece:2 * piece + 2, 0:cols].bitcast(F32), ALU.subtract
                                            ).then_inc(sem["w_split"], 1)

            for s in range(2):
                load_and_split(s, s, CW, fresh=True)
            with pool.Fori(1, groups // 2) as j:
                for s in range(2):
                    load_and_split(2 * j + s, s, CW)
            load_and_split(groups - 1, 0, CW)
            load_and_split(groups, 1, dtw)

        def prepare(eng, n, t, u):
            src = hT[:, t, :, :].rearrange("p o k t -> p (o k t)")
            if eng is nc.scalar:
                nc.scalar.copy(h_hi[u][:, :], src).then_inc(sem["h_hi_ready"], 1)
            else:
                eng.wait_ge(sem["h_hi_ready"], n)
                nc.vector.tensor_tensor(h_lo[u][:, :], src, h_hi[u][:, :].bitcast(F32), ALU.subtract
                                        ).then_inc(sem["h_split"], 1)

        @block.scalar
        def _(act):
            for u in range(2):
                prepare(act, u + 1, ds(u, 1), u)
            act.wait_ge(sem["ones_set"], 1)

            def tile(g, i, u, kind, t_next):
                n = step(g, i, u)
                act.wait_ge(sem["out_ready"], n + 1)
                if kind != "rope":
                    act.wait_ge(sem["stored"][u], 16 * (g * (NT // 2) + i + 1))
                    src = out[u][:, :]
                    if kind == "v":
                        done = nc.scalar.copy(v_stage[:, u, :, 0:DH], src.rearrange("p (h d) -> p h d", d=DH))
                    elif kind == "silu":
                        done = nc.scalar.activation(stage[:, u, :], src, ACT.Silu)
                    elif kind == "plain":
                        done = nc.scalar.copy(stage[:, u, :], src)
                    else:
                        done = nc.scalar.copy(stage[:, u, 0:dtw], out[u][:, 0:dtw])
                    done.then_inc(sem["staged"], 1)
                prepare(nc.scalar, n + 3, t_next, u)

            for g0, count, kind, _name in kinds:
                with act.Fori(g0, g0 + count) as g:
                    with act.Fori(0, NT // 2 - 1) as i:
                        for u in range(2):
                            tile(g, i, u, kind, ds(2 * i + 2 + u, 1))
                    for u in range(2):
                        tile(g, NT // 2 - 1, u, kind, ds(u, 1))

        @block.vector
        def _(dve):
            for u in range(2):
                prepare(dve, u + 1, ds(u, 1), u)
            dve.wait_ge(sem["rope_in"], 16)

            def tile(g, i, u, kind, t_next):
                n = step(g, i, u)
                if kind == "rope":
                    dve.wait_ge(sem["out_ready"], n + 1)
                    dve.wait_ge(sem["stored"][u], 16 * (g * (NT // 2) + i + 1))
                    t = ds(2 * i + u, 1)
                    cos = table[:, t, 0, :].to_broadcast([P, CW // (DH // 2), DH // 2])
                    sines = table[:, t, 1:3, :].to_broadcast([P, CW // DH, 2, DH // 2])
                    halves = out[u][:, :].rearrange("p (h a d) -> p h a d", a=2, d=DH // 2)
                    nc.vector.tensor_tensor(stage[:, u, :].rearrange("p (h d) -> p h d", d=DH // 2),
                                            out[u][:, :].rearrange("p (h d) -> p h d", d=DH // 2), cos, ALU.mult)
                    nc.vector.tensor_tensor(turned[:, u, :].rearrange("p (h a d) -> p h a d", a=2, d=DH // 2),
                                            halves[:, :, ::-1, :], sines, ALU.mult).then_inc(sem["turned"], 1)
                    dve.wait_ge(sem["turned"], n + 1)
                    nc.vector.tensor_tensor(stage[:, u, :], stage[:, u, :], turned[:, u, :], ALU.add
                                            ).then_inc(sem["rotated"], 1)
                prepare(dve, n + 3, t_next, u)

            for g0, count, kind, _name in kinds:
                with dve.Fori(g0, g0 + count) as g:
                    with dve.Fori(0, NT // 2 - 1) as i:
                        for u in range(2):
                            tile(g, i, u, kind, ds(2 * i + 2 + u, 1))
                    for u in range(2):
                        tile(g, NT // 2 - 1, u, kind, ds(u, 1))

        @block.tensor
        def _(pe):
            def tile(g, i, u, s, cols, rope):
                n = step(g, i, u)
                pe.wait_ge(sem["w_split"], (g + 1) * (KT // 2) + 1)
                pe.wait_ge(sem["h_split"], n + 1)
                pe.wait_ge(sem["rotated"], n + 1 if rope else rotated_steps + 2)
                if not rope:
                    pe.wait_ge(sem["staged"], n - rotated_steps + 1)
                last = None
                for a, b in ((h_hi, w_hi), (h_hi, w_lo), (h_lo, w_hi)):
                    for k in range(KT):
                        first = last is None
                        stop = a is h_lo and k == KT - 1
                        last = nc.tensor.matmul(out[u][:, 0:cols], a[u][:, k * P:(k + 1) * P], b[s][:, k, 0:cols],
                                                start=first, stop=stop)
                last.then_inc(sem["out_ready"], 1)

            def group(g, s, cols, rope=False):
                with pe.Fori(0, NT // 2) as i:
                    for u in range(2):
                        tile(g, i, u, s, cols, rope)

            for j0, j1, rope in ((0, rope_groups // 2, True), (rope_groups // 2, groups // 2, False)):
                with pe.Fori(j0, j1) as j:
                    for s in range(2):
                        group(2 * j + s, s, CW, rope)
            group(groups - 1, 0, CW)
            group(groups, 1, dtw)

        @block.sync
        def _(sp):
            sp.dma_start(table[:, :, :, :], rope).then_inc(sem["rope_in"], 16)
            for g0, count, kind, name in kinds:
                padded = name in ("k", "v")
                with sp.Fori(g0, g0 + count) as g:
                    for seq in range(2):
                        half0 = TOK_BASE[seq] // P // 2
                        row0 = KV_BASE[seq] if padded else TOK_BASE[seq]
                        rows = scratch[name][row0:row0 + SEQS[seq], :].rearrange("(t u p) n -> t u p n", u=2, p=P)
                        with sp.Fori(0, TILES[seq] // 2) as i:
                            for u in range(2):
                                n = step(g, half0 + i, u)
                                if kind == "rope":
                                    sp.wait_ge(sem["rotated"], n + 3)
                                else:
                                    sp.wait_ge(sem["staged"], n - rotated_steps + 3)
                                if kind == "v":
                                    width, src = CW // DH * VW, v_stage[:, u, :, :].rearrange("p h d -> p (h d)")
                                elif kind == "dt":
                                    width, src = dtw, stage[:, u, 0:dtw]
                                else:
                                    width, src = CW, stage[:, u, :]
                                dst = rows[ds(i, 1), u, :, ds((g - g0) * width, width)]
                                sp.dma_start(dst.rearrange("o p n -> p (o n)"), src).then_inc(sem["stored"][u], 16)
            total = 16 * (1 + (groups + 1) * (NT // 2))
            for u in range(2):
                sp.wait_ge(sem["stored"][u], total)


def conv_phase(nc, sem, c, conv_w, conv_b, scratch):
    chan_tiles = D_XBC // P
    x_tiles, b_end = D_SSD // P, (D_SSD + GROUPS * NST) // P
    taps = 5
    halo = taps // 2
    quads = tuple(t // 4 for t in TILES)
    quad0 = (0, quads[0])
    per_ct = sum(quads)
    with ExitStack() as stack:
        mem = Core(nc, stack, "conv")
        rows = mem.sbuf("rows", [taps * chan_tiles + chan_tiles, P])
        consts = mem.sbuf("consts", [P, (taps + 1) * chan_tiles])
        raw = [mem.sbuf(f"raw{s}", [P, TILES[s], P]) for s in range(2)]
        chan = [mem.sbuf(f"chan{s}", [P, SEQS[s] + 2 * halo]) for s in range(2)]
        acc = [mem.sbuf(f"acc{s}", [P, SEQS[s]]) for s in range(2)]
        done = [mem.sbuf(f"done{s}", [P, SEQS[s]]) for s in range(2)]
        toks = [mem.sbuf(f"toks{s}", [P, TILES[s], P]) for s in range(2)]
        turn_in = [mem.psum(f"turn_in{b}", [P, 4 * P]) for b in range(2)]
        turn_back = [mem.psum(f"turn_back{b}", [P, 4 * P]) for b in range(2)]
        turn_consts = mem.psum("turn_consts", [P, (taps + 1) * chan_tiles])
        block = stack.enter_context(nc.Block())

        def seq_rows(name, s):
            return scratch[name][TOK_BASE[s]:TOK_BASE[s] + SEQS[s], :].rearrange("(t p) n -> p t n", p=P)

        def kind(ct):
            return "x" if not isinstance(ct, int) or ct < x_tiles else ("B" if ct < b_end else "C")

        @block.gpsimd
        def _(pool):
            for s in range(2):
                nc.gpsimd.memset(chan[s][:, 0:halo], 0.0).then_inc(sem["halo_set"], 1)
                nc.gpsimd.memset(chan[s][:, halo + SEQS[s]:2 * halo + SEQS[s]], 0.0).then_inc(sem["halo_set"], 1)
            give_credit(nc, c).then_inc(sem["conv_turned"], per_ct)
            give_credit(nc, c).then_inc(sem["conv_copied"], 2)
            give_credit(nc, c).then_inc(sem["conv_done"], 2)
            give_credit(nc, c).then_inc(sem["silu_done"], 2)
            give_credit(nc, c).then_inc(sem["back_turned"], per_ct)
            give_credit(nc, c).then_inc(sem["back_copied"], 2)
            for s in range(2):
                give_credit(nc, c).then_inc(sem["toks_stored"][s], 16)

        @block.sync
        def _(sp):
            sp.dma_start(rows[0:taps * chan_tiles, :], conv_w.rearrange("o k (c p) -> (o k c) p", p=P)
                         ).then_inc(sem["rows_in"], 16)
            sp.dma_start(rows[taps * chan_tiles:, :], conv_b.rearrange("o (c p) -> (o c) p", p=P)
                         ).then_inc(sem["rows_in"], 16)

            def load(ct, s):
                sp.wait_ge(sem["conv_turned"], ct * per_ct + quad0[s] + quads[s])
                sp.dma_start(raw[s][:, :, :], seq_rows("xbc", s)[:, :, ds(ct * P, P)]
                             ).then_inc(sem["raw_in"][s], 16)

            def store(ct, s):
                if kind(ct) != "C":
                    sp.wait_ge(sem["back_copied"], ct * per_ct + quad0[s] + quads[s] + 2)
                    sp.dma_start(seq_rows("xb", s)[:, :, ds(ct * P, P)], toks[s][:, :, :]
                                 ).then_inc(sem["toks_stored"][s], 16)
                if kind(ct) != "x":
                    sp.wait_ge(sem["silu_done"], 2 * ct + s + 1 + 2)
                    sp.dma_start(scratch["bct"][(ct - x_tiles) * P:(ct - x_tiles + 1) * P,
                                                TOK_BASE[s]:TOK_BASE[s] + SEQS[s]], done[s][:, :]
                                 ).then_inc(sem["chans_stored"][s], 16)

            for s in range(2):
                load(0, s)
            with sp.Fori(0, x_tiles) as ct:
                for s in range(2):
                    load(ct + 1, s)
                    store(ct, s)
            for ct in range(x_tiles, chan_tiles):
                for s in range(2):
                    if ct + 1 < chan_tiles:
                        load(ct + 1, s)
                    store(ct, s)
            for s in range(2):
                sp.wait_ge(sem["toks_stored"][s], 16 * (b_end + 1))
                sp.wait_ge(sem["chans_stored"][s], 16 * (chan_tiles - x_tiles))

        @block.tensor
        def _(pe):
            pe.wait_ge(sem["rows_in"], 32)
            n = (taps + 1) * chan_tiles
            nc.tensor.transpose(turn_consts[:, :], rows[:, :], c["ident"][0:n, 0:n]).then_inc(sem["consts_turned"], 1)

            def turn(ct, s):
                pe.wait_ge(sem["raw_in"][s], 16 * (ct + 1))
                for q in range(quads[s]):
                    number = ct * per_ct + quad0[s] + q
                    b = (quad0[s] + q) % 2
                    pe.wait_ge(sem["conv_copied"], number + 1)
                    for j in range(4):
                        last = nc.tensor.transpose(turn_in[b][:, j * P:(j + 1) * P], raw[s][:, 4 * q + j, :],
                                                   c["ident"][:, :])
                    last.then_inc(sem["conv_turned"], 1)

            def turn_to_tokens(ct, s):
                pe.wait_ge(sem["silu_done"], 2 * ct + s + 1 + 2)
                for q in range(quads[s]):
                    number = ct * per_ct + quad0[s] + q
                    b = (quad0[s] + q) % 2
                    pe.wait_ge(sem["back_copied"], number + 1)
                    for j in range(4):
                        at = (4 * q + j) * P
                        last = nc.tensor.transpose(turn_back[b][:, j * P:(j + 1) * P], done[s][:, at:at + P],
                                                   c["ident"][:, :])
                    last.then_inc(sem["back_turned"], 1)

            def body(ct, more=True):
                turn(ct, 1)
                if kind(ct) != "C":
                    turn_to_tokens(ct, 0)
                if more:
                    turn(ct + 1, 0)
                if kind(ct) != "C":
                    turn_to_tokens(ct, 1)

            turn(0, 0)
            with pe.Fori(0, x_tiles) as ct:
                body(ct)
            for ct in range(x_tiles, chan_tiles):
                body(ct, ct + 1 < chan_tiles)

        @block.scalar
        def _(act):
            act.wait_ge(sem["consts_turned"], 1)
            nc.scalar.copy(consts[:, :], turn_consts[:, :]).then_inc(sem["consts_ready"], 1)
            act.wait_ge(sem["halo_set"], 4)
            act.wait_ge(sem["consts_ready"], 1)

            def take_in(ct, s):
                act.wait_ge(sem["conv_done"], 2 * ct + s + 1)
                for q in range(quads[s]):
                    number = ct * per_ct + quad0[s] + q
                    b = (quad0[s] + q) % 2
                    act.wait_ge(sem["conv_turned"], number + 1 + per_ct)
                    nc.scalar.copy(chan[s][:, halo + q * 4 * P:halo + (q + 1) * 4 * P], turn_in[b][:, :]
                                   ).then_inc(sem["conv_copied"], 1)

            def silu(ct, s):
                act.wait_ge(sem["conv_done"], 2 * ct + s + 1 + 2)
                turned = ct if kind(ct) == "x" else min(ct, b_end)
                act.wait_ge(sem["back_turned"], turned * per_ct + quad0[s] + quads[s])
                if isinstance(ct, int) and ct > x_tiles:
                    act.wait_ge(sem["chans_stored"][s], 16 * (ct - x_tiles))
                nc.scalar.activation(done[s][:, :], acc[s][:, :], ACT.Silu).then_inc(sem["silu_done"], 1)

            def take_back(ct, s):
                act.wait_ge(sem["toks_stored"][s], 16 * (ct + 1))
                for q in range(quads[s]):
                    number = ct * per_ct + quad0[s] + q
                    b = (quad0[s] + q) % 2
                    act.wait_ge(sem["back_turned"], number + 1 + per_ct)
                    nc.scalar.copy(toks[s][:, 4 * q:4 * q + 4, :].rearrange("p t n -> p (t n)"), turn_back[b][:, :]
                                   ).then_inc(sem["back_copied"], 1)

            def body(ct, more=True):
                take_in(ct, 1)
                silu(ct, 0)
                if kind(ct) != "C":
                    take_back(ct, 0)
                if more:
                    take_in(ct + 1, 0)
                silu(ct, 1)
                if kind(ct) != "C":
                    take_back(ct, 1)

            take_in(0, 0)
            with act.Fori(0, x_tiles) as ct:
                body(ct)
            for ct in range(x_tiles, chan_tiles):
                body(ct, ct + 1 < chan_tiles)

        @block.vector
        def _(dve):
            dve.wait_ge(sem["consts_ready"], 1)

            def convolve(ct, s):
                n = 2 * ct + s
                dve.wait_ge(sem["conv_copied"], ct * per_ct + quad0[s] + quads[s] + 2)
                dve.wait_ge(sem["silu_done"], n + 1)
                nc.vector.tensor_scalar(acc[s][:, :], chan[s][:, 0:SEQS[s]], consts[:, ds(ct, 1)],
                                        consts[:, ds(taps * chan_tiles + ct, 1)], ALU.mult, ALU.add).then_inc(sem["tap_done"], 1)
                for k in range(1, taps):
                    dve.wait_ge(sem["tap_done"], n * (taps - 1) + k)
                    nc.vector.scalar_tensor_tensor(acc[s][:, :], chan[s][:, k:k + SEQS[s]],
                                                   consts[:, ds(k * chan_tiles + ct, 1)], acc[s][:, :],
                                                   ALU.mult, ALU.add
                                                   ).then_inc(sem["tap_done" if k < taps - 1 else "conv_done"], 1)

            with dve.Fori(0, x_tiles) as ct:
                for s in range(2):
                    convolve(ct, s)
            for ct in range(x_tiles, chan_tiles):
                for s in range(2):
                    convolve(ct, s)


DIR = 2
DTW = DIR * HEADS


def ssd_stats_phase(nc, sem, c, params, scratch, st):
    cols = NT * DTW
    with ExitStack() as stack:
        mem = Core(nc, stack, "stats")
        raw = mem.sbuf("raw", [P, NT, DTW])
        bias = mem.sbuf("bias", [P, DTW])
        a_log = mem.sbuf("a_log", [P, DTW])
        rate = mem.sbuf("rate", [P, DTW])
        minus = mem.sbuf("minus", [P, NT, DTW])
        e = mem.sbuf("e", [P, NT, DTW])
        one_e = mem.sbuf("one_e", [P, NT, DTW])
        log = mem.sbuf("log", [P, NT, DTW])
        fix = mem.sbuf("fix", [P, NT, DTW])
        inv = mem.sbuf("inv", [P, NT, DTW])
        a = st["a"]
        def bank_of_sums(name):
            return mem.psum(name, [P, 512])[:, 0:NT * HEADS].rearrange("p (c h) -> p c h", h=HEADS)

        rest = [bank_of_sums(f"rest{d}") for d in range(DIR)]
        upto = [bank_of_sums(f"upto{d}") for d in range(DIR)]
        whole = [bank_of_sums(f"whole{d}") for d in range(DIR)]
        block = stack.enter_context(nc.Block())

        def heads(t, d):
            return t[:, :, d * HEADS:(d + 1) * HEADS]

        @block.sync
        def _(sp):
            sp.dma_start(raw[:, :, :], scratch["dt"].rearrange("(c p) n -> p c n", p=P)).then_inc(sem["stats_in"], 16)
            for d in range(DIR):
                cut = slice(d * HEADS, (d + 1) * HEADS)
                sp.dma_start(bias[:, cut], params["dt_bias"][d].to_broadcast([P, HEADS])).then_inc(sem["stats_in"], 16)
                sp.dma_start(a_log[:, cut], params["a_log"][d].to_broadcast([P, HEADS])).then_inc(sem["stats_in"], 16)

        @block.gpsimd
        def _(pool):
            for m, (op, sign) in enumerate(((ALU.is_gt, 1), (ALU.is_gt, -1), (ALU.is_ge, -1), (ALU.is_ge, 1))):
                nc.gpsimd.memset(st["masks"][:, m, :], 1.0).then_inc(sem["masks_set"], 1)
                pool.wait_ge(sem["masks_set"], 2 * m + 1)
                nc.gpsimd.affine_select(out=st["masks"][:, m, :], in_=st["masks"][:, m, :], compare_op=op, fill=0.0,
                                        base=0, pattern=[[-sign, P]], channel_multiplier=sign
                                        ).then_inc(sem["masks_set"], 1)
            nc.gpsimd.memset(st["ones"][:, :], 1.0).then_inc(sem["masks_set"], 1)

        @block.scalar
        def _(act):
            act.wait_ge(sem["stats_in"], 16 * (1 + 2 * DIR))
            nc.scalar.activation(rate[:, :], a_log[:, :], ACT.Exp).then_inc(sem["stats_act"], 1)
            act.wait_ge(sem["stats_dve"], 2)
            nc.scalar.activation(e[:, :, :], minus[:, :, :], ACT.Exp).then_inc(sem["stats_act"], 1)
            act.wait_ge(sem["stats_dve"], 3)
            nc.scalar.activation(log[:, :, :], one_e[:, :, :], ACT.Ln).then_inc(sem["stats_act"], 1)
            for i, (ps, out) in enumerate(((rest, "decay"), (upto, "entry"), (whole, "total"))):
                act.wait_ge(sem["sums_ready"], i + 1)
                for d in range(DIR):
                    last = nc.scalar.activation(heads(st[out], d), ps[d][:, :, :], ACT.Exp)
                last.then_inc(sem["stats_act"], 1)

        @block.vector
        def _(dve):
            dve.wait_ge(sem["stats_in"], 16 * (1 + 2 * DIR))
            b = bias[:, :].rearrange("p (o n) -> p o n", o=1).to_broadcast([P, NT, DTW])
            nc.vector.tensor_tensor(raw[:, :, :], raw[:, :, :], b, ALU.add).then_inc(sem["stats_dve"], 1)
            dve.wait_ge(sem["stats_dve"], 1)
            nc.vector.scalar_tensor_tensor(minus[:, :, :], raw[:, :, :], -1.0, raw[:, :, :], ALU.mult, ALU.min
                                           ).then_inc(sem["stats_dve"], 1)
            dve.wait_ge(sem["stats_act"], 2)
            nc.vector.tensor_scalar(one_e[:, :, :], e[:, :, :], 1.0, None, ALU.add).then_inc(sem["stats_dve"], 1)
            dve.wait_ge(sem["stats_dve"], 3)
            nc.vector.tensor_scalar(fix[:, :, :], one_e[:, :, :], -1.0, None, ALU.add).then_inc(sem["stats_dve"], 1)
            dve.wait_ge(sem["stats_dve"], 4)
            nc.vector.tensor_tensor(fix[:, :, :], e[:, :, :], fix[:, :, :], ALU.subtract).then_inc(sem["stats_dve"], 1)
            nc.vector.reciprocal(inv[:, :, :], one_e[:, :, :]).then_inc(sem["stats_dve"], 1)
            dve.wait_ge(sem["stats_dve"], 6)
            nc.vector.tensor_tensor(fix[:, :, :], fix[:, :, :], inv[:, :, :], ALU.mult).then_inc(sem["stats_dve"], 1)
            dve.wait_ge(sem["stats_dve"], 7)
            dve.wait_ge(sem["stats_act"], 3)
            nc.vector.tensor_tensor(log[:, :, :], log[:, :, :], fix[:, :, :], ALU.add).then_inc(sem["stats_dve"], 1)
            dve.wait_ge(sem["stats_dve"], 8)
            nc.vector.scalar_tensor_tensor(st["dt"][:, :, :], raw[:, :, :], 0.0, log[:, :, :], ALU.max, ALU.add
                                           ).then_inc(sem["stats_dve"], 1)
            dve.wait_ge(sem["stats_dve"], 9)
            r = rate[:, :].rearrange("p (o n) -> p o n", o=1).to_broadcast([P, NT, DTW])
            nc.vector.scalar_tensor_tensor(a[:, :, :], st["dt"][:, :, :], -1.0, r, ALU.mult, ALU.mult
                                           ).then_inc(sem["a_ready"], 1)
            dve.wait_ge(sem["stats_act"], 4)
            nc.vector.tensor_tensor(st["weight"][:, :, :], st["dt"][:, :, :], st["decay"][:, :, :], ALU.mult)

        @block.tensor
        def _(pe):
            pe.wait_ge(sem["masks_set"], 9)
            pe.wait_ge(sem["a_ready"], 1)
            m = st["masks"]
            for ps, lhs in ((rest, (m[:, 0, :], m[:, 1, :])), (upto, (m[:, 2, :], m[:, 3, :])),
                            (whole, (st["ones"][:, :], st["ones"][:, :]))):
                for d in range(DIR):
                    last = nc.tensor.matmul(ps[d][:, :, :], lhs[d], heads(a, d), start=True, stop=True)
                last.then_inc(sem["sums_ready"], 1)


def backward_states_phase(nc, sem, c, scratch, st):
    with ExitStack() as stack:
        mem = Core(nc, stack, "back")
        xb = mem.sbuf("xb", [P, 2, D_SSD + GROUPS * NST])
        xw = mem.sbuf("xw", [P, 2, HEADS, DH])
        kept = mem.sbuf("kept", [P, 2, HEADS, DH])
        state = mem.sbuf("state", [P, 2, HEADS, DH])
        added = [mem.psum(f"added{u}", [P, D_SSD]) for u in range(2)]
        block = stack.enter_context(nc.Block())
        chunks = scratch["xb"].rearrange("(c p) n -> c p n", p=P)
        states = scratch["states"]
        seq1 = TILES[1] // 2
        seq0 = TILES[0] // 2
        ranges = ((0, seq1), (seq1, seq1 + seq0))

        @block.sync
        def _(sp):
            def load(n, u):
                sp.wait_ge(sem["b_added"], n + 1)
                sp.dma_start(xb[:, u, :], chunks[ds(n * -1 + (NT - 1), 1), :, :].rearrange("o p n -> p (o n)")
                             ).then_inc(sem["b_in"][u], 16)

            for n0, n1 in ranges:
                with sp.Fori(n0, n1) as i:
                    for u in range(2):
                        load(2 * i + u, u)
                        sp.wait_ge(sem["b_state"], 2 * i + u + (2 if n0 == 0 else 3))
                        sp.dma_start(states[ds(i * -2 + (NT - 1 - u), 1), :, :].rearrange("o p n -> p (o n)"),
                                     state[:, u, :, :].rearrange("p h d -> p (h d)")).then_inc(sem["b_stored"][u], 16)
            for u in range(2):
                sp.wait_ge(sem["b_stored"][u], 16 * (NT // 2 + 1))

        @block.gpsimd
        def _(pool):
            give_credit(nc, c).then_inc(sem["b_added"], 2)
            for u in range(2):
                give_credit(nc, c).then_inc(sem["b_stored"][u], 16)
            with pool.Fori(0, NT // 2) as i:
                for u in range(2):
                    n = 2 * i + u
                    pool.wait_ge(sem["b_added"], n + 1)
                    pool.wait_ge(sem["b_in"][u], 16 * (i + 1))
                    w = st["weight"][:, ds(n * -1 + (NT - 1), 1), HEADS:].rearrange("p o h -> p h o")
                    nc.gpsimd.tensor_tensor(xw[:, u, :, :], xb[:, u, 0:D_SSD].rearrange("p (h d) -> p h d", d=DH),
                                            w.to_broadcast([P, HEADS, DH]), ALU.mult).then_inc(sem["b_weighted"], 1)

        @block.tensor
        def _(pe):
            for n0, n1 in ranges:
                with pe.Fori(n0, n1) as i:
                    for u in range(2):
                        n = 2 * i + u
                        pe.wait_ge(sem["b_weighted"], n + 1)
                        pe.wait_ge(sem["b_state"], n + (1 if n0 == 0 else 2))
                        for g in range(GROUPS):
                            last = nc.tensor.matmul(added[u][:, g * 512:(g + 1) * 512],
                                                    xb[:, u, D_SSD + g * NST:D_SSD + (g + 1) * NST],
                                                    xw[:, u, g * HG:(g + 1) * HG, :], start=True, stop=True)
                        last.then_inc(sem["b_added"], 1)

        @block.vector
        def _(dve):
            give_credit(nc, c, nc.vector).then_inc(sem["b_state"], 1)
            for n0, n1 in ranges:
                if n0:
                    dve.wait_ge(sem["b_state"], 2 * n0 + 2)
                nc.vector.memset(state[:, 0, :, :], 0.0).then_inc(sem["b_state"], 1)
                with dve.Fori(n0, n1) as i:
                    for u in range(2):
                        n = 2 * i + u
                        dve.wait_ge(sem["b_state"], n + (2 if n0 == 0 else 3))
                        tot = st["total"][:, ds(n * -1 + (NT - 1), 1), HEADS:].rearrange("p o h -> p h o")
                        nc.vector.tensor_tensor(kept[:, u, :, :], state[:, u, :, :], tot.to_broadcast([P, HEADS, DH]),
                                                ALU.mult).then_inc(sem["b_kept"], 1)
                        dve.wait_ge(sem["b_kept"], n + 1)
                        dve.wait_ge(sem["b_added"], n + 1 + 2)
                        dve.wait_ge(sem["b_stored"][1 - u], 16 * (i + u + 1))
                        nc.vector.tensor_tensor(state[:, 1 - u, :, :].rearrange("p h d -> p (h d)"),
                                                kept[:, u, :, :].rearrange("p h d -> p (h d)"), added[u][:, :],
                                                ALU.add).then_inc(sem["b_state"], 1)


def ssd_phase(nc, sem, c, params, scratch, st):
    quads = HEADS // 4
    with ExitStack() as stack:
        mem = Core(nc, stack, "ssd")
        xb = mem.sbuf("xb", [P, 2, D_SSD + GROUPS * NST])
        bc = mem.sbuf("bc", [P, 2, 2 * GROUPS, P])
        gate = mem.sbuf("gate", [P, 2, D_SSD])
        s_back = mem.sbuf("s_back", [P, 2, D_SSD])
        s_fwd = mem.sbuf("s_fwd", [P, 2, D_SSD])
        kept = mem.sbuf("kept", [P, HEADS, DH])
        spread = [[mem.sbuf(f"spread{d}{b}", [P, 4, P]) for b in range(2)] for d in range(DIR)]
        decay = mem.sbuf("decay", [P, 2, HEADS, P])
        cb = [mem.sbuf(f"cb{d}", [P, 2, GROUPS, P]) for d in range(DIR)]
        m_f = mem.sbuf("m_f", [P, 2, HEADS, P])
        m_b = mem.sbuf("m_b", [P, HEADS, P])
        xw = mem.sbuf("xw", [P, 2, HEADS, DH])
        xd = mem.sbuf("xd", [P, 2, HEADS, DH])
        y = mem.sbuf("y", [P, 2, D_SSD])
        y_back = mem.sbuf("y_back", [P, D_SSD])
        sq = mem.sbuf("sq", [P, D_SSD])
        y_out = mem.sbuf("y_out", [P, 2, D_SSD])
        gain = mem.sbuf("gain", [P, D_SSD])
        skip = mem.sbuf("skip", [P, HEADS])
        ssum = mem.sbuf("ssum", [P, 2])
        lg = mem.sbuf("lg", [P, 2])
        rinv = mem.sbuf("rinv", [P, 2])
        seg = [mem.psum(f"seg{b}", [P, 512]) for b in range(2)]
        cb_ps = mem.psum("cb_ps", [P, 512])
        off = mem.psum("off", [P, D_SSD])
        diag = mem.psum("diag", [P, D_SSD])
        added = mem.psum("added", [P, 512])
        block = stack.enter_context(nc.Block())
        last_pair = NT // 2 - 1
        seq1_pair = TILES[0] // 2

        def per_head(t, width=DH):
            return t.rearrange("p (h o) -> p h o", o=1).to_broadcast([P, t.shape[-1], width])

        def chunk_row(name, n):
            return st[name][:, ds(n, 1), :].rearrange("p o n -> p (o n)")

        def by_head(t):
            return t.rearrange("p (h d) -> p h d", d=DH)

        @block.sync
        def _(sp):
            sp.dma_start(gain[:, :], params["norm_ssd"].to_broadcast([P, D_SSD])).then_inc(sem["f_consts"], 16)
            sp.dma_start(skip[:, :], params["d_skip"].to_broadcast([P, HEADS])).then_inc(sem["f_consts"], 16)

            def load(n, u, first=False):
                if not first:
                    sp.wait_ge(sem["f_off"], 2 * n - 2)
                sp.dma_start(bc[:, u, :, :], scratch["bct"].rearrange("(g n) t -> n g t", n=NST)
                             [:, :, ds(n * P, P)]).then_inc(sem["f_bc_in"][u], 16)
                sp.wait_ge(sem["f_gated"], n + 1)
                sp.dma_start(xb[:, u, :], scratch["xb"].rearrange("(c p) n -> c p n", p=P)[ds(n, 1), :, :]
                             .rearrange("o p n -> p (o n)")).then_inc(sem["f_in"][u], 16)
                sp.dma_start(gate[:, u, :], scratch["zs"].rearrange("(c p) n -> c p n", p=P)[ds(n, 1), :, :]
                             .rearrange("o p n -> p (o n)")).then_inc(sem["f_in"][u], 16)
                sp.dma_start(s_back[:, u, :], scratch["states"][ds(n, 1), :, :]
                             .rearrange("o p n -> p (o n)")).then_inc(sem["f_in"][u], 16)

            def store(n, u):
                sp.wait_ge(sem["f_out"], n + 1 + 2)
                sp.dma_start(scratch["y_ssd"].rearrange("(c p) n -> c p n", p=P)[ds(n, 1), :, :]
                             .rearrange("o p n -> p (o n)"), y_out[:, u, :]).then_inc(sem["f_stored"][u], 16)

            for u in range(2):
                load(u, u, first=True)
            with sp.Fori(0, last_pair) as i:
                for u in range(2):
                    load(2 * i + 2 + u, u)
                    store(2 * i + u, u)
            for u in range(2):
                store(NT - 2 + u, u)
            for u in range(2):
                sp.wait_ge(sem["f_stored"][u], 16 * (NT // 2 + 1))

        @block.gpsimd
        def _(pool):
            for name, count in (("f_gated", 2), ("f_spread_used", 2), ("f_seg_used", 2), ("f_m_ready", 2), ("f_out", 2),
                                ("f_off_used", 1), ("f_cb_masked", 1), ("f_added_used", 1), ("f_diag", 2)):
                give_credit(nc, c).then_inc(sem[name], count)
            for u in range(2):
                give_credit(nc, c).then_inc(sem["f_stored"][u], 16)
            pool.wait_ge(sem["f_consts"], 32)

            def spread_a(n, q):
                b = q % 2
                pool.wait_ge(sem["f_spread_used"], n * quads + q + 1)
                for d in range(DIR):
                    at = d * HEADS + 4 * q
                    mask = st["masks"][:, 2 + d, :].rearrange("p (o l) -> p o l", o=1)
                    last = nc.gpsimd.tensor_tensor(spread[d][b][:, :, :], mask.to_broadcast([P, 4, P]),
                                                   per_head(chunk_row("a", n)[:, at:at + 4], P), ALU.mult)
                last.then_inc(sem["f_spread"], 1)

            def backward_m(n, u):
                pool.wait_ge(sem["f_cb_masked"], n + 1 + 1)
                if not (isinstance(n, int) and n == 0):
                    pool.wait_ge(sem["f_m_summed"], n)
                for g in range(GROUPS):
                    h0 = HEADS + g * HG
                    last = nc.gpsimd.tensor_tensor(m_b[:, g * HG:(g + 1) * HG, :],
                                                   cb[1][:, u, g:g + 1, :].to_broadcast([P, HG, P]),
                                                   per_head(chunk_row("dt", n)[:, h0:h0 + HG], P), ALU.mult)
                last.then_inc(sem["f_m_back"], 1)

            def scale_x(n, i, u):
                pool.wait_ge(sem["f_in"][u], 48 * (i + 1))
                pool.wait_ge(sem["f_gated"], n + 1)
                x = by_head(xb[:, u, 0:D_SSD])
                nc.gpsimd.tensor_tensor(xw[:, u, :, :], x, per_head(chunk_row("weight", n)[:, 0:HEADS]), ALU.mult
                                        ).then_inc(sem["f_scaled"], 1)
                nc.gpsimd.tensor_tensor(xd[:, u, :, :], x, per_head(skip[:, :]), ALU.mult).then_inc(sem["f_scaled"], 1)

            def add_skip(n, u):
                pool.wait_ge(sem["f_off_used"], 2 * n + 2 + 1)
                pool.wait_ge(sem["f_scaled"], 2 * n + 2)
                nc.gpsimd.tensor_tensor(y_back[:, :], y_back[:, :], xd[:, u, :, :].rearrange("p h d -> p (h d)"),
                                        ALU.add).then_inc(sem["f_rest"], 1)

            def chunk(n, i, u):
                nxt = 1 - u
                for q in range(2):
                    spread_a(n + 1, q)
                backward_m(n + 1, nxt)
                for q in range(2, quads):
                    spread_a(n + 1, q)
                add_skip(n, u)
                scale_x(n + 1, i + u, nxt)

            for q in range(quads):
                spread_a(0, q)
            scale_x(0, 0, 0)
            backward_m(0, 0)
            with pool.Fori(0, last_pair) as i:
                for u in range(2):
                    chunk(2 * i + u, i, u)
            chunk(NT - 2, last_pair, 0)
            add_skip(NT - 1, 1)

        @block.tensor
        def _(pe):
            def decays(n, q):
                b = q % 2
                pe.wait_ge(sem["f_spread"], n * quads + q + 1)
                pe.wait_ge(sem["f_seg_used"], n * quads + q + 1)
                for d in range(DIR):
                    last = nc.tensor.matmul(seg[b][:, :], st["masks"][:, d, :],
                                            spread[d][b][:, :, :], start=d == 0, stop=d == 1)
                last.then_inc(sem["f_spread_used"], 1)

            def products(n, i, u):
                pe.wait_ge(sem["f_bc_in"][u], 16 * (i + 1))
                pe.wait_ge(sem["f_cb_masked"], n + 1)
                for g in range(GROUPS):
                    last = nc.tensor.matmul(cb_ps[:, g * P:(g + 1) * P], bc[:, u, g, :], bc[:, u, GROUPS + g, :],
                                            start=True, stop=True)
                last.then_inc(sem["f_cb"], 1)

            def state_part(n, u, d, state):
                pe.wait_ge(sem["f_off_used"], 2 * n + d + 1)
                for g in range(GROUPS):
                    last = nc.tensor.matmul(off[:, g * 512:(g + 1) * 512], bc[:, u, GROUPS + g, :],
                                            state[:, u, g * 512:(g + 1) * 512], start=True, stop=True)
                last.then_inc(sem["f_off"], 1)

            def chunk(n, i, u, reset, more=True):
                if more:
                    products(n + 1, i + u, 1 - u)
                pe.wait_ge(sem["f_added_used"], 2 * n + 1)
                pe.wait_ge(sem["f_zeroed"], 1 + reset)
                state_part(n, u, 0, s_fwd)
                pe.wait_ge(sem["f_scaled"], 2 * n + 2)
                for g in range(GROUPS):
                    pe.wait_ge(sem["f_added_used"], 2 * n + g + 1)
                    nc.tensor.matmul(added[:, :], xb[:, u, D_SSD + g * NST:D_SSD + (g + 1) * NST],
                                     xw[:, u, g * HG:(g + 1) * HG, :], start=True, stop=True
                                     ).then_inc(sem["f_added"], 1)
                    if more:
                        decays(n + 1, g)
                state_part(n, u, 1, s_back)
                if more:
                    for q in range(2, quads):
                        decays(n + 1, q)
                pe.wait_ge(sem["f_gated"], n + 2)
                pe.wait_ge(sem["f_m_ready"], n + 1 + 2)
                for h in range(HEADS):
                    last = nc.tensor.matmul(diag[:, h * DH:(h + 1) * DH], m_f[:, u, h, :],
                                            xb[:, u, h * DH:(h + 1) * DH], start=True, stop=True)
                last.then_inc(sem["f_diag"], 1)

            products(0, 0, 0)
            for q in range(quads):
                decays(0, q)
            for i0, i1, reset in ((0, seq1_pair, 0), (seq1_pair, last_pair, 1)):
                with pe.Fori(i0, i1) as i:
                    for u in range(2):
                        chunk(2 * i + u, i, u, reset)
            chunk(NT - 2, last_pair, 0, 1)
            chunk(NT - 1, last_pair, 1, 1, more=False)

        @block.scalar
        def _(act):
            def decays(n, u):
                act.wait_ge(sem["f_m_ready"], n + 1)
                for q in range(quads):
                    act.wait_ge(sem["f_spread_used"], n * quads + q + 1 + 2)
                    nc.scalar.activation(decay[:, u, 4 * q:4 * q + 4, :].rearrange("p h l -> p (h l)"),
                                         seg[q % 2][:, :], ACT.Exp).then_inc(sem["f_seg_used"], 1)

            def norm(n, u):
                act.wait_ge(sem["f_gated"], n + 1 + 2)
                nc.scalar.activation(sq[:, :], y[:, u, :], ACT.Square, accum_out=ssum[:, u:u + 1]
                                     ).then_inc(sem["f_norm_steps"], 1)
                act.wait_ge(sem["f_norm_steps"], 2 * n + 1)
                nc.scalar.activation(lg[:, u:u + 1], ssum[:, u:u + 1], ACT.Ln, scale=1.0 / D_SSD,
                                     bias=c["eps"][:, :]).then_inc(sem["f_norm_steps"], 1)
                act.wait_ge(sem["f_norm_steps"], 2 * n + 2)
                act.wait_ge(sem["f_out"], n + 1)
                nc.scalar.activation(rinv[:, u:u + 1], lg[:, u:u + 1], ACT.Exp, scale=-0.5).then_inc(sem["f_root"], 1)

            decays(0, 0)
            with act.Fori(0, last_pair) as i:
                for u in range(2):
                    decays(2 * i + u + 1, 1 - u)
                    norm(2 * i + u, u)
            decays(NT - 1, 1)
            norm(NT - 2, 0)
            norm(NT - 1, 1)

        @block.vector
        def _(dve):
            dve.wait_ge(sem["f_consts"], 32)

            def mask_products(n, u):
                dve.wait_ge(sem["f_cb"], n + 1)
                dve.wait_ge(sem["f_m_ready"], n + 1)
                for d in range(DIR):
                    mask = st["masks"][:, 2 + d, :].rearrange("p (o l) -> p o l", o=1).to_broadcast([P, GROUPS, P])
                    last = nc.vector.tensor_tensor(cb[d][:, u, :, :], mask,
                                                   cb_ps[:, 0:GROUPS * P].rearrange("p (g l) -> p g l", l=P),
                                                   ALU.mult)
                last.then_inc(sem["f_cb_masked"], 1)

            def forward_m(n, u):
                dve.wait_ge(sem["f_cb_masked"], n + 1 + 1)
                dve.wait_ge(sem["f_diag"], n + 1)
                for g in range(GROUPS):
                    h = slice(g * HG, (g + 1) * HG)
                    last = nc.vector.tensor_tensor(m_f[:, u, h, :], cb[0][:, u, g:g + 1, :].to_broadcast([P, HG, P]),
                                                   per_head(chunk_row("dt", n)[:, h], P), ALU.mult)
                last.then_inc(sem["f_m_part"], 1)

            def whole_m(n, u):
                dve.wait_ge(sem["f_m_part"], n + 1)
                dve.wait_ge(sem["f_m_back"], n + 1)
                nc.vector.tensor_tensor(m_f[:, u, :, :], m_f[:, u, :, :], m_b[:, :, :], ALU.add
                                        ).then_inc(sem["f_m_summed"], 1)
                dve.wait_ge(sem["f_m_summed"], n + 1)
                dve.wait_ge(sem["f_seg_used"], (n + 1) * quads + 2)
                nc.vector.tensor_tensor(m_f[:, u, :, :], m_f[:, u, :, :], decay[:, u, :, :], ALU.mult
                                        ).then_inc(sem["f_m_ready"], 1)

            def state_part(n, u, d, dst):
                dve.wait_ge(sem["f_off"], 2 * n + d + 1)
                nc.vector.tensor_tensor(by_head(dst), by_head(off[:, :]),
                                        per_head(chunk_row("entry", n)[:, d * HEADS:(d + 1) * HEADS]), ALU.mult
                                        ).then_inc(sem["f_off_used"], 1)

            def next_state(n, u, reset):
                dve.wait_ge(sem["f_added_used"], 2 * n + 1)
                dve.wait_ge(sem["f_zeroed"], 1 + reset)
                nc.vector.tensor_tensor(kept[:, :, :], by_head(s_fwd[:, u, :]),
                                        per_head(chunk_row("total", n)[:, 0:HEADS]), ALU.mult
                                        ).then_inc(sem["f_kept"], 1)
                dve.wait_ge(sem["f_kept"], n + 1)
                for g in range(GROUPS):
                    dve.wait_ge(sem["f_added"], 2 * n + g + 1)
                    half = slice(g * 512, (g + 1) * 512)
                    nc.vector.tensor_tensor(s_fwd[:, 1 - u, half], kept[:, g * HG:(g + 1) * HG, :].rearrange(
                        "p h d -> p (h d)"), added[:, :], ALU.add).then_inc(sem["f_added_used"], 1)

            def finish(n, i, u):
                dve.wait_ge(sem["f_root"], n + 1)
                dve.wait_ge(sem["f_stored"][u], 16 * (i + 1))
                nc.vector.scalar_tensor_tensor(y_out[:, u, :], y[:, u, :], rinv[:, u:u + 1], gain[:, :],
                                               ALU.mult, ALU.mult).then_inc(sem["f_out"], 1)

            def chunk(n, i, u, reset, first=False, more=True):
                dve.wait_ge(sem["f_out"], n + 1)
                state_part(n, u, 0, y[:, u, :])
                if more:
                    mask_products(n + 1, 1 - u)
                next_state(n, u, reset)
                if more:
                    forward_m(n + 1, 1 - u)
                if not first:
                    dve.wait_ge(sem["f_y_steps"], 2 * n)
                state_part(n, u, 1, y_back[:, :])
                if not first:
                    finish(n - 1, i + u - 1, 1 - u)
                if more:
                    whole_m(n + 1, 1 - u)
                dve.wait_ge(sem["f_rest"], n + 1)
                nc.vector.tensor_tensor(y[:, u, :], y[:, u, :], y_back[:, :], ALU.add).then_inc(sem["f_y_steps"], 1)
                dve.wait_ge(sem["f_y_steps"], 2 * n + 1)
                dve.wait_ge(sem["f_diag"], n + 1 + 2)
                nc.vector.tensor_tensor(y[:, u, :], y[:, u, :], diag[:, :], ALU.add).then_inc(sem["f_y_steps"], 1)
                dve.wait_ge(sem["f_y_steps"], 2 * n + 2)
                nc.vector.tensor_tensor(y[:, u, :], y[:, u, :], gate[:, u, :], ALU.mult).then_inc(sem["f_gated"], 1)

            nc.vector.memset(s_fwd[:, 0, :], 0.0).then_inc(sem["f_zeroed"], 1)
            mask_products(0, 0)
            forward_m(0, 0)
            whole_m(0, 0)
            for u in range(2):
                chunk(u, 0, u, 0, first=u == 0)
            for i0, i1, reset in ((1, seq1_pair, 0), (seq1_pair, last_pair, 1)):
                if reset:
                    dve.wait_ge(sem["f_added_used"], 4 * i0 + 1)
                    nc.vector.memset(s_fwd[:, 0, :], 0.0).then_inc(sem["f_zeroed"], 1)
                with dve.Fori(i0, i1) as i:
                    for u in range(2):
                        chunk(2 * i + u, i, u, reset)
            chunk(NT - 2, last_pair, 0, 1)
            chunk(NT - 1, last_pair, 1, 1, more=False)
            finish(NT - 1, last_pair, 1)


OW = VW + 1
BAND = 64
NEG = -1e30
DILATIONS = (1, 4, 16)
GROUP4 = HEADS // 4


class Pass:

    def __init__(self, pattern, s, before=None):
        self.pattern, self.s, self.dil = pattern, s, DILATIONS[pattern]
        length = SEQS[s] // self.dil
        self.banded = length > P
        self.keys = 2 if self.banded else 1
        self.subs = self.dil if self.banded else 1
        self.tiles = length // P if self.banded else TILES[s]
        self.chunks = self.tiles + self.keys - 1
        self.halves = max(1, P // length)
        self.tile0 = before.tile0 + before.subs * before.tiles if before else 0
        self.chunk0 = before.chunk0 + before.subs * before.chunks if before else 0
        self.slot0 = ([before.slot0[b] + before.subs * before.in_slot(b) * before.halves for b in range(2)]
                      if before else [0, 0])
        self.strip0 = before.strip0 + (before.tiles if before.banded else 1) if before else 0

    def in_slot(self, b):
        return (self.chunks + 1 - b) // 2

    def tile(self, r, t):
        return r * self.tiles + t + self.tile0

    def chunk(self, r, k):
        return r * self.chunks + k + self.chunk0

    def slot_loads(self, r, half_k, b):
        return (r * self.in_slot(b) + half_k + 1) * self.halves + self.slot0[b]

    def tile_dmas(self, r, i):
        return (r * (self.tiles // 2) + i) * self.halves + self.tile0 // 2

    def token_rows(self, t_all, width):
        rows = t_all[TOK_BASE[self.s]:TOK_BASE[self.s] + SEQS[self.s], 0:width]
        if self.banded:
            return rows.rearrange("(t p r) n -> r t p n", p=P, r=self.dil)
        return rows.rearrange("(p t h) n -> t h p n", t=self.tiles, h=self.halves)

    def key_rows(self, t_all, width):
        if self.banded:
            reach = BAND * self.dil
            rows = t_all[KV_BASE[self.s] - reach:KV_BASE[self.s] + SEQS[self.s] + reach, 0:width]
            return rows.rearrange("(t p r) n -> r t p n", p=P, r=self.dil)
        rows = t_all[KV_BASE[self.s]:KV_BASE[self.s] + SEQS[self.s], 0:width]
        return rows.rearrange("(p t h) n -> t h p n", t=self.tiles, h=self.halves)

    def parts(self, rows, r, t, buf):
        if self.banded:
            r = ds(r, 1)
            src = rows[r, ds(t, 1), :, :].rearrange("a b p n -> p (a b n)")
            return [(src, buf)]
        n = P // self.halves
        return [(rows[ds(t, 1), h, :, :].rearrange("a p n -> p (a n)"), buf[h * n:(h + 1) * n, :])
                for h in range(self.halves)]


def attention_passes():
    passes = []
    for s in (1, 0):
        for pattern in range(len(DILATIONS)):
            passes.append(Pass(pattern, s, passes[-1] if passes else None))
    return passes


def for_tiles(eng, p, start, body):
    def sub(r):
        start(r)
        if p.tiles > 2:
            with eng.Fori(0, p.tiles // 2 - 1) as i:
                for u in range(2):
                    body(r, i, u, True)
        body(r, p.tiles // 2 - 1, 0, True)
        body(r, p.tiles // 2 - 1, 1, False)

    if p.subs > 1:
        with eng.Fori(0, p.subs) as r:
            sub(r)
    else:
        sub(0)


def attention_phase(nc, sem, c, scratch):
    passes = attention_passes()
    strips = passes[-1].strip0 + 1
    scale = DH ** -0.5
    with ExitStack() as stack:
        mem = Core(nc, stack, "attn")
        q_raw = [mem.sbuf(f"q_raw{u}", [P, D_ATTN]) for u in range(2)]
        k_raw = [mem.sbuf(f"k_raw{u}", [P, D_ATTN]) for u in range(2)]
        v = [mem.sbuf(f"v{u}", [P, HEADS * VW]) for u in range(2)]
        q_hi = [mem.sbuf(f"q_hi{u}", [P, HEADS // 2, P], F32R) for u in range(2)]
        q_lo = [mem.sbuf(f"q_lo{u}", [P, HEADS // 2, P], F32R) for u in range(2)]
        k_hi = mem.sbuf("k_hi", [P, HEADS // 2, 2, P], F32R)
        k_lo = mem.sbuf("k_lo", [P, HEADS // 2, 2, P], F32R)
        p_sb = [mem.sbuf(f"p_sb{u}", [P, 4, 2 * P]) for u in range(2)]
        pt_sb = [mem.sbuf(f"pt_sb{u}", [P, 4, 2 * P]) for u in range(2)]
        o_sb = [mem.sbuf(f"o_sb{u}", [P, HEADS, OW]) for u in range(2)]
        mask = mem.sbuf("mask", [P, strips, 2 * P], BF16)
        ident_b = mem.sbuf("ident_b", [P, P], BF16)
        s_ps = [mem.psum(f"s_ps{u}", [P, 4, 2 * P]) for u in range(2)]
        pt_ps = mem.psum("pt_ps", [P, 4, 2 * P])
        turn = mem.psum("turn", [P, 4, P])
        o_ps = mem.psum("o_ps", [P, 512])[:, 0:4 * VW].rearrange("p (x d) -> p x d", d=VW)
        block = stack.enter_context(nc.Block())

        def heads_of(jj, t):
            return t[:, 4 * jj:4 * jj + 4, :].rearrange("p (a b) d -> p b a d", b=2)

        def head(jj, x):
            return 4 * jj + 2 * (x % 2) + x // 2

        @block.gpsimd
        def _(pool):
            for name, n in (("a_q_turned", 4), ("a_k_turned", 4), ("a_scores", 8), ("a_p", 2), ("a_p_turned", 2),
                            ("a_o", 2), ("a_o_copied", 1)):
                give_credit(nc, c).then_inc(sem[name], n)
            for u in range(2):
                give_credit(nc, c).then_inc(sem["a_stored"][u], 16)
            nc.gpsimd.memset(ident_b[:, :], 0.0).then_inc(sem["a_mask_steps"], 1)
            nc.gpsimd.memset(mask[:, :, :], 0.0).then_inc(sem["a_mask_steps"], 1)
            pool.wait_ge(sem["a_mask_steps"], 2)
            nc.gpsimd.affine_select(out=ident_b[:, :], in_=ident_b[:, :], compare_op=ALU.not_equal, fill=1.0,
                                    base=0, pattern=[[-1, P]], channel_multiplier=1
                                    ).then_inc(sem["a_mask_steps"], 1)
            steps = 3
            for p in passes:
                rules = ()
                if p.banded:
                    rules = [(mask[:, p.strip0 + u:p.strip0 + p.tiles:2, (u + k) % 2 * P:((u + k) % 2 + 1) * P],
                              0, (-1, 1)[k], (1, -1)[k]) for u in range(2) for k in range(2)]
                elif p.halves == 1:
                    rules = [(mask[:, p.strip0:p.strip0 + 1, 0:P], BAND, by, -by) for by in (-1, 1)]
                else:
                    n = P // p.halves
                    for h in range(p.halves):
                        for other in range(p.halves):
                            if other != h:
                                pool.wait_ge(sem["a_mask_steps"], steps)
                                nc.gpsimd.memset(mask[h * n:(h + 1) * n, p.strip0, other * n:(other + 1) * n], NEG
                                                 ).then_inc(sem["a_mask_steps"], 1)
                                steps += 1
                for cut, base, by_query, by_key in rules:
                    pool.wait_ge(sem["a_mask_steps"], steps)
                    nc.gpsimd.affine_select(out=cut, in_=cut, compare_op=ALU.is_ge, fill=NEG, base=base,
                                            pattern=[[0, cut.shape[1]], [by_key, cut.shape[2]]],
                                            channel_multiplier=by_query).then_inc(sem["a_mask_steps"], 1)
                    steps += 1
                if p.banded:
                    pool.wait_ge(sem["a_mask_steps"], steps)
                    nc.gpsimd.memset(mask[:, p.strip0, 0:BAND], NEG).then_inc(sem["a_mask_steps"], 1)
                    pool.wait_ge(sem["a_mask_steps"], steps + 1)
                    nc.gpsimd.memset(mask[:, p.strip0 + p.tiles - 1, P - BAND:P], NEG
                                     ).then_inc(sem["a_mask_steps"], 1)
                    steps += 2
            c["a_mask_total"] = steps

            for p in passes:
                rows = p.key_rows(scratch["v"], HEADS * VW)

                def load_v(r, k, half_k, b, p=p, rows=rows):
                    opening = isinstance(k, int) and k < p.keys
                    pool.wait_ge(sem["a_o"], p.tile(r, 0 if opening else k - 1) * GROUP4 + 2)
                    for src, dst in p.parts(rows, r, k, v[b][:, :]):
                        pool.dma_start(dst, src).then_inc(sem["a_v_in"][b], 16)

                def start(r):
                    load_v(r, 0, 0, 0)
                    if p.banded:
                        load_v(r, 1, 0, 1)

                def body(r, i, u, more):
                    if not more:
                        return
                    k = 2 * i + u + p.keys
                    b = (u + p.keys) % 2
                    load_v(r, k, i + (u + p.keys) // 2, b)

                for_tiles(pool, p, start, body)

        @block.sync
        def _(sp):
            for p in passes:
                q_rows, k_rows = p.token_rows(scratch["q"], D_ATTN), p.key_rows(scratch["k"], D_ATTN)

                def q_free(r, t):
                    sp.wait_ge(sem["a_q_turned"], p.tile(r, t) * 2 + 2)

                def load_q(r, t, u):
                    for src, dst in p.parts(q_rows, r, t, q_raw[u][:, :]):
                        sp.dma_start(dst, src).then_inc(sem["a_q_in"][u], 16)

                def load_k(r, k, b, first=False):
                    sp.wait_ge(sem["a_k_turned"], p.chunk(r, k) * 2 + (4 if first else 2))
                    for src, dst in p.parts(k_rows, r, k, k_raw[b][:, :]):
                        sp.dma_start(dst, src).then_inc(sem["a_k_in"][b], 16)

                def start(r):
                    load_k(r, 0, 0, first=True)
                    q_free(r, 0)
                    load_q(r, 0, 0)
                    if p.banded:
                        load_k(r, 1, 1)

                def body(r, i, u, more):
                    if more:
                        q_free(r, 2 * i + u + 1)
                        load_k(r, 2 * i + u + p.keys, (u + p.keys) % 2)
                        load_q(r, 2 * i + u + 1, 1 - u)

                for_tiles(sp, p, start, body)

        @block.tensor
        def _(pe):
            pe.wait_ge(sem["a_mask_steps"], c["a_mask_total"])
            for p in passes:
                width = p.keys * P

                def turn_q(r, i, u, h, p=p):
                    if h == 0:
                        pe.wait_ge(sem["a_q_in"][u], (p.tile_dmas(r, i) + p.halves) * 16)
                    pe.wait_ge(sem["a_k_split"], p.chunk(r, 2 * i + u + p.keys - 1) * 2 + h + 1)
                    for j in range(4):
                        last = nc.tensor.transpose(turn[:, j, :], q_raw[u][:, (4 * h + j) * P:(4 * h + j + 1) * P],
                                                   c["ident"][:, :])
                    last.then_inc(sem["a_q_turned"], 1)

                def turn_k(r, k, half_k, b, h, tile_before, p=p):
                    if h == 0:
                        pe.wait_ge(sem["a_k_in"][b], p.slot_loads(r, half_k, b) * 16)
                    if tile_before is not None:
                        pe.wait_ge(sem["a_q_split"], tile_before * 2 + h + 1)
                    else:
                        pe.wait_ge(sem["a_k_split"], p.chunk(r, k) * 2 + h + 1)
                    for j in range(4):
                        last = nc.tensor.transpose(turn[:, j, :], k_raw[b][:, (4 * h + j) * P:(4 * h + j + 1) * P],
                                                   c["ident"][:, :])
                    last.then_inc(sem["a_k_turned"], 1)

                def scores(r, i, u, jj, p=p, width=width):
                    t = 2 * i + u
                    n = p.tile(r, t) * GROUP4 + jj
                    pe.wait_ge(sem["a_p"], n + 1)
                    if jj % 2 == 0:
                        pe.wait_ge(sem["a_q_split"], p.tile(r, t) * 2 + jj // 2 + 1)
                        pe.wait_ge(sem["a_k_split"], p.chunk(r, t + p.keys - 1) * 2 + jj // 2 + 2)
                    strip = ds(t + p.strip0, 1) if p.banded else slice(p.strip0, p.strip0 + 1)
                    m = mask[:, strip, 0:width].to_broadcast([P, 2, width])
                    slots = slice(0, 2) if p.banded else slice(u, u + 1)
                    for half in range(2):
                        nc.tensor.matmul(s_ps[jj % 2][:, 2 * half:2 * half + 2, 0:width], ident_b[:, :], m,
                                         start=True, stop=False)
                    for a in range(2):
                        pair = 2 * jj + a
                        for qs, ks in ((q_hi, k_hi), (q_hi, k_lo), (q_lo, k_hi)):
                            for half in range(2):
                                rows = slice(64 * half, 64 * half + 64)
                                last = nc.tensor.matmul(
                                    s_ps[jj % 2][:, 2 * half + a, 0:width], qs[u][rows, pair, :],
                                    ks[rows, pair, slots, :].rearrange("p s n -> p (s n)"), start=False,
                                    stop=a == 1 and qs is q_lo)
                    last.then_inc(sem["a_scores"], 1)

                def turn_p(r, i, u, jj, p=p):
                    n = p.tile(r, 2 * i + u) * GROUP4 + jj
                    pe.wait_ge(sem["a_p"], n + 1 + 2)
                    pe.wait_ge(sem["a_p_copied"], n + 1)
                    for x in range(4):
                        for k in range(p.keys):
                            cut = slice(k * P, (k + 1) * P)
                            last = nc.tensor.transpose(pt_ps[:, x, cut], p_sb[jj % 2][:, x, cut], c["ident"][:, :])
                    last.then_inc(sem["a_p_turned"], 1)

                def outputs(r, i, u, jj, p=p):
                    n = p.tile(r, 2 * i + u) * GROUP4 + jj
                    if jj == 0:
                        b = (u + p.keys - 1) % 2
                        pe.wait_ge(sem["a_v_in"][b], p.slot_loads(r, i + (u + p.keys - 1) // 2, b) * 16)
                        if p.banded:
                            pe.wait_ge(sem["a_v_in"][u], p.slot_loads(r, i, u) * 16)
                    pe.wait_ge(sem["a_p_copied"], n + 1 + 1)
                    pe.wait_ge(sem["a_o_copied"], n + 1)
                    for x in range(4):
                        h = head(jj, x)
                        for k in range(p.keys):
                            last = nc.tensor.matmul(o_ps[:, x, :], pt_sb[jj % 2][:, x, k * P:(k + 1) * P],
                                                    v[k if p.banded else u][:, h * VW:(h + 1) * VW],
                                                    start=k == 0, stop=k == p.keys - 1)
                    last.then_inc(sem["a_o"], 1)

                def start(r, p=p):
                    if p.banded:
                        for h in range(2):
                            turn_k(r, 0, 0, 0, h, None)
                    for h in range(2):
                        turn_q(r, 0, 0, h)
                        turn_k(r, p.keys - 1, 0, p.keys - 1, h, p.tile(r, 0))
                    scores(r, 0, 0, 0)
                    scores(r, 0, 0, 1)

                def body(r, i, u, more, p=p):
                    nxt = (r, i + u, 1 - u)
                    next_k = (r, 2 * i + u + p.keys, i + (u + p.keys) // 2, (u + p.keys) % 2)
                    next_tile = p.tile(r, 2 * i + u + 1)
                    turn_p(r, i, u, 0)
                    scores(r, i, u, 2)
                    if more:
                        turn_q(*nxt, 0)
                    turn_p(r, i, u, 1)
                    outputs(r, i, u, 0)
                    scores(r, i, u, 3)
                    if more:
                        turn_k(*next_k, 0, next_tile)
                    turn_p(r, i, u, 2)
                    outputs(r, i, u, 1)
                    if more:
                        turn_q(*nxt, 1)
                        scores(*nxt, 0)
                        turn_k(*next_k, 1, next_tile)
                    turn_p(r, i, u, 3)
                    outputs(r, i, u, 2)
                    if more:
                        scores(*nxt, 1)
                    outputs(r, i, u, 3)

                for_tiles(pe, p, start, body)

        @block.scalar
        def _(act):
            for p in passes:
                width = p.keys * P
                o_rows = p.token_rows(scratch["o"][p.pattern], HEADS * OW)

                def high_q(r, i, u, h, p=p):
                    t = p.tile(r, 2 * i + u)
                    act.wait_ge(sem["a_scores"], t * GROUP4 + 4)
                    act.wait_ge(sem["a_q_turned"], t * 2 + h + 1 + 4)
                    nc.scalar.activation(q_hi[u][:, 4 * h:4 * h + 4, :], turn[:, :, :], ACT.Copy, scale=scale
                                         ).then_inc(sem["a_q_high"], 1)

                def high_k(r, k, b, h, p=p):
                    opening = isinstance(k, int) and k < p.keys
                    act.wait_ge(sem["a_scores"], p.tile(r, 0) * GROUP4 + 8 if opening else
                                p.tile(r, k - 1) * GROUP4 + 6 + 2 * h)
                    act.wait_ge(sem["a_k_turned"], p.chunk(r, k) * 2 + h + 1 + 4)
                    nc.scalar.copy(k_hi[:, 4 * h:4 * h + 4, b, :], turn[:, :, :]).then_inc(sem["a_k_high"], 1)

                def exponentials(r, i, u, jj, p=p, width=width):
                    n = p.tile(r, 2 * i + u) * GROUP4 + jj
                    act.wait_ge(sem["a_max"], n + 1)
                    act.wait_ge(sem["a_p_turned"], n + 1)
                    for x in range(4):
                        h = head(jj, x)
                        last = nc.scalar.activation(p_sb[jj % 2][:, x, 0:width], s_ps[jj % 2][:, x, 0:width], ACT.Exp,
                                                    bias=o_sb[u][:, h, VW:OW])
                    last.then_inc(sem["a_p"], 1)

                def copy_o(r, i, u, jj, p=p):
                    n = p.tile(r, 2 * i + u) * GROUP4 + jj
                    act.wait_ge(sem["a_o"], n + 1 + 2)
                    nc.scalar.copy(heads_of(jj, o_sb[u])[:, :, :, 0:VW],
                                   o_ps[:, :, :].rearrange("p (b a) d -> p b a d", a=2)).then_inc(sem["a_o_copied"], 1)

                def store(r, i, u, p=p, o_rows=o_rows):
                    act.wait_ge(sem["a_o_copied"], (p.tile(r, 2 * i + u) + 1) * GROUP4 + 1)
                    for dst, src in p.parts(o_rows, r, 2 * i + u, o_sb[u][:, :, :].rearrange("p h d -> p (h d)")):
                        act.dma_start(dst, src).then_inc(sem["a_stored"][u], 16)

                def start(r, p=p):
                    if p.banded:
                        for h in range(2):
                            high_k(r, 0, 0, h)
                    for h in range(2):
                        high_q(r, 0, 0, h)
                        high_k(r, p.keys - 1, p.keys - 1, h)
                    exponentials(r, 0, 0, 0)
                    exponentials(r, 0, 0, 1)

                def body(r, i, u, more, p=p):
                    nxt = (r, i + u, 1 - u)
                    next_k = (r, 2 * i + u + p.keys, (u + p.keys) % 2)
                    if more:
                        high_q(*nxt, 0)
                    exponentials(r, i, u, 2)
                    copy_o(r, i, u, 0)
                    if more:
                        high_k(*next_k, 0)
                    exponentials(r, i, u, 3)
                    copy_o(r, i, u, 1)
                    if more:
                        high_q(*nxt, 1)
                        high_k(*next_k, 1)
                        exponentials(*nxt, 0)
                    copy_o(r, i, u, 2)
                    if more:
                        exponentials(*nxt, 1)
                    copy_o(r, i, u, 3)
                    store(r, i, u)

                for_tiles(act, p, start, body)
            for u in range(2):
                p = passes[-1]
                act.wait_ge(sem["a_stored"][u], 16 * (p.tile_dmas(p.subs - 1, p.tiles // 2) + 1))

        @block.vector
        def _(dve):
            give_credit(nc, c, nc.vector).then_inc(sem["a_k_split"], 1)
            give_credit(nc, c, nc.vector).then_inc(sem["a_p_copied"], 1)
            for p in passes:
                width = p.keys * P

                def low_q(r, i, u, h, p=p):
                    dve.wait_ge(sem["a_q_high"], p.tile(r, 2 * i + u) * 2 + h + 1)
                    half = slice(4 * h, 4 * h + 4)
                    nc.vector.scalar_tensor_tensor(q_lo[u][:, half, :], turn[:, :, :], scale,
                                                   q_hi[u][:, half, :].bitcast(F32), ALU.mult, ALU.subtract
                                                   ).then_inc(sem["a_q_split"], 1)

                def low_k(r, k, b, h, p=p):
                    dve.wait_ge(sem["a_k_high"], p.chunk(r, k) * 2 + h + 1)
                    half = slice(4 * h, 4 * h + 4)
                    nc.vector.tensor_tensor(k_lo[:, half, b, :], turn[:, :, :], k_hi[:, half, b, :].bitcast(F32),
                                            ALU.subtract).then_inc(sem["a_k_split"], 1)

                def maximum(r, i, u, jj, p=p, width=width):
                    n = p.tile(r, 2 * i + u) * GROUP4 + jj
                    if jj == 0:
                        dve.wait_ge(sem["a_stored"][u], p.tile_dmas(r, i) * 16 + 16)
                    dve.wait_ge(sem["a_scores"], n + 1 + 8)
                    nc.vector.tensor_reduce(heads_of(jj, o_sb[u])[:, :, :, VW:OW],
                                            s_ps[jj % 2][:, :, 0:width].rearrange("p (b a) n -> p b a n", a=2),
                                            AX.X, ALU.max, negate=True).then_inc(sem["a_max"], 1)

                def copy_p(r, i, u, jj, p=p, width=width):
                    n = p.tile(r, 2 * i + u) * GROUP4 + jj
                    dve.wait_ge(sem["a_p_turned"], n + 1 + 2)
                    dve.wait_ge(sem["a_o"], n + 1)
                    nc.vector.tensor_copy(pt_sb[jj % 2][:, :, 0:width], pt_ps[:, :, 0:width]
                                          ).then_inc(sem["a_p_copied"], 1)

                def start(r, p=p):
                    if p.banded:
                        for h in range(2):
                            low_k(r, 0, 0, h)
                    for h in range(2):
                        low_q(r, 0, 0, h)
                        low_k(r, p.keys - 1, p.keys - 1, h)
                    maximum(r, 0, 0, 0)
                    maximum(r, 0, 0, 1)

                def body(r, i, u, more, p=p):
                    nxt = (r, i + u, 1 - u)
                    next_k = (r, 2 * i + u + p.keys, (u + p.keys) % 2)
                    copy_p(r, i, u, 0)
                    maximum(r, i, u, 2)
                    if more:
                        low_q(*nxt, 0)
                    copy_p(r, i, u, 1)
                    maximum(r, i, u, 3)
                    if more:
                        low_k(*next_k, 0)
                    copy_p(r, i, u, 2)
                    if more:
                        low_q(*nxt, 1)
                        maximum(*nxt, 0)
                        low_k(*next_k, 1)
                    copy_p(r, i, u, 3)
                    if more:
                        maximum(*nxt, 1)

                for_tiles(dve, p, start, body)


def output_phase(nc, sem, c, x_parts, y_parts, w_out, norm_f, scratch):
    half_k = D_SSD // P
    with ExitStack() as stack:
        mem = Core(nc, stack, "output")
        w_hi = mem.sbuf("w_hi", [P, 2 * half_k, D], F32R)
        w_lo = mem.sbuf("w_lo", [P, 2 * half_k, D], F32R)
        w_raw = mem.sbuf("w_raw", [P, 2, D])
        mix_hi = [mem.sbuf(f"mix_hi{b}", [P, D], F32R) for b in range(2)]
        mix_lo = [mem.sbuf(f"mix_lo{b}", [P, D], F32R) for b in range(2)]
        parts = mem.sbuf("parts", [P, 3, HEADS, OW])
        gate = mem.sbuf("gate", [P, D])
        y_ssd = mem.sbuf("y_ssd", [P, 2, D])
        y_attn = mem.sbuf("y_attn", [P, 2, D])
        x_t = mem.sbuf("x_t", [P, 2, D])
        gain = mem.sbuf("gain", [P, D])
        square = mem.sbuf("square", [P, D])
        low = mem.sbuf("low", [P, 1, HEADS])
        share = mem.sbuf("share", [P, 3, HEADS])
        weight = mem.sbuf("weight", [P, 3, HEADS])
        over = mem.sbuf("over", [P, HEADS])
        ssum = mem.sbuf("ssum", [P, 2])
        root = mem.sbuf("root", [P, 2])
        rinv = mem.sbuf("rinv", [P, 2])
        tr = [mem.psum(f"tr{b}", [P, D]) for b in range(2)]
        out = [mem.psum(f"out{u}", [P, D]) for u in range(2)]
        block = stack.enter_context(nc.Block())

        def per_head(t, width):
            return t.rearrange("p (h o) -> p h o", o=1).to_broadcast([P, HEADS, width])

        def by_head(t):
            return t.rearrange("p (h d) -> p h d", d=DH)

        @block.gpsimd
        def _(pool):
            for name, n in (("e_turned", 2), ("e_products", 2)):
                give_credit(nc, c).then_inc(sem[name], n)
            for k in range(2 * half_k):
                pool.wait_ge(sem["e_w_hi"], k + 1)
                nc.gpsimd.tensor_tensor(w_lo[:, k, :], w_raw[:, k % 2, :], w_hi[:, k, :].bitcast(F32),
                                        ALU.subtract).then_inc(sem["e_w_split"], 1)
            for y, first, tiles in y_parts:
                rows = y.rearrange("o (t u p) d -> (o t) u p d", u=2, p=P)
                with pool.Fori(0, tiles // 2) as i:
                    for u in range(2):
                        pool.wait_ge(sem["e_normed"], first + 2 * i + u + 1)
                        pool.dma_start(rows[ds(i, 1), u, :, :].rearrange("o p d -> p (o d)"), x_t[:, u, :]
                                       ).then_inc(sem["e_stored"][u], 16)
            for u in range(2):
                pool.wait_ge(sem["e_stored"][u], 16 * (NT // 2))

        @block.sync
        def _(sp):
            sp.dma_start(gain[:, :], norm_f.rearrange("(o d) -> o d", o=1).to_broadcast([P, D])).then_inc(sem["e_gain_in"], 16)
            y_rows = scratch["y_ssd"].rearrange("(c p) n -> c p n", p=P)
            o_rows = scratch["o"].rearrange("a (c p) n -> c p a n", p=P)
            gate_rows = scratch["za"].rearrange("(c p) n -> c p n", p=P)

            def load(rows, first, i, u, peeled=False):
                n = first + 2 * i + u
                at = ds(n, 1)
                if not peeled:
                    sp.wait_ge(sem["e_turned"], 2 * n)
                sp.dma_start(y_ssd[:, u, :], y_rows[at, :, :].rearrange("o p n -> p (o n)")
                             ).then_inc(sem["e_y_in"][u], 16)
                if not (peeled and u == 0):
                    sp.wait_ge(sem["e_merged"], n)
                sp.dma_start(parts[:, :, :, :].rearrange("p a h d -> p a (h d)"),
                             o_rows[at, :, :, :].rearrange("o p a n -> p (o a) n")).then_inc(sem["e_parts_in"], 16)
                sp.dma_start(gate[:, :], gate_rows[at, :, :].rearrange("o p n -> p (o n)")
                             ).then_inc(sem["e_parts_in"], 16)
                if not peeled:
                    sp.wait_ge(sem["e_stored"][u], 16 * (first // 2 + i))
                sp.dma_start(x_t[:, u, :], rows[ds(i, 1), u, :, :].rearrange("o p d -> p (o d)")
                             ).then_inc(sem["e_x_in"][u], 16)

            for x, first, tiles in x_parts:
                rows = x.rearrange("o (t u p) d -> (o t) u p d", u=2, p=P)
                if first == 0:
                    for u in range(2):
                        load(rows, first, 0, u, peeled=True)
                with sp.Fori(1 if first == 0 else 0, tiles // 2) as i:
                    for u in range(2):
                        load(rows, first, i, u)

        def for_tiles_ahead(eng, start, body):
            start()
            with eng.Fori(0, NT // 2 - 1) as i:
                for u in range(2):
                    body(2 * i + u, i, u, True)
            body(NT - 2, NT // 2 - 1, 0, True)
            body(NT - 1, NT // 2 - 1, 1, False)

        @block.tensor
        def _(pe):
            def turn(n, i, u, b):
                if b == 0:
                    pe.wait_ge(sem["e_y_in"][u], 16 * i + 16)
                else:
                    pe.wait_ge(sem["e_merged"], n + 1)
                pe.wait_ge(sem["e_split"], 2 * n + b + 1)
                src = (y_ssd, y_attn)[b]
                for k in range(half_k):
                    last = nc.tensor.transpose(tr[b][:, k * P:(k + 1) * P], src[:, u, k * P:(k + 1) * P],
                                               c["ident"][:, :])
                last.then_inc(sem["e_turned"], 1)

            def product(n, u, b):
                pe.wait_ge(sem["e_split"], 2 * n + b + 3)
                if b == 0:
                    pe.wait_ge(sem["e_added"], n + 1)
                for half in range(2):
                    cols = slice(half * CW, (half + 1) * CW)
                    for j, (lhs, rhs) in enumerate(((mix_hi, w_hi), (mix_hi, w_lo), (mix_lo, w_hi))):
                        for k in range(half_k):
                            last = nc.tensor.matmul(out[u][:, cols], lhs[b][:, k * P:(k + 1) * P],
                                                    rhs[:, b * half_k + k, cols], start=b == 0 and j == 0 and k == 0,
                                                    stop=b == 1 and j == 2 and k == half_k - 1)
                last.then_inc(sem["e_products"], 1)

            def start():
                turn(0, 0, 0, 0)
                pe.wait_ge(sem["e_w_split"], 2 * half_k)

            def body(n, i, u, more):
                turn(n, i, u, 1)
                product(n, u, 0)
                if more:
                    turn(n + 1, i + u, 1 - u, 0)
                product(n, u, 1)

            for_tiles_ahead(pe, start, body)

        @block.scalar
        def _(act):
            w_rows = w_out.rearrange("o (k p) n -> p (o k) n", p=P)

            def load_w(k):
                if k >= 2:
                    act.wait_ge(sem["e_w_split"], k - 1)
                act.dma_start(w_raw[:, k % 2, :], w_rows[:, k, :]).then_inc(sem["e_w_in"][k % 2], 16)

            def shares(n):
                act.wait_ge(sem["e_diff"], n + 1)
                act.wait_ge(sem["e_merge_steps"], 3 * n + 1)
                nc.scalar.activation(weight[:, :, :], share[:, :, :], ACT.Exp).then_inc(sem["e_shares"], 1)

            def high(n, b):
                act.wait_ge(sem["e_turned"], 2 * n + b + 1 + 2)
                act.wait_ge(sem["e_products"], 2 * n + b + 1)
                nc.scalar.copy(mix_hi[b][:, :], tr[b][:, :]).then_inc(sem["e_high"], 1)

            def norm(n, u):
                act.wait_ge(sem["e_added"], n + 1 + 2)
                nc.scalar.activation(square[:, :], x_t[:, u, :], ACT.Square, accum_out=ssum[:, u:u + 1]
                                     ).then_inc(sem["e_ssum"], 1)
                act.wait_ge(sem["e_ssum"], n + 1)
                nc.scalar.activation(root[:, u:u + 1], ssum[:, u:u + 1], ACT.Sqrt, scale=1.0 / D,
                                     bias=c["eps"][:, :]).then_inc(sem["e_root"], 1)

            def start():
                load_w(0)
                for k in range(2 * half_k):
                    if k + 1 < 2 * half_k:
                        load_w(k + 1)
                    act.wait_ge(sem["e_w_in"][k % 2], 16 * (k // 2 + 1))
                    nc.scalar.copy(w_hi[:, k, :], w_raw[:, k % 2, :]).then_inc(sem["e_w_hi"], 1)
                shares(0)
                high(0, 0)

            def body(n, i, u, more):
                high(n, 1)
                if more:
                    shares(n + 1)
                    high(n + 1, 0)
                norm(n, u)

            for_tiles_ahead(act, start, body)

        @block.vector
        def _(dve):
            give_credit(nc, c, nc.vector).then_inc(sem["e_split"], 2)
            give_credit(nc, c, nc.vector).then_inc(sem["e_added"], 2)
            give_credit(nc, c, nc.vector).then_inc(sem["e_diff_steps"], 1)
            give_credit(nc, c, nc.vector).then_inc(sem["e_merge_steps"], 1)
            dve.wait_ge(sem["e_gain_in"], 16)

            def low_part(n, b):
                dve.wait_ge(sem["e_high"], 2 * n + b + 1)
                nc.vector.tensor_tensor(mix_lo[b][:, :], tr[b][:, :], mix_hi[b][:, :].bitcast(F32), ALU.subtract
                                        ).then_inc(sem["e_split"], 1)

            def merge(n, u):
                dve.wait_ge(sem["e_parts_in"], 32 * n + 32)
                nc.vector.tensor_reduce(low[:, 0, :], parts[:, :, :, VW].rearrange("p a h -> p h a"), AX.X, ALU.min
                                        ).then_inc(sem["e_diff_steps"], 1)
                dve.wait_ge(sem["e_diff_steps"], n + 1 + 1)
                nc.vector.tensor_tensor(share[:, :, :], low[:, :, :].to_broadcast([P, 3, HEADS]),
                                        parts[:, :, :, VW], ALU.subtract).then_inc(sem["e_diff"], 1)
                dve.wait_ge(sem["e_shares"], n + 1)
                weights = weight[:, :, :].rearrange("p a (h o) -> p a h o", o=1)
                nc.vector.tensor_tensor(parts[:, :, :, 0:VW], parts[:, :, :, 0:VW],
                                        weights.to_broadcast([P, 3, HEADS, VW]), ALU.mult
                                        ).then_inc(sem["e_merge_steps"], 1)
                for a in range(2):
                    dve.wait_ge(sem["e_merge_steps"], 3 * n + a + 1 + 1)
                    nc.vector.tensor_tensor(parts[:, 0, :, 0:VW], parts[:, 0, :, 0:VW], parts[:, a + 1, :, 0:VW],
                                            ALU.add).then_inc(sem["e_merge_steps"], 1)
                dve.wait_ge(sem["e_merge_steps"], 3 * n + 3 + 1)
                nc.vector.reciprocal(over[:, :], parts[:, 0, :, DH]).then_inc(sem["e_over"], 1)
                dve.wait_ge(sem["e_turned"], 2 * n if not isinstance(n, int) or n else 2)
                nc.vector.tensor_tensor(by_head(y_attn[:, u, :]), parts[:, 0, :, 0:DH], by_head(gate[:, :]), ALU.mult
                                        ).then_inc(sem["e_gated"], 1)
                dve.wait_ge(sem["e_over"], n + 1)
                dve.wait_ge(sem["e_gated"], n + 1)
                nc.vector.tensor_tensor(by_head(y_attn[:, u, :]), by_head(y_attn[:, u, :]), per_head(over[:, :], DH),
                                        ALU.mult).then_inc(sem["e_merged"], 1)

            def residual(n, i, u):
                dve.wait_ge(sem["e_x_in"][u], 16 * i + 16)
                dve.wait_ge(sem["e_products"], 2 * n + 2 + 2)
                nc.vector.tensor_tensor(x_t[:, u, :], x_t[:, u, :], out[u][:, :], ALU.add
                                        ).then_inc(sem["e_added"], 1)

            def norm(n, u):
                dve.wait_ge(sem["e_root"], n + 1)
                nc.vector.reciprocal(rinv[:, u:u + 1], root[:, u:u + 1]).then_inc(sem["e_rinv"], 1)
                dve.wait_ge(sem["e_rinv"], n + 1)
                nc.vector.scalar_tensor_tensor(x_t[:, u, :], x_t[:, u, :], rinv[:, u:u + 1], gain[:, :],
                                               ALU.mult, ALU.mult).then_inc(sem["e_normed"], 1)

            def start():
                merge(0, 0)
                low_part(0, 0)

            def body(n, i, u, more):
                low_part(n, 1)
                if more:
                    merge(n + 1, 1 - u)
                    low_part(n + 1, 0)
                residual(n, i, u)
                norm(n, u)

            for_tiles_ahead(dve, start, body)


SEMAPHORES = (
    "ident_zeroed", "gain_in", "h_ready", "zero_set", "pads_stored", "tr_copied", "ssum_ready", "root_ready",
    "tr_ready", "rinv_ready", "turned", "ones_set", "rotated", "staged", "w_split", "out_ready", "w_hi_ready",
    "h_hi_ready", "h_split", "rope_in", "halo_set", "conv_turned", "conv_copied", "conv_done", "silu_done",
    "back_turned", "back_copied", "rows_in", "consts_turned", "consts_ready", "tap_done", "stats_in",
    "masks_set", "stats_act", "stats_dve", "sums_ready", "a_ready", "b_added", "b_state", "b_weighted",
    "b_kept", "f_consts", "f_off", "f_gated", "f_out", "f_spread_used", "f_seg_used", "f_m_ready",
    "f_off_used", "f_cb_masked", "f_added_used", "f_diag", "f_spread", "f_m_summed", "f_m_back", "f_scaled",
    "f_rest", "f_cb", "f_zeroed", "f_added", "f_norm_steps", "f_root", "f_m_part", "f_kept", "f_y_steps",
    "a_q_turned", "a_k_turned", "a_scores", "a_p", "a_p_turned", "a_o", "a_o_copied", "a_mask_steps",
    "a_k_split", "a_q_split", "a_p_copied", "a_q_high", "a_k_high", "a_max", "e_turned", "e_products",
    "e_w_hi", "e_w_split", "e_normed", "e_gain_in", "e_merged", "e_parts_in", "e_split", "e_added", "e_diff",
    "e_merge_steps", "e_shares", "e_high", "e_ssum", "e_root", "e_diff_steps", "e_over", "e_gated", "e_rinv",
)
SLOT_SEMAPHORES = (
    "x_in", "stored", "w_in", "toks_stored", "raw_in", "chans_stored", "b_in", "b_stored", "f_bc_in", "f_in",
    "f_stored", "a_stored", "a_v_in", "a_q_in", "a_k_in", "e_stored", "e_y_in", "e_x_in", "e_w_in",
)


def build(nc, t_in, y_parts):
    tokens = sum(SEQS)
    widths = {"q": D_ATTN, "k": D_ATTN, "v": HEADS * VW, "za": D_ATTN, "zs": D_SSD, "xbc": D_XBC, "dt": 2 * HEADS,
              "xb": D_SSD + GROUPS * NST, "y_ssd": D_SSD}
    scratch = {name: nc.dram_tensor(f"s_{name}", [KV_ROWS if name in ("k", "v") else tokens, width], F32).ap()
               for name, width in widths.items()}
    scratch["bct"] = nc.dram_tensor("s_bct", [2 * GROUPS * NST, tokens], F32).ap()
    scratch["states"] = nc.dram_tensor("s_states", [NT, P, D_SSD], F32).ap()
    scratch["o"] = nc.dram_tensor("s_o", [len(DILATIONS), tokens, HEADS * OW], F32).ap()
    params = {"dt_bias": (t_in["dt_bias_fwd"], t_in["dt_bias_bwd"]), "a_log": (t_in["a_log_fwd"], t_in["a_log_bwd"]),
              "d_skip": t_in["d_skip"], "norm_ssd": t_in["norm_ssd"]}
    x_parts = (t_in["x_prompt"], t_in["x_sample"])

    def with_tiles(arrays):
        return [(a, TOK_BASE[s] // P, TILES[s]) for s, a in enumerate(arrays)]

    with ExitStack() as stack:
        sem = {name: stack.enter_context(nc.semaphore(name)) for name in SEMAPHORES}
        for name in SLOT_SEMAPHORES:
            sem[name] = [stack.enter_context(nc.semaphore(f"{name}{u}")) for u in range(2)]
        c = {name: stack.enter_context(nc.sbuf_tensor(name, [P, width], F32))
             for name, width in (("ident", P), ("credit", 64), ("one", 1), ("eps", 1))}
        c["credit_column"] = itertools.count()
        make_constants(nc, sem, c)
        with nc.sbuf_tensor("hT", [P, NT, KT, P], F32) as hT:
            norm_phase(nc, sem, c, x_parts, t_in["norm_in"], hT, scratch)
            project_phase(nc, sem, c, t_in["w_in"], t_in["rope"], hT, scratch)
        conv_phase(nc, sem, c, t_in["conv_w"], t_in["conv_b"], scratch)
        with ExitStack() as ssd:
            st = {name: ssd.enter_context(nc.sbuf_tensor(f"st_{name}", [P, NT, 2 * HEADS], F32))
                  for name in ("a", "dt", "decay", "entry", "total", "weight")}
            st["masks"] = ssd.enter_context(nc.sbuf_tensor("masks", [P, 4, P], F32))
            st["ones"] = ssd.enter_context(nc.sbuf_tensor("ones", [P, P], F32))
            ssd_stats_phase(nc, sem, c, params, scratch, st)
            backward_states_phase(nc, sem, c, scratch, st)
            ssd_phase(nc, sem, c, params, scratch, st)
        attention_phase(nc, sem, c, scratch)
        output_phase(nc, sem, c, with_tiles(x_parts), with_tiles(y_parts), t_in["w_out"], t_in["norm_f"], scratch)


def rope_table():
    half = DH // 2
    inv = np.float32(10000.0) ** (-np.arange(half, dtype=np.float32) * np.float32(2.0) / np.float32(DH))
    table = np.zeros((P, NT, 3, half), np.float32)
    for s in range(len(SEQS)):
        angles = np.arange(SEQS[s], dtype=np.float32)[:, None] * inv[None, :]
        first = TOK_BASE[s] // P
        for a, values in enumerate((np.cos(angles), -np.sin(angles), np.sin(angles))):
            table[:, first:first + TILES[s], a, :] = values.reshape(TILES[s], P, half).transpose(1, 0, 2)
    return table


def kernel(x_prompt, x_sample, w_in, conv_w, conv_b, dt_bias_fwd, dt_bias_bwd, a_log_fwd, a_log_bwd,
           d_skip, norm_ssd, norm_in, w_out, norm_f):
    import concourse.bacc as _bacc
    from concourse.bass_utils import run_bass_kernel_spmd as _run

    arrays = {"x_prompt": x_prompt, "x_sample": x_sample, "w_in": w_in, "conv_w": conv_w, "conv_b": conv_b,
              "dt_bias_fwd": dt_bias_fwd, "dt_bias_bwd": dt_bias_bwd, "a_log_fwd": a_log_fwd,
              "a_log_bwd": a_log_bwd, "d_skip": d_skip, "norm_ssd": norm_ssd, "norm_in": norm_in,
              "w_out": w_out, "norm_f": norm_f}
    arrays = {name: np.ascontiguousarray(a) for name, a in arrays.items()}
    arrays["rope"] = rope_table()
    nc = _bacc.Bacc("TRN2", target_bir_lowering=False, num_devices=1)
    t_in = {name: nc.dram_tensor(name, list(a.shape), F32, kind="ExternalInput").ap() for name, a in arrays.items()}
    y_parts = [nc.dram_tensor(name, [1, SEQS[s], D], F32, kind="ExternalOutput").ap()
               for s, name in enumerate(("y_prompt", "y_sample"))]
    build(nc, t_in, y_parts)
    r = _run(nc, [arrays], core_ids=[0])
    return r.results[0]["y_prompt"], r.results[0]["y_sample"]
```

```python
import itertools
from contextlib import ExitStack

import numpy as np
import concourse.bass as bass
from concourse import mybir

F32 = mybir.dt.float32
F32R = mybir.dt.float32r
BF16 = mybir.dt.bfloat16
ALU = mybir.AluOpType
ACT = mybir.ActivationFunctionType
AX = mybir.AxisListType

P = 128
D = 1024
KT = D // P
SEQS = (1024, 2048)
TILES = tuple(s // P for s in SEQS)
NT = sum(TILES)
HEADS = 16
DH = 64
D_ATTN = HEADS * DH
D_SSD = 1024
GROUPS = 2
NST = 128
HG = HEADS // GROUPS
D_XBC = D_SSD + 2 * GROUPS * NST
D_PROJ = 4 * D_ATTN + D_SSD + D_XBC + 2 * HEADS
CW = 512
EPS = 1e-5
PAD = 256
KV_ROWS = PAD + SEQS[0] + PAD + SEQS[1] + PAD
KV_BASE = (PAD, PAD + SEQS[0] + PAD)
TOK_BASE = (0, SEQS[0])
VW = DH + 1
ds = bass.ds


class Core:

    def __init__(self, nc, stack, phase):
        self.nc, self.stack, self.phase = nc, stack, phase

    def sbuf(self, name, shape, dtype=F32):
        return self.stack.enter_context(self.nc.sbuf_tensor(f"{self.phase}_{name}", shape, dtype))

    def psum(self, name, shape, dtype=F32):
        return self.stack.enter_context(self.nc.psum_tensor(f"{self.phase}_{name}", shape, dtype))


def give_credit(nc, c, engine=None):
    col = next(c["credit_column"])
    return (engine or nc.gpsimd).memset(c["credit"][:, col:col + 1], 0.0)


def make_constants(nc, sem, c):
    with nc.Block() as block:
        @block.gpsimd
        def _(pool):
            nc.gpsimd.memset(c["ident"][:, :], 0.0).then_inc(sem["ident_zeroed"], 1)
            nc.gpsimd.memset(c["eps"][:, :], EPS)
            nc.gpsimd.memset(c["one"][:, :], 1.0)
            pool.wait_ge(sem["ident_zeroed"], 1)
            nc.gpsimd.affine_select(out=c["ident"][:, :], in_=c["ident"][:, :], compare_op=ALU.not_equal,
                                    fill=1.0, base=0, pattern=[[-1, P]], channel_multiplier=1)


class Weights:

    def __init__(self, nc, stack, sem, c, w_in):
        mem = Core(nc, stack, "weights")
        self.nc, self.sem = nc, sem
        self.raw = mem.sbuf("raw", [P, 2, 2, CW])
        self.hi = [mem.sbuf(f"hi{s}", [P, KT, CW], F32R) for s in range(2)]
        self.lo = [mem.sbuf(f"lo{s}", [P, KT, CW], F32R) for s in range(2)]
        self.rows = w_in.rearrange("o (k p) n -> p (o k) n", p=P)
        self.one = c["one"][:, :].rearrange("p (a b) -> p a b", b=1)

    def load_and_split(self, pool, g, s, cols=CW, fresh=False):
        nc, sem = self.nc, self.sem
        for piece in range(KT // 2):
            b = piece % 2
            pieces = g * (KT // 2) + piece
            raw = self.raw[:, b, :, 0:cols]
            hi = self.hi[s][:, 2 * piece:2 * piece + 2, 0:cols]
            pool.wait_ge(sem["w_split"], pieces + 1)
            pool.dma_start(raw, self.rows[:, 2 * piece:2 * piece + 2, ds(g * CW, cols)]).then_inc(sem["w_in"][b], 16)
            if piece == 0 and not fresh:
                pool.wait_ge(sem["out_ready"], (g - 1) * NT)
            pool.wait_ge(sem["w_in"][b], 16 * (g * (KT // 4) + piece // 2 + 1))
            nc.gpsimd.tensor_tensor(hi, raw, self.one.to_broadcast([P, 2, cols]), ALU.mult
                                    ).then_inc(sem["w_hi_ready"], 1)
            pool.wait_ge(sem["w_hi_ready"], pieces + 1)
            nc.gpsimd.tensor_tensor(self.lo[s][:, 2 * piece:2 * piece + 2, 0:cols], raw, hi.bitcast(F32), ALU.subtract
                                    ).then_inc(sem["w_split"], 1)


def norm_phase(nc, sem, c, x_parts, norm_in, hT, weights, scratch):
    with ExitStack() as stack:
        mem = Core(nc, stack, "norm")
        x_t = mem.sbuf("x_t", [P, 2, D])
        h_t = mem.sbuf("h_t", [P, 2, D])
        sq = mem.sbuf("sq", [P, D])
        gain = mem.sbuf("gain", [P, D])
        ssum = mem.sbuf("ssum", [P, 2])
        root = mem.sbuf("root", [P, 2])
        rinv = mem.sbuf("rinv", [P, 2])
        zero = mem.sbuf("zero", [P, HEADS * VW])
        tr = [mem.psum(f"tr{u}", [P, D]) for u in range(2)]
        block = stack.enter_context(nc.Block())
        parts = [(x, TOK_BASE[s] // P, TILES[s]) for s, x in enumerate(x_parts)]

        @block.sync
        def _(sp):
            sp.dma_start(gain[:, :], norm_in.to_broadcast([P, D])).then_inc(sem["gain_in"], 16)
            for x, first, tiles in parts:
                rows = x.rearrange("o (t u p) d -> (o t) u p d", u=2, p=P)
                with sp.Fori(0, tiles // 2) as i:
                    for u in range(2):
                        sp.wait_ge(sem["h_ready"], first + 2 * i + u + 1)
                        sp.dma_start(x_t[:, u, :], rows[ds(i, 1), u, :, :].rearrange("o p d -> p (o d)")
                                     ).then_inc(sem["x_in"][u], 16)
            sp.wait_ge(sem["zero_set"], 1)
            for row in (0, KV_BASE[1] - PAD, KV_ROWS - PAD):
                for half in range(PAD // P):
                    at = row + half * P
                    sp.dma_start(scratch["k"][at:at + P, :], zero[:, 0:D_ATTN]).then_inc(sem["pads_stored"], 16)
                    sp.dma_start(scratch["v"][at:at + P, :], zero[:, :]).then_inc(sem["pads_stored"], 16)
            sp.wait_ge(sem["pads_stored"], 16 * 2 * 3 * (PAD // P))

        @block.gpsimd
        def _(pool):
            nc.gpsimd.memset(zero[:, :], 0.0).then_inc(sem["zero_set"], 1)
            give_credit(nc, c).then_inc(sem["h_ready"], 2)
            give_credit(nc, c).then_inc(sem["tr_copied"], 2)
            give_credit(nc, c).then_inc(sem["w_split"], 1)
            for s in range(2):
                weights.load_and_split(pool, s, s, fresh=True)

        @block.scalar
        def _(act):
            def statistics(n, i, u):
                act.wait_ge(sem["x_in"][u], 16 * (i + 1))
                nc.scalar.activation(sq[:, :], x_t[:, u, :], ACT.Square, accum_out=ssum[:, u:u + 1]
                                     ).then_inc(sem["ssum_ready"], 1)
                act.wait_ge(sem["ssum_ready"], n + 1)
                nc.scalar.activation(root[:, u:u + 1], ssum[:, u:u + 1], ACT.Sqrt, scale=1.0 / D,
                                     bias=c["eps"][:, :]).then_inc(sem["root_ready"], 1)

            def keep(n, t, u):
                act.wait_ge(sem["tr_ready"], n + 1)
                nc.scalar.copy(hT[:, t, :, :].rearrange("p o k t -> p (o k t)"), tr[u][:, :]
                               ).then_inc(sem["tr_copied"], 1)

            statistics(0, 0, 0)
            with act.Fori(0, NT // 2 - 1) as i:
                for u in range(2):
                    statistics(2 * i + u + 1, i + u, 1 - u)
                    keep(2 * i + u, ds(2 * i + u, 1), u)
            statistics(NT - 1, NT // 2 - 1, 1)
            for u in range(2):
                keep(NT - 2 + u, ds(NT - 2 + u, 1), u)

        @block.vector
        def _(dve):
            dve.wait_ge(sem["gain_in"], 16)
            for x, first, tiles in parts:
                with dve.Fori(0, tiles // 2) as i:
                    for u in range(2):
                        dve.wait_ge(sem["root_ready"], first + 2 * i + u + 1)
                        nc.vector.reciprocal(rinv[:, u:u + 1], root[:, u:u + 1]).then_inc(sem["rinv_ready"], 1)
                        dve.wait_ge(sem["rinv_ready"], first + 2 * i + u + 1)
                        dve.wait_ge(sem["tr_copied"], first + 2 * i + u + 1)
                        nc.vector.scalar_tensor_tensor(h_t[:, u, :], x_t[:, u, :], rinv[:, u:u + 1], gain[:, :],
                                                       ALU.mult, ALU.mult).then_inc(sem["h_ready"], 1)

        @block.tensor
        def _(pe):
            for x, first, tiles in parts:
                with pe.Fori(0, tiles // 2) as i:
                    for u in range(2):
                        pe.wait_ge(sem["h_ready"], first + 2 * i + u + 3)
                        pe.wait_ge(sem["tr_copied"], first + 2 * i + u + 1)
                        for k in range(KT):
                            last = nc.tensor.transpose(tr[u][:, k * P:(k + 1) * P], h_t[:, u, k * P:(k + 1) * P],
                                                       c["ident"][:, :])
                        last.then_inc(sem["tr_ready"], 1)


def project_phase(nc, sem, c, weights, rope, hT, scratch):
    groups = D_PROJ // CW
    dtw = D_PROJ - groups * CW
    with ExitStack() as stack:
        mem = Core(nc, stack, "project")
        h_hi = [mem.sbuf(f"h_hi{u}", [P, KT * P], F32R) for u in range(2)]
        h_lo = [mem.sbuf(f"h_lo{u}", [P, KT * P], F32R) for u in range(2)]
        stage = mem.sbuf("stage", [P, 2, CW])
        v_stage = mem.sbuf("v_stage", [P, 2, CW // DH, VW])
        turned = mem.sbuf("turned", [P, 2, CW])
        table = mem.sbuf("table", [P, NT, 3, DH // 2])
        out = [mem.psum(f"out{u}", [P, CW]) for u in range(2)]
        block = stack.enter_context(nc.Block())
        w_hi, w_lo = weights.hi, weights.lo

        kinds = [(0, 2, "rope", "q"), (2, 2, "rope", "k"), (4, 2, "v", "v"), (6, 2, "silu", "za"),
                 (8, 2, "silu", "zs"), (10, 3, "plain", "xbc"), (13, 1, "dt", "dt")]

        rope_groups = 4
        rotated_steps = rope_groups * NT

        def step(g, i, u):
            return g * NT + 2 * i + u

        @block.gpsimd
        def _(pool):
            nc.gpsimd.memset(v_stage[:, :, :, :], 1.0).then_inc(sem["ones_set"], 1)
            give_credit(nc, c).then_inc(sem["rotated"], 2)
            give_credit(nc, c).then_inc(sem["staged"], 2)
            for u in range(2):
                give_credit(nc, c).then_inc(sem["stored"][u], 16)

            with pool.Fori(1, groups // 2) as j:
                for s in range(2):
                    weights.load_and_split(pool, 2 * j + s, s)
            weights.load_and_split(pool, groups - 1, 0)
            weights.load_and_split(pool, groups, 1, dtw)

        def prepare(eng, n, t, u):
            src = hT[:, t, :, :].rearrange("p o k t -> p (o k t)")
            if eng is nc.scalar:
                nc.scalar.copy(h_hi[u][:, :], src).then_inc(sem["h_hi_ready"], 1)
            else:
                eng.wait_ge(sem["h_hi_ready"], n)
                nc.vector.tensor_tensor(h_lo[u][:, :], src, h_hi[u][:, :].bitcast(F32), ALU.subtract
                                        ).then_inc(sem["h_split"], 1)

        @block.scalar
        def _(act):
            for u in range(2):
                prepare(act, u + 1, ds(u, 1), u)
            act.wait_ge(sem["ones_set"], 1)

            def tile(g, i, u, kind, t_next):
                n = step(g, i, u)
                act.wait_ge(sem["out_ready"], n + 1)
                if kind != "rope":
                    act.wait_ge(sem["stored"][u], 16 * (g * (NT // 2) + i + 1))
                    src = out[u][:, :]
                    if kind == "v":
                        done = nc.scalar.copy(v_stage[:, u, :, 0:DH], src.rearrange("p (h d) -> p h d", d=DH))
                    elif kind == "silu":
                        done = nc.scalar.activation(stage[:, u, :], src, ACT.Silu)
                    elif kind == "plain":
                        done = nc.scalar.copy(stage[:, u, :], src)
                    else:
                        done = nc.scalar.copy(stage[:, u, 0:dtw], out[u][:, 0:dtw])
                    done.then_inc(sem["staged"], 1)
                prepare(nc.scalar, n + 3, t_next, u)

            for g0, count, kind, _name in kinds:
                with act.Fori(g0, g0 + count) as g:
                    with act.Fori(0, NT // 2 - 1) as i:
                        for u in range(2):
                            tile(g, i, u, kind, ds(2 * i + 2 + u, 1))
                    for u in range(2):
                        tile(g, NT // 2 - 1, u, kind, ds(u, 1))

        @block.vector
        def _(dve):
            for u in range(2):
                prepare(dve, u + 1, ds(u, 1), u)
            dve.wait_ge(sem["rope_in"], 16)

            def tile(g, i, u, kind, t_next):
                n = step(g, i, u)
                if kind == "rope":
                    dve.wait_ge(sem["out_ready"], n + 1)
                    dve.wait_ge(sem["stored"][u], 16 * (g * (NT // 2) + i + 1))
                    t = ds(2 * i + u, 1)
                    cos = table[:, t, 0, :].to_broadcast([P, CW // (DH // 2), DH // 2])
                    sines = table[:, t, 1:3, :].to_broadcast([P, CW // DH, 2, DH // 2])
                    halves = out[u][:, :].rearrange("p (h a d) -> p h a d", a=2, d=DH // 2)
                    nc.vector.tensor_tensor(stage[:, u, :].rearrange("p (h d) -> p h d", d=DH // 2),
                                            out[u][:, :].rearrange("p (h d) -> p h d", d=DH // 2), cos, ALU.mult)
                    nc.vector.tensor_tensor(turned[:, u, :].rearrange("p (h a d) -> p h a d", a=2, d=DH // 2),
                                            halves[:, :, ::-1, :], sines, ALU.mult).then_inc(sem["turned"], 1)
                    dve.wait_ge(sem["turned"], n + 1)
                    nc.vector.tensor_tensor(stage[:, u, :], stage[:, u, :], turned[:, u, :], ALU.add
                                            ).then_inc(sem["rotated"], 1)
                prepare(dve, n + 3, t_next, u)

            for g0, count, kind, _name in kinds:
                with dve.Fori(g0, g0 + count) as g:
                    with dve.Fori(0, NT // 2 - 1) as i:
                        for u in range(2):
                            tile(g, i, u, kind, ds(2 * i + 2 + u, 1))
                    for u in range(2):
                        tile(g, NT // 2 - 1, u, kind, ds(u, 1))

        @block.tensor
        def _(pe):
            def tile(g, i, u, s, cols, rope):
                n = step(g, i, u)
                pe.wait_ge(sem["w_split"], (g + 1) * (KT // 2) + 1)
                pe.wait_ge(sem["h_split"], n + 1)
                pe.wait_ge(sem["rotated"], n + 1 if rope else rotated_steps + 2)
                if not rope:
                    pe.wait_ge(sem["staged"], n - rotated_steps + 1)
                last = None
                for a, b in ((h_hi, w_hi), (h_hi, w_lo), (h_lo, w_hi)):
                    for k in range(KT):
                        first = last is None
                        stop = a is h_lo and k == KT - 1
                        last = nc.tensor.matmul(out[u][:, 0:cols], a[u][:, k * P:(k + 1) * P], b[s][:, k, 0:cols],
                                                start=first, stop=stop)
                last.then_inc(sem["out_ready"], 1)

            def group(g, s, cols, rope=False):
                with pe.Fori(0, NT // 2) as i:
                    for u in range(2):
                        tile(g, i, u, s, cols, rope)

            for j0, j1, rope in ((0, rope_groups // 2, True), (rope_groups // 2, groups // 2, False)):
                with pe.Fori(j0, j1) as j:
                    for s in range(2):
                        group(2 * j + s, s, CW, rope)
            group(groups - 1, 0, CW)
            group(groups, 1, dtw)

        @block.sync
        def _(sp):
            sp.dma_start(table[:, :, :, :], rope).then_inc(sem["rope_in"], 16)
            for g0, count, kind, name in kinds:
                padded = name in ("k", "v")
                with sp.Fori(g0, g0 + count) as g:
                    for seq in range(2):
                        half0 = TOK_BASE[seq] // P // 2
                        row0 = KV_BASE[seq] if padded else TOK_BASE[seq]
                        rows = scratch[name][row0:row0 + SEQS[seq], :].rearrange("(t u p) n -> t u p n", u=2, p=P)
                        with sp.Fori(0, TILES[seq] // 2) as i:
                            for u in range(2):
                                n = step(g, half0 + i, u)
                                if kind == "rope":
                                    sp.wait_ge(sem["rotated"], n + 3)
                                else:
                                    sp.wait_ge(sem["staged"], n - rotated_steps + 3)
                                if kind == "v":
                                    width, src = CW // DH * VW, v_stage[:, u, :, :].rearrange("p h d -> p (h d)")
                                elif kind == "dt":
                                    width, src = dtw, stage[:, u, 0:dtw]
                                else:
                                    width, src = CW, stage[:, u, :]
                                dst = rows[ds(i, 1), u, :, ds((g - g0) * width, width)]
                                sp.dma_start(dst.rearrange("o p n -> p (o n)"), src).then_inc(sem["stored"][u], 16)
            total = 16 * (1 + (groups + 1) * (NT // 2))
            for u in range(2):
                sp.wait_ge(sem["stored"][u], total)


def conv_phase(nc, sem, c, conv_w, conv_b, scratch):
    chan_tiles = D_XBC // P
    x_tiles, b_end = D_SSD // P, (D_SSD + GROUPS * NST) // P
    taps = 5
    halo = taps // 2
    quads = tuple(t // 4 for t in TILES)
    quad0 = (0, quads[0])
    per_ct = sum(quads)
    with ExitStack() as stack:
        mem = Core(nc, stack, "conv")
        rows = mem.sbuf("rows", [taps * chan_tiles + chan_tiles, P])
        consts = mem.sbuf("consts", [P, (taps + 1) * chan_tiles])
        raw = [mem.sbuf(f"raw{s}", [P, TILES[s], P]) for s in range(2)]
        chan = [mem.sbuf(f"chan{s}", [P, SEQS[s] + 2 * halo]) for s in range(2)]
        acc = [mem.sbuf(f"acc{s}", [P, SEQS[s]]) for s in range(2)]
        done = [mem.sbuf(f"done{s}", [P, SEQS[s]]) for s in range(2)]
        toks = [mem.sbuf(f"toks{s}", [P, TILES[s], P]) for s in range(2)]
        turn_in = [mem.psum(f"turn_in{b}", [P, 4 * P]) for b in range(2)]
        turn_back = [mem.psum(f"turn_back{b}", [P, 4 * P]) for b in range(2)]
        turn_consts = mem.psum("turn_consts", [P, (taps + 1) * chan_tiles])
        block = stack.enter_context(nc.Block())

        def seq_rows(name, s):
            return scratch[name][TOK_BASE[s]:TOK_BASE[s] + SEQS[s], :].rearrange("(t p) n -> p t n", p=P)

        def kind(ct):
            return "x" if not isinstance(ct, int) or ct < x_tiles else ("B" if ct < b_end else "C")

        @block.gpsimd
        def _(pool):
            for s in range(2):
                nc.gpsimd.memset(chan[s][:, 0:halo], 0.0).then_inc(sem["halo_set"], 1)
                nc.gpsimd.memset(chan[s][:, halo + SEQS[s]:2 * halo + SEQS[s]], 0.0).then_inc(sem["halo_set"], 1)
            give_credit(nc, c).then_inc(sem["conv_turned"], per_ct)
            give_credit(nc, c).then_inc(sem["conv_copied"], 2)
            give_credit(nc, c).then_inc(sem["conv_done"], 2)
            give_credit(nc, c).then_inc(sem["silu_done"], 2)
            give_credit(nc, c).then_inc(sem["back_turned"], per_ct)
            give_credit(nc, c).then_inc(sem["back_copied"], 2)
            for s in range(2):
                give_credit(nc, c).then_inc(sem["toks_stored"][s], 16)

        @block.sync
        def _(sp):
            sp.dma_start(rows[0:taps * chan_tiles, :], conv_w.rearrange("o k (c p) -> (o k c) p", p=P)
                         ).then_inc(sem["rows_in"], 16)
            sp.dma_start(rows[taps * chan_tiles:, :], conv_b.rearrange("o (c p) -> (o c) p", p=P)
                         ).then_inc(sem["rows_in"], 16)

            def load(ct, s):
                sp.wait_ge(sem["conv_turned"], ct * per_ct + quad0[s] + quads[s])
                sp.dma_start(raw[s][:, :, :], seq_rows("xbc", s)[:, :, ds(ct * P, P)]
                             ).then_inc(sem["raw_in"][s], 16)

            def store(ct, s):
                if kind(ct) != "C":
                    sp.wait_ge(sem["back_copied"], ct * per_ct + quad0[s] + quads[s] + 2)
                    sp.dma_start(seq_rows("xb", s)[:, :, ds(ct * P, P)], toks[s][:, :, :]
                                 ).then_inc(sem["toks_stored"][s], 16)
                if kind(ct) != "x":
                    sp.wait_ge(sem["silu_done"], 2 * ct + s + 1 + 2)
                    sp.dma_start(scratch["bct"][(ct - x_tiles) * P:(ct - x_tiles + 1) * P,
                                                TOK_BASE[s]:TOK_BASE[s] + SEQS[s]], done[s][:, :]
                                 ).then_inc(sem["chans_stored"][s], 16)

            for s in range(2):
                load(0, s)
            with sp.Fori(0, x_tiles) as ct:
                for s in range(2):
                    load(ct + 1, s)
                    store(ct, s)
            for ct in range(x_tiles, chan_tiles):
                for s in range(2):
                    if ct + 1 < chan_tiles:
                        load(ct + 1, s)
                    store(ct, s)
            for s in range(2):
                sp.wait_ge(sem["toks_stored"][s], 16 * (b_end + 1))
                sp.wait_ge(sem["chans_stored"][s], 16 * (chan_tiles - x_tiles))

        @block.tensor
        def _(pe):
            pe.wait_ge(sem["rows_in"], 32)
            n = (taps + 1) * chan_tiles
            nc.tensor.transpose(turn_consts[:, :], rows[:, :], c["ident"][0:n, 0:n]).then_inc(sem["consts_turned"], 1)

            def turn(ct, s):
                pe.wait_ge(sem["raw_in"][s], 16 * (ct + 1))
                for q in range(quads[s]):
                    number = ct * per_ct + quad0[s] + q
                    b = (quad0[s] + q) % 2
                    pe.wait_ge(sem["conv_copied"], number + 1)
                    for j in range(4):
                        last = nc.tensor.transpose(turn_in[b][:, j * P:(j + 1) * P], raw[s][:, 4 * q + j, :],
                                                   c["ident"][:, :])
                    last.then_inc(sem["conv_turned"], 1)

            def turn_to_tokens(ct, s):
                pe.wait_ge(sem["silu_done"], 2 * ct + s + 1 + 2)
                for q in range(quads[s]):
                    number = ct * per_ct + quad0[s] + q
                    b = (quad0[s] + q) % 2
                    pe.wait_ge(sem["back_copied"], number + 1)
                    for j in range(4):
                        at = (4 * q + j) * P
                        last = nc.tensor.transpose(turn_back[b][:, j * P:(j + 1) * P], done[s][:, at:at + P],
                                                   c["ident"][:, :])
                    last.then_inc(sem["back_turned"], 1)

            def body(ct, more=True):
                turn(ct, 1)
                if kind(ct) != "C":
                    turn_to_tokens(ct, 0)
                if more:
                    turn(ct + 1, 0)
                if kind(ct) != "C":
                    turn_to_tokens(ct, 1)

            turn(0, 0)
            with pe.Fori(0, x_tiles) as ct:
                body(ct)
            for ct in range(x_tiles, chan_tiles):
                body(ct, ct + 1 < chan_tiles)

        @block.scalar
        def _(act):
            act.wait_ge(sem["consts_turned"], 1)
            nc.scalar.copy(consts[:, :], turn_consts[:, :]).then_inc(sem["consts_ready"], 1)
            act.wait_ge(sem["halo_set"], 4)
            act.wait_ge(sem["consts_ready"], 1)

            def take_in(ct, s):
                act.wait_ge(sem["conv_done"], 2 * ct + s + 1)
                for q in range(quads[s]):
                    number = ct * per_ct + quad0[s] + q
                    b = (quad0[s] + q) % 2
                    act.wait_ge(sem["conv_turned"], number + 1 + per_ct)
                    nc.scalar.copy(chan[s][:, halo + q * 4 * P:halo + (q + 1) * 4 * P], turn_in[b][:, :]
                                   ).then_inc(sem["conv_copied"], 1)

            def silu(ct, s):
                act.wait_ge(sem["conv_done"], 2 * ct + s + 1 + 2)
                turned = ct if kind(ct) == "x" else min(ct, b_end)
                act.wait_ge(sem["back_turned"], turned * per_ct + quad0[s] + quads[s])
                if isinstance(ct, int) and ct > x_tiles:
                    act.wait_ge(sem["chans_stored"][s], 16 * (ct - x_tiles))
                nc.scalar.activation(done[s][:, :], acc[s][:, :], ACT.Silu).then_inc(sem["silu_done"], 1)

            def take_back(ct, s):
                act.wait_ge(sem["toks_stored"][s], 16 * (ct + 1))
                for q in range(quads[s]):
                    number = ct * per_ct + quad0[s] + q
                    b = (quad0[s] + q) % 2
                    act.wait_ge(sem["back_turned"], number + 1 + per_ct)
                    nc.scalar.copy(toks[s][:, 4 * q:4 * q + 4, :].rearrange("p t n -> p (t n)"), turn_back[b][:, :]
                                   ).then_inc(sem["back_copied"], 1)

            def body(ct, more=True):
                take_in(ct, 1)
                silu(ct, 0)
                if kind(ct) != "C":
                    take_back(ct, 0)
                if more:
                    take_in(ct + 1, 0)
                silu(ct, 1)
                if kind(ct) != "C":
                    take_back(ct, 1)

            take_in(0, 0)
            with act.Fori(0, x_tiles) as ct:
                body(ct)
            for ct in range(x_tiles, chan_tiles):
                body(ct, ct + 1 < chan_tiles)

        @block.vector
        def _(dve):
            dve.wait_ge(sem["consts_ready"], 1)

            def convolve(ct, s):
                n = 2 * ct + s
                dve.wait_ge(sem["conv_copied"], ct * per_ct + quad0[s] + quads[s] + 2)
                dve.wait_ge(sem["silu_done"], n + 1)
                nc.vector.tensor_scalar(acc[s][:, :], chan[s][:, 0:SEQS[s]], consts[:, ds(ct, 1)],
                                        consts[:, ds(taps * chan_tiles + ct, 1)], ALU.mult, ALU.add).then_inc(sem["tap_done"], 1)
                for k in range(1, taps):
                    dve.wait_ge(sem["tap_done"], n * (taps - 1) + k)
                    nc.vector.scalar_tensor_tensor(acc[s][:, :], chan[s][:, k:k + SEQS[s]],
                                                   consts[:, ds(k * chan_tiles + ct, 1)], acc[s][:, :],
                                                   ALU.mult, ALU.add
                                                   ).then_inc(sem["tap_done" if k < taps - 1 else "conv_done"], 1)

            with dve.Fori(0, x_tiles) as ct:
                for s in range(2):
                    convolve(ct, s)
            for ct in range(x_tiles, chan_tiles):
                for s in range(2):
                    convolve(ct, s)


DIR = 2
DTW = DIR * HEADS


def ssd_stats_phase(nc, sem, c, params, scratch, st):
    cols = NT * DTW
    with ExitStack() as stack:
        mem = Core(nc, stack, "stats")
        raw = mem.sbuf("raw", [P, NT, DTW])
        bias = mem.sbuf("bias", [P, DTW])
        a_log = mem.sbuf("a_log", [P, DTW])
        rate = mem.sbuf("rate", [P, DTW])
        minus = mem.sbuf("minus", [P, NT, DTW])
        e = mem.sbuf("e", [P, NT, DTW])
        one_e = mem.sbuf("one_e", [P, NT, DTW])
        log = mem.sbuf("log", [P, NT, DTW])
        fix = mem.sbuf("fix", [P, NT, DTW])
        inv = mem.sbuf("inv", [P, NT, DTW])
        a = st["a"]
        def bank_of_sums(name):
            return mem.psum(name, [P, 512])[:, 0:NT * HEADS].rearrange("p (c h) -> p c h", h=HEADS)

        rest = [bank_of_sums(f"rest{d}") for d in range(DIR)]
        upto = [bank_of_sums(f"upto{d}") for d in range(DIR)]
        whole = [bank_of_sums(f"whole{d}") for d in range(DIR)]
        block = stack.enter_context(nc.Block())

        def heads(t, d):
            return t[:, :, d * HEADS:(d + 1) * HEADS]

        @block.sync
        def _(sp):
            sp.dma_start(raw[:, :, :], scratch["dt"].rearrange("(c p) n -> p c n", p=P)).then_inc(sem["stats_in"], 16)
            for d in range(DIR):
                cut = slice(d * HEADS, (d + 1) * HEADS)
                sp.dma_start(bias[:, cut], params["dt_bias"][d].to_broadcast([P, HEADS])).then_inc(sem["stats_in"], 16)
                sp.dma_start(a_log[:, cut], params["a_log"][d].to_broadcast([P, HEADS])).then_inc(sem["stats_in"], 16)

        @block.gpsimd
        def _(pool):
            for m, (op, sign) in enumerate(((ALU.is_gt, 1), (ALU.is_gt, -1), (ALU.is_ge, -1), (ALU.is_ge, 1))):
                nc.gpsimd.memset(st["masks"][:, m, :], 1.0).then_inc(sem["masks_set"], 1)
                pool.wait_ge(sem["masks_set"], 2 * m + 1)
                nc.gpsimd.affine_select(out=st["masks"][:, m, :], in_=st["masks"][:, m, :], compare_op=op, fill=0.0,
                                        base=0, pattern=[[-sign, P]], channel_multiplier=sign
                                        ).then_inc(sem["masks_set"], 1)
            nc.gpsimd.memset(st["ones"][:, :], 1.0).then_inc(sem["masks_set"], 1)

        @block.scalar
        def _(act):
            act.wait_ge(sem["stats_in"], 16 * (1 + 2 * DIR))
            nc.scalar.activation(rate[:, :], a_log[:, :], ACT.Exp).then_inc(sem["stats_act"], 1)
            act.wait_ge(sem["stats_dve"], 2)
            nc.scalar.activation(e[:, :, :], minus[:, :, :], ACT.Exp).then_inc(sem["stats_act"], 1)
            act.wait_ge(sem["stats_dve"], 3)
            nc.scalar.activation(log[:, :, :], one_e[:, :, :], ACT.Ln).then_inc(sem["stats_act"], 1)
            for i, (ps, out) in enumerate(((rest, "decay"), (upto, "entry"), (whole, "total"))):
                act.wait_ge(sem["sums_ready"], i + 1)
                for d in range(DIR):
                    last = nc.scalar.activation(heads(st[out], d), ps[d][:, :, :], ACT.Exp)
                last.then_inc(sem["stats_act"], 1)

        @block.vector
        def _(dve):
            dve.wait_ge(sem["stats_in"], 16 * (1 + 2 * DIR))
            b = bias[:, :].rearrange("p (o n) -> p o n", o=1).to_broadcast([P, NT, DTW])
            nc.vector.tensor_tensor(raw[:, :, :], raw[:, :, :], b, ALU.add).then_inc(sem["stats_dve"], 1)
            dve.wait_ge(sem["stats_dve"], 1)
            nc.vector.scalar_tensor_tensor(minus[:, :, :], raw[:, :, :], -1.0, raw[:, :, :], ALU.mult, ALU.min
                                           ).then_inc(sem["stats_dve"], 1)
            dve.wait_ge(sem["stats_act"], 2)
            nc.vector.tensor_scalar(one_e[:, :, :], e[:, :, :], 1.0, None, ALU.add).then_inc(sem["stats_dve"], 1)
            dve.wait_ge(sem["stats_dve"], 3)
            nc.vector.tensor_scalar(fix[:, :, :], one_e[:, :, :], -1.0, None, ALU.add).then_inc(sem["stats_dve"], 1)
            dve.wait_ge(sem["stats_dve"], 4)
            nc.vector.tensor_tensor(fix[:, :, :], e[:, :, :], fix[:, :, :], ALU.subtract).then_inc(sem["stats_dve"], 1)
            nc.vector.reciprocal(inv[:, :, :], one_e[:, :, :]).then_inc(sem["stats_dve"], 1)
            dve.wait_ge(sem["stats_dve"], 6)
            nc.vector.tensor_tensor(fix[:, :, :], fix[:, :, :], inv[:, :, :], ALU.mult).then_inc(sem["stats_dve"], 1)
            dve.wait_ge(sem["stats_dve"], 7)
            dve.wait_ge(sem["stats_act"], 3)
            nc.vector.tensor_tensor(log[:, :, :], log[:, :, :], fix[:, :, :], ALU.add).then_inc(sem["stats_dve"], 1)
            dve.wait_ge(sem["stats_dve"], 8)
            nc.vector.scalar_tensor_tensor(st["dt"][:, :, :], raw[:, :, :], 0.0, log[:, :, :], ALU.max, ALU.add
                                           ).then_inc(sem["stats_dve"], 1)
            dve.wait_ge(sem["stats_dve"], 9)
            r = rate[:, :].rearrange("p (o n) -> p o n", o=1).to_broadcast([P, NT, DTW])
            nc.vector.scalar_tensor_tensor(a[:, :, :], st["dt"][:, :, :], -1.0, r, ALU.mult, ALU.mult
                                           ).then_inc(sem["a_ready"], 1)
            dve.wait_ge(sem["stats_act"], 4)
            nc.vector.tensor_tensor(st["weight"][:, :, :], st["dt"][:, :, :], st["decay"][:, :, :], ALU.mult)

        @block.tensor
        def _(pe):
            pe.wait_ge(sem["masks_set"], 9)
            pe.wait_ge(sem["a_ready"], 1)
            m = st["masks"]
            for ps, lhs in ((rest, (m[:, 0, :], m[:, 1, :])), (upto, (m[:, 2, :], m[:, 3, :])),
                            (whole, (st["ones"][:, :], st["ones"][:, :]))):
                for d in range(DIR):
                    last = nc.tensor.matmul(ps[d][:, :, :], lhs[d], heads(a, d), start=True, stop=True)
                last.then_inc(sem["sums_ready"], 1)


def backward_states_phase(nc, sem, c, scratch, st):
    with ExitStack() as stack:
        mem = Core(nc, stack, "back")
        ring = 4
        xb = mem.sbuf("xb", [P, ring, D_SSD + GROUPS * NST])
        xw = mem.sbuf("xw", [P, 2, HEADS, DH])
        kept = mem.sbuf("kept", [P, 2, HEADS, DH])
        state = mem.sbuf("state", [P, 2, HEADS, DH])
        added = [mem.psum(f"added{u}", [P, D_SSD]) for u in range(2)]
        block = stack.enter_context(nc.Block())
        chunks = scratch["xb"].rearrange("(c p) n -> c p n", p=P)
        states = scratch["states"]
        seq1 = TILES[1] // 2
        seq0 = TILES[0] // 2
        ranges = ((0, seq1), (seq1, seq1 + seq0))

        @block.scalar
        def _(act):
            with act.Fori(0, NT // ring) as j:
                for slot in range(ring):
                    n = ring * j + slot
                    act.wait_ge(sem["b_added"], n + 1)
                    act.dma_start(xb[:, slot, :], chunks[ds(n * -1 + (NT - 1), 1), :, :].rearrange("o p n -> p (o n)")
                                  ).then_inc(sem["b_in"][slot], 16)

        @block.sync
        def _(sp):
            for n0, n1 in ranges:
                with sp.Fori(n0, n1) as i:
                    for u in range(2):
                        sp.wait_ge(sem["b_state"], 2 * i + u + (2 if n0 == 0 else 3))
                        sp.dma_start(states[ds(i * -2 + (NT - 1 - u), 1), :, :].rearrange("o p n -> p (o n)"),
                                     state[:, u, :, :].rearrange("p h d -> p (h d)")).then_inc(sem["b_stored"][u], 16)
            for u in range(2):
                sp.wait_ge(sem["b_stored"][u], 16 * (NT // 2 + 1))

        @block.gpsimd
        def _(pool):
            give_credit(nc, c).then_inc(sem["b_added"], ring)
            for u in range(2):
                give_credit(nc, c).then_inc(sem["b_stored"][u], 16)
            with pool.Fori(0, NT // ring) as j:
                for slot in range(ring):
                    n, u = ring * j + slot, slot % 2
                    pool.wait_ge(sem["b_added"], n - 1 + ring)
                    pool.wait_ge(sem["b_in"][slot], 16 * (j + 1))
                    w = st["weight"][:, ds(n * -1 + (NT - 1), 1), HEADS:].rearrange("p o h -> p h o")
                    nc.gpsimd.tensor_tensor(xw[:, u, :, :], xb[:, slot, 0:D_SSD].rearrange("p (h d) -> p h d", d=DH),
                                            w.to_broadcast([P, HEADS, DH]), ALU.mult).then_inc(sem["b_weighted"], 1)

        @block.tensor
        def _(pe):
            for n0, n1 in ranges:
                with pe.Fori(n0 // 2, n1 // 2) as j:
                    for slot in range(ring):
                        n, u = ring * j + slot, slot % 2
                        pe.wait_ge(sem["b_weighted"], n + 1)
                        pe.wait_ge(sem["b_state"], n + (1 if n0 == 0 else 2))
                        for g in range(GROUPS):
                            last = nc.tensor.matmul(added[u][:, g * 512:(g + 1) * 512],
                                                    xb[:, slot, D_SSD + g * NST:D_SSD + (g + 1) * NST],
                                                    xw[:, u, g * HG:(g + 1) * HG, :], start=True, stop=True)
                        last.then_inc(sem["b_added"], 1)

        @block.vector
        def _(dve):
            give_credit(nc, c, nc.vector).then_inc(sem["b_state"], 1)
            for n0, n1 in ranges:
                if n0:
                    dve.wait_ge(sem["b_state"], 2 * n0 + 2)
                nc.vector.memset(state[:, 0, :, :], 0.0).then_inc(sem["b_state"], 1)
                with dve.Fori(n0, n1) as i:
                    for u in range(2):
                        n = 2 * i + u
                        dve.wait_ge(sem["b_state"], n + (2 if n0 == 0 else 3))
                        tot = st["total"][:, ds(n * -1 + (NT - 1), 1), HEADS:].rearrange("p o h -> p h o")
                        nc.vector.tensor_tensor(kept[:, u, :, :], state[:, u, :, :], tot.to_broadcast([P, HEADS, DH]),
                                                ALU.mult).then_inc(sem["b_kept"], 1)
                        dve.wait_ge(sem["b_kept"], n + 1)
                        dve.wait_ge(sem["b_added"], n + 1 + ring)
                        dve.wait_ge(sem["b_stored"][1 - u], 16 * (i + u + 1))
                        nc.vector.tensor_tensor(state[:, 1 - u, :, :].rearrange("p h d -> p (h d)"),
                                                kept[:, u, :, :].rearrange("p h d -> p (h d)"), added[u][:, :],
                                                ALU.add).then_inc(sem["b_state"], 1)


def ssd_phase(nc, sem, c, params, scratch, st):
    quads = HEADS // 4
    with ExitStack() as stack:
        mem = Core(nc, stack, "ssd")
        xb = mem.sbuf("xb", [P, 2, D_SSD + GROUPS * NST])
        bc = mem.sbuf("bc", [P, 2, 2 * GROUPS, P])
        gate = mem.sbuf("gate", [P, 2, D_SSD])
        s_back = mem.sbuf("s_back", [P, 2, D_SSD])
        s_fwd = mem.sbuf("s_fwd", [P, 2, D_SSD])
        kept = mem.sbuf("kept", [P, HEADS, DH])
        spread = [[mem.sbuf(f"spread{d}{b}", [P, 4, P]) for b in range(2)] for d in range(DIR)]
        decay = mem.sbuf("decay", [P, 2, HEADS, P])
        cb = [mem.sbuf(f"cb{d}", [P, 2, GROUPS, P]) for d in range(DIR)]
        m_f = mem.sbuf("m_f", [P, 2, HEADS, P])
        m_b = mem.sbuf("m_b", [P, HEADS, P])
        xw = mem.sbuf("xw", [P, 2, HEADS, DH])
        xd = mem.sbuf("xd", [P, 2, HEADS, DH])
        y = mem.sbuf("y", [P, 2, D_SSD])
        y_back = mem.sbuf("y_back", [P, D_SSD])
        sq = mem.sbuf("sq", [P, D_SSD])
        y_out = mem.sbuf("y_out", [P, 2, D_SSD])
        gain = mem.sbuf("gain", [P, D_SSD])
        skip = mem.sbuf("skip", [P, HEADS])
        ssum = mem.sbuf("ssum", [P, 2])
        lg = mem.sbuf("lg", [P, 2])
        rinv = mem.sbuf("rinv", [P, 2])
        seg = [mem.psum(f"seg{b}", [P, 512]) for b in range(2)]
        cb_ps = mem.psum("cb_ps", [P, 512])
        off = mem.psum("off", [P, D_SSD])
        diag = mem.psum("diag", [P, D_SSD])
        added = mem.psum("added", [P, 512])
        block = stack.enter_context(nc.Block())
        last_pair = NT // 2 - 1
        seq1_pair = TILES[0] // 2

        def per_head(t, width=DH):
            return t.rearrange("p (h o) -> p h o", o=1).to_broadcast([P, t.shape[-1], width])

        def chunk_row(name, n):
            return st[name][:, ds(n, 1), :].rearrange("p o n -> p (o n)")

        def by_head(t):
            return t.rearrange("p (h d) -> p h d", d=DH)

        @block.sync
        def _(sp):
            sp.dma_start(gain[:, :], params["norm_ssd"].to_broadcast([P, D_SSD])).then_inc(sem["f_consts"], 16)
            sp.dma_start(skip[:, :], params["d_skip"].to_broadcast([P, HEADS])).then_inc(sem["f_consts"], 16)

            def load(n, u, first=False):
                if not first:
                    sp.wait_ge(sem["f_off"], 2 * n - 2)
                sp.dma_start(bc[:, u, :, :], scratch["bct"].rearrange("(g n) t -> n g t", n=NST)
                             [:, :, ds(n * P, P)]).then_inc(sem["f_bc_in"][u], 16)
                sp.wait_ge(sem["f_gated"], n + 1)
                sp.dma_start(xb[:, u, :], scratch["xb"].rearrange("(c p) n -> c p n", p=P)[ds(n, 1), :, :]
                             .rearrange("o p n -> p (o n)")).then_inc(sem["f_in"][u], 16)
                sp.dma_start(gate[:, u, :], scratch["zs"].rearrange("(c p) n -> c p n", p=P)[ds(n, 1), :, :]
                             .rearrange("o p n -> p (o n)")).then_inc(sem["f_in"][u], 16)
                sp.dma_start(s_back[:, u, :], scratch["states"][ds(n, 1), :, :]
                             .rearrange("o p n -> p (o n)")).then_inc(sem["f_in"][u], 16)

            def store(n, u):
                sp.wait_ge(sem["f_out"], n + 1 + 2)
                sp.dma_start(scratch["y_ssd"].rearrange("(c p) n -> c p n", p=P)[ds(n, 1), :, :]
                             .rearrange("o p n -> p (o n)"), y_out[:, u, :]).then_inc(sem["f_stored"][u], 16)

            for u in range(2):
                load(u, u, first=True)
            with sp.Fori(0, last_pair) as i:
                for u in range(2):
                    load(2 * i + 2 + u, u)
                    store(2 * i + u, u)
            for u in range(2):
                store(NT - 2 + u, u)
            for u in range(2):
                sp.wait_ge(sem["f_stored"][u], 16 * (NT // 2 + 1))

        @block.gpsimd
        def _(pool):
            for name, count in (("f_gated", 2), ("f_spread_used", 2), ("f_seg_used", 2), ("f_m_ready", 2), ("f_out", 2),
                                ("f_off_used", 1), ("f_cb_masked", 1), ("f_added_used", 1), ("f_diag", 2)):
                give_credit(nc, c).then_inc(sem[name], count)
            for u in range(2):
                give_credit(nc, c).then_inc(sem["f_stored"][u], 16)
            pool.wait_ge(sem["f_consts"], 32)

            def spread_a(n, q):
                b = q % 2
                pool.wait_ge(sem["f_spread_used"], n * quads + q + 1)
                for d in range(DIR):
                    at = d * HEADS + 4 * q
                    mask = st["masks"][:, 2 + d, :].rearrange("p (o l) -> p o l", o=1)
                    last = nc.gpsimd.tensor_tensor(spread[d][b][:, :, :], mask.to_broadcast([P, 4, P]),
                                                   per_head(chunk_row("a", n)[:, at:at + 4], P), ALU.mult)
                last.then_inc(sem["f_spread"], 1)

            def backward_m(n, u):
                pool.wait_ge(sem["f_cb_masked"], n + 1 + 1)
                if not (isinstance(n, int) and n == 0):
                    pool.wait_ge(sem["f_m_summed"], n)
                for g in range(GROUPS):
                    h0 = HEADS + g * HG
                    last = nc.gpsimd.tensor_tensor(m_b[:, g * HG:(g + 1) * HG, :],
                                                   cb[1][:, u, g:g + 1, :].to_broadcast([P, HG, P]),
                                                   per_head(chunk_row("dt", n)[:, h0:h0 + HG], P), ALU.mult)
                last.then_inc(sem["f_m_back"], 1)

            def scale_x(n, i, u):
                pool.wait_ge(sem["f_in"][u], 48 * (i + 1))
                pool.wait_ge(sem["f_gated"], n + 1)
                x = by_head(xb[:, u, 0:D_SSD])
                nc.gpsimd.tensor_tensor(xw[:, u, :, :], x, per_head(chunk_row("weight", n)[:, 0:HEADS]), ALU.mult
                                        ).then_inc(sem["f_scaled"], 1)
                nc.gpsimd.tensor_tensor(xd[:, u, :, :], x, per_head(skip[:, :]), ALU.mult).then_inc(sem["f_scaled"], 1)

            def add_skip(n, u):
                pool.wait_ge(sem["f_off_used"], 2 * n + 2 + 1)
                pool.wait_ge(sem["f_scaled"], 2 * n + 2)
                nc.gpsimd.tensor_tensor(y_back[:, :], y_back[:, :], xd[:, u, :, :].rearrange("p h d -> p (h d)"),
                                        ALU.add).then_inc(sem["f_rest"], 1)

            def chunk(n, i, u):
                nxt = 1 - u
                for q in range(2):
                    spread_a(n + 1, q)
                backward_m(n + 1, nxt)
                for q in range(2, quads):
                    spread_a(n + 1, q)
                add_skip(n, u)
                scale_x(n + 1, i + u, nxt)

            for q in range(quads):
                spread_a(0, q)
            scale_x(0, 0, 0)
            backward_m(0, 0)
            with pool.Fori(0, last_pair) as i:
                for u in range(2):
                    chunk(2 * i + u, i, u)
            chunk(NT - 2, last_pair, 0)
            add_skip(NT - 1, 1)

        @block.tensor
        def _(pe):
            def decays(n, q):
                b = q % 2
                pe.wait_ge(sem["f_spread"], n * quads + q + 1)
                pe.wait_ge(sem["f_seg_used"], n * quads + q + 1)
                for d in range(DIR):
                    last = nc.tensor.matmul(seg[b][:, :], st["masks"][:, d, :],
                                            spread[d][b][:, :, :], start=d == 0, stop=d == 1)
                last.then_inc(sem["f_spread_used"], 1)

            def products(n, i, u):
                pe.wait_ge(sem["f_bc_in"][u], 16 * (i + 1))
                pe.wait_ge(sem["f_cb_masked"], n + 1)
                for g in range(GROUPS):
                    last = nc.tensor.matmul(cb_ps[:, g * P:(g + 1) * P], bc[:, u, g, :], bc[:, u, GROUPS + g, :],
                                            start=True, stop=True)
                last.then_inc(sem["f_cb"], 1)

            def state_part(n, u, d, state):
                pe.wait_ge(sem["f_off_used"], 2 * n + d + 1)
                for g in range(GROUPS):
                    last = nc.tensor.matmul(off[:, g * 512:(g + 1) * 512], bc[:, u, GROUPS + g, :],
                                            state[:, u, g * 512:(g + 1) * 512], start=True, stop=True)
                last.then_inc(sem["f_off"], 1)

            def chunk(n, i, u, reset, more=True):
                if more:
                    products(n + 1, i + u, 1 - u)
                pe.wait_ge(sem["f_added_used"], 2 * n + 1)
                pe.wait_ge(sem["f_zeroed"], 1 + reset)
                state_part(n, u, 0, s_fwd)
                pe.wait_ge(sem["f_scaled"], 2 * n + 2)
                for g in range(GROUPS):
                    pe.wait_ge(sem["f_added_used"], 2 * n + g + 1)
                    nc.tensor.matmul(added[:, :], xb[:, u, D_SSD + g * NST:D_SSD + (g + 1) * NST],
                                     xw[:, u, g * HG:(g + 1) * HG, :], start=True, stop=True
                                     ).then_inc(sem["f_added"], 1)
                    if more:
                        decays(n + 1, g)
                state_part(n, u, 1, s_back)
                if more:
                    for q in range(2, quads):
                        decays(n + 1, q)
                pe.wait_ge(sem["f_gated"], n + 2)
                pe.wait_ge(sem["f_m_ready"], n + 1 + 2)
                for h in range(HEADS):
                    last = nc.tensor.matmul(diag[:, h * DH:(h + 1) * DH], m_f[:, u, h, :],
                                            xb[:, u, h * DH:(h + 1) * DH], start=True, stop=True)
                last.then_inc(sem["f_diag"], 1)

            products(0, 0, 0)
            for q in range(quads):
                decays(0, q)
            for i0, i1, reset in ((0, seq1_pair, 0), (seq1_pair, last_pair, 1)):
                with pe.Fori(i0, i1) as i:
                    for u in range(2):
                        chunk(2 * i + u, i, u, reset)
            chunk(NT - 2, last_pair, 0, 1)
            chunk(NT - 1, last_pair, 1, 1, more=False)

        @block.scalar
        def _(act):
            def decays(n, u):
                act.wait_ge(sem["f_m_ready"], n + 1)
                for q in range(quads):
                    act.wait_ge(sem["f_spread_used"], n * quads + q + 1 + 2)
                    nc.scalar.activation(decay[:, u, 4 * q:4 * q + 4, :].rearrange("p h l -> p (h l)"),
                                         seg[q % 2][:, :], ACT.Exp).then_inc(sem["f_seg_used"], 1)

            def norm(n, u):
                act.wait_ge(sem["f_gated"], n + 1 + 2)
                nc.scalar.activation(sq[:, :], y[:, u, :], ACT.Square, accum_out=ssum[:, u:u + 1]
                                     ).then_inc(sem["f_norm_steps"], 1)
                act.wait_ge(sem["f_norm_steps"], 2 * n + 1)
                nc.scalar.activation(lg[:, u:u + 1], ssum[:, u:u + 1], ACT.Ln, scale=1.0 / D_SSD,
                                     bias=c["eps"][:, :]).then_inc(sem["f_norm_steps"], 1)
                act.wait_ge(sem["f_norm_steps"], 2 * n + 2)
                act.wait_ge(sem["f_out"], n + 1)
                nc.scalar.activation(rinv[:, u:u + 1], lg[:, u:u + 1], ACT.Exp, scale=-0.5).then_inc(sem["f_root"], 1)

            decays(0, 0)
            with act.Fori(0, last_pair) as i:
                for u in range(2):
                    decays(2 * i + u + 1, 1 - u)
                    norm(2 * i + u, u)
            decays(NT - 1, 1)
            norm(NT - 2, 0)
            norm(NT - 1, 1)

        @block.vector
        def _(dve):
            dve.wait_ge(sem["f_consts"], 32)

            def mask_products(n, u):
                dve.wait_ge(sem["f_cb"], n + 1)
                dve.wait_ge(sem["f_m_ready"], n + 1)
                for d in range(DIR):
                    mask = st["masks"][:, 2 + d, :].rearrange("p (o l) -> p o l", o=1).to_broadcast([P, GROUPS, P])
                    last = nc.vector.tensor_tensor(cb[d][:, u, :, :], mask,
                                                   cb_ps[:, 0:GROUPS * P].rearrange("p (g l) -> p g l", l=P),
                                                   ALU.mult)
                last.then_inc(sem["f_cb_masked"], 1)

            def forward_m(n, u):
                dve.wait_ge(sem["f_cb_masked"], n + 1 + 1)
                dve.wait_ge(sem["f_diag"], n + 1)
                for g in range(GROUPS):
                    h = slice(g * HG, (g + 1) * HG)
                    last = nc.vector.tensor_tensor(m_f[:, u, h, :], cb[0][:, u, g:g + 1, :].to_broadcast([P, HG, P]),
                                                   per_head(chunk_row("dt", n)[:, h], P), ALU.mult)
                last.then_inc(sem["f_m_part"], 1)

            def whole_m(n, u):
                dve.wait_ge(sem["f_m_part"], n + 1)
                dve.wait_ge(sem["f_m_back"], n + 1)
                nc.vector.tensor_tensor(m_f[:, u, :, :], m_f[:, u, :, :], m_b[:, :, :], ALU.add
                                        ).then_inc(sem["f_m_summed"], 1)
                dve.wait_ge(sem["f_m_summed"], n + 1)
                dve.wait_ge(sem["f_seg_used"], (n + 1) * quads + 2)
                nc.vector.tensor_tensor(m_f[:, u, :, :], m_f[:, u, :, :], decay[:, u, :, :], ALU.mult
                                        ).then_inc(sem["f_m_ready"], 1)

            def state_part(n, u, d, dst):
                dve.wait_ge(sem["f_off"], 2 * n + d + 1)
                nc.vector.tensor_tensor(by_head(dst), by_head(off[:, :]),
                                        per_head(chunk_row("entry", n)[:, d * HEADS:(d + 1) * HEADS]), ALU.mult
                                        ).then_inc(sem["f_off_used"], 1)

            def next_state(n, u, reset):
                dve.wait_ge(sem["f_added_used"], 2 * n + 1)
                dve.wait_ge(sem["f_zeroed"], 1 + reset)
                nc.vector.tensor_tensor(kept[:, :, :], by_head(s_fwd[:, u, :]),
                                        per_head(chunk_row("total", n)[:, 0:HEADS]), ALU.mult
                                        ).then_inc(sem["f_kept"], 1)
                dve.wait_ge(sem["f_kept"], n + 1)
                for g in range(GROUPS):
                    dve.wait_ge(sem["f_added"], 2 * n + g + 1)
                    half = slice(g * 512, (g + 1) * 512)
                    nc.vector.tensor_tensor(s_fwd[:, 1 - u, half], kept[:, g * HG:(g + 1) * HG, :].rearrange(
                        "p h d -> p (h d)"), added[:, :], ALU.add).then_inc(sem["f_added_used"], 1)

            def finish(n, i, u):
                dve.wait_ge(sem["f_root"], n + 1)
                dve.wait_ge(sem["f_stored"][u], 16 * (i + 1))
                nc.vector.scalar_tensor_tensor(y_out[:, u, :], y[:, u, :], rinv[:, u:u + 1], gain[:, :],
                                               ALU.mult, ALU.mult).then_inc(sem["f_out"], 1)

            def chunk(n, i, u, reset, first=False, more=True):
                dve.wait_ge(sem["f_out"], n + 1)
                state_part(n, u, 0, y[:, u, :])
                if more:
                    mask_products(n + 1, 1 - u)
                next_state(n, u, reset)
                if more:
                    forward_m(n + 1, 1 - u)
                if not first:
                    dve.wait_ge(sem["f_y_steps"], 2 * n)
                state_part(n, u, 1, y_back[:, :])
                if not first:
                    finish(n - 1, i + u - 1, 1 - u)
                if more:
                    whole_m(n + 1, 1 - u)
                dve.wait_ge(sem["f_rest"], n + 1)
                nc.vector.tensor_tensor(y[:, u, :], y[:, u, :], y_back[:, :], ALU.add).then_inc(sem["f_y_steps"], 1)
                dve.wait_ge(sem["f_y_steps"], 2 * n + 1)
                dve.wait_ge(sem["f_diag"], n + 1 + 2)
                nc.vector.tensor_tensor(y[:, u, :], y[:, u, :], diag[:, :], ALU.add).then_inc(sem["f_y_steps"], 1)
                dve.wait_ge(sem["f_y_steps"], 2 * n + 2)
                nc.vector.tensor_tensor(y[:, u, :], y[:, u, :], gate[:, u, :], ALU.mult).then_inc(sem["f_gated"], 1)

            nc.vector.memset(s_fwd[:, 0, :], 0.0).then_inc(sem["f_zeroed"], 1)
            mask_products(0, 0)
            forward_m(0, 0)
            whole_m(0, 0)
            for u in range(2):
                chunk(u, 0, u, 0, first=u == 0)
            for i0, i1, reset in ((1, seq1_pair, 0), (seq1_pair, last_pair, 1)):
                if reset:
                    dve.wait_ge(sem["f_added_used"], 4 * i0 + 1)
                    nc.vector.memset(s_fwd[:, 0, :], 0.0).then_inc(sem["f_zeroed"], 1)
                with dve.Fori(i0, i1) as i:
                    for u in range(2):
                        chunk(2 * i + u, i, u, reset)
            chunk(NT - 2, last_pair, 0, 1)
            chunk(NT - 1, last_pair, 1, 1, more=False)
            finish(NT - 1, last_pair, 1)


OW = VW + 1
BAND = 64
NEG = -1e30
DILATIONS = (1, 4, 16)
GROUP4 = HEADS // 4


class Pass:

    def __init__(self, pattern, s, before=None):
        self.pattern, self.s, self.dil = pattern, s, DILATIONS[pattern]
        length = SEQS[s] // self.dil
        self.banded = length > P
        self.keys = 2 if self.banded else 1
        self.subs = self.dil if self.banded else 1
        self.tiles = length // P if self.banded else TILES[s]
        self.chunks = self.tiles + self.keys - 1
        self.halves = max(1, P // length)
        self.tile0 = before.tile0 + before.subs * before.tiles if before else 0
        self.chunk0 = before.chunk0 + before.subs * before.chunks if before else 0
        self.slot0 = ([before.slot0[b] + before.subs * before.in_slot(b) * before.halves for b in range(2)]
                      if before else [0, 0])
        self.strip0 = before.strip0 + (before.tiles if before.banded else 1) if before else 0

    def in_slot(self, b):
        return (self.chunks + 1 - b) // 2

    def tile(self, r, t):
        return r * self.tiles + t + self.tile0

    def chunk(self, r, k):
        return r * self.chunks + k + self.chunk0

    def slot_loads(self, r, half_k, b):
        return (r * self.in_slot(b) + half_k + 1) * self.halves + self.slot0[b]

    def tile_dmas(self, r, i):
        return (r * (self.tiles // 2) + i) * self.halves + self.tile0 // 2

    def token_rows(self, t_all, width):
        rows = t_all[TOK_BASE[self.s]:TOK_BASE[self.s] + SEQS[self.s], 0:width]
        if self.banded:
            return rows.rearrange("(t p r) n -> r t p n", p=P, r=self.dil)
        return rows.rearrange("(p t h) n -> t h p n", t=self.tiles, h=self.halves)

    def key_rows(self, t_all, width):
        if self.banded:
            reach = BAND * self.dil
            rows = t_all[KV_BASE[self.s] - reach:KV_BASE[self.s] + SEQS[self.s] + reach, 0:width]
            return rows.rearrange("(t p r) n -> r t p n", p=P, r=self.dil)
        rows = t_all[KV_BASE[self.s]:KV_BASE[self.s] + SEQS[self.s], 0:width]
        return rows.rearrange("(p t h) n -> t h p n", t=self.tiles, h=self.halves)

    def parts(self, rows, r, t, buf):
        if self.banded:
            r = ds(r, 1)
            src = rows[r, ds(t, 1), :, :].rearrange("a b p n -> p (a b n)")
            return [(src, buf)]
        n = P // self.halves
        return [(rows[ds(t, 1), h, :, :].rearrange("a p n -> p (a n)"), buf[h * n:(h + 1) * n, :])
                for h in range(self.halves)]


def attention_passes():
    passes = []
    for s in (1, 0):
        for pattern in range(len(DILATIONS)):
            passes.append(Pass(pattern, s, passes[-1] if passes else None))
    return passes


def for_tiles(eng, passes, start, body):
    start(passes[0], 0)
    for p, following in zip(passes, passes[1:] + [None]):
        def subsequence(r, after):
            if p.tiles > 2:
                with eng.Fori(0, p.tiles // 2 - 1) as i:
                    for u in range(2):
                        body(p, r, i, u, True, None)
            body(p, r, p.tiles // 2 - 1, 0, True, None)
            body(p, r, p.tiles // 2 - 1, 1, False, after)

        if p.subs > 1:
            with eng.Fori(0, p.subs - 1) as r:
                subsequence(r, (p, r + 1))
        subsequence(p.subs - 1, following and (following, 0))


def attention_phase(nc, sem, c, out_weights, scratch):
    passes = attention_passes()
    strips = passes[-1].strip0 + 1
    scale = DH ** -0.5
    with ExitStack() as stack:
        mem = Core(nc, stack, "attn")
        q_raw = [mem.sbuf(f"q_raw{u}", [P, D_ATTN]) for u in range(2)]
        k_raw = [mem.sbuf(f"k_raw{u}", [P, D_ATTN]) for u in range(2)]
        v = [mem.sbuf(f"v{u}", [P, HEADS * VW]) for u in range(2)]
        q_hi = [mem.sbuf(f"q_hi{u}", [P, HEADS // 2, P], F32R) for u in range(2)]
        q_lo = [mem.sbuf(f"q_lo{u}", [P, HEADS // 2, P], F32R) for u in range(2)]
        k_hi = mem.sbuf("k_hi", [P, HEADS // 2, 2, P], F32R)
        k_lo = mem.sbuf("k_lo", [P, HEADS // 2, 2, P], F32R)
        q_one = [mem.sbuf(f"q_one{u}", [P, HEADS // 2, P]) for u in range(2)]
        k_one = [mem.sbuf(f"k_one{u}", [P, HEADS // 2, P]) for u in range(2)]
        p_sb = [mem.sbuf(f"p_sb{u}", [P, 4, 2 * P]) for u in range(2)]
        pt_sb = [mem.sbuf(f"pt_sb{u}", [P, 4, 2 * P]) for u in range(2)]
        o_sb = [mem.sbuf(f"o_sb{u}", [P, HEADS, OW]) for u in range(2)]
        mask = mem.sbuf("mask", [P, strips, 2 * P], BF16)
        ident_b = mem.sbuf("ident_b", [P, P], BF16)
        s_ps = [mem.psum(f"s_ps{u}", [P, 4, 2 * P]) for u in range(2)]
        pt_ps = mem.psum("pt_ps", [P, 4, 2 * P])
        turn = mem.psum("turn", [P, 4, P])
        o_ps = mem.psum("o_ps", [P, 512])[:, 0:4 * VW].rearrange("p (x d) -> p x d", d=VW)
        block = stack.enter_context(nc.Block())

        def heads_of(jj, t):
            return t[:, 4 * jj:4 * jj + 4, :].rearrange("p (a b) d -> p b a d", b=2)

        def padded(steps):
            return steps + [lambda: None] * (6 - len(steps))

        def head(jj, x):
            return 4 * jj + 2 * (x % 2) + x // 2

        @block.gpsimd
        def _(pool):
            for name, n in (("a_q_turned", 4), ("a_k_turned", 4), ("a_scores", 8), ("a_p", 2), ("a_p_turned", 2),
                            ("a_o", 2), ("a_o_copied", 1)):
                give_credit(nc, c).then_inc(sem[name], n)
            for u in range(2):
                give_credit(nc, c).then_inc(sem["a_stored"][u], 16)
            nc.gpsimd.memset(ident_b[:, :], 0.0).then_inc(sem["a_mask_steps"], 1)
            nc.gpsimd.memset(mask[:, :, :], 0.0).then_inc(sem["a_mask_steps"], 1)
            pool.wait_ge(sem["a_mask_steps"], 2)
            nc.gpsimd.affine_select(out=ident_b[:, :], in_=ident_b[:, :], compare_op=ALU.not_equal, fill=1.0,
                                    base=0, pattern=[[-1, P]], channel_multiplier=1
                                    ).then_inc(sem["a_mask_steps"], 1)
            steps = 3
            for p in passes:
                rules = ()
                if p.banded:
                    rules = [(mask[:, p.strip0 + u:p.strip0 + p.tiles:2, (u + k) % 2 * P:((u + k) % 2 + 1) * P],
                              0, (-1, 1)[k], (1, -1)[k]) for u in range(2) for k in range(2)]
                elif p.halves == 1:
                    rules = [(mask[:, p.strip0:p.strip0 + 1, 0:P], BAND, by, -by) for by in (-1, 1)]
                else:
                    n = P // p.halves
                    for h in range(p.halves):
                        for other in range(p.halves):
                            if other != h:
                                pool.wait_ge(sem["a_mask_steps"], steps)
                                nc.gpsimd.memset(mask[h * n:(h + 1) * n, p.strip0, other * n:(other + 1) * n], NEG
                                                 ).then_inc(sem["a_mask_steps"], 1)
                                steps += 1
                for cut, base, by_query, by_key in rules:
                    pool.wait_ge(sem["a_mask_steps"], steps)
                    nc.gpsimd.affine_select(out=cut, in_=cut, compare_op=ALU.is_ge, fill=NEG, base=base,
                                            pattern=[[0, cut.shape[1]], [by_key, cut.shape[2]]],
                                            channel_multiplier=by_query).then_inc(sem["a_mask_steps"], 1)
                    steps += 1
                if p.banded:
                    pool.wait_ge(sem["a_mask_steps"], steps)
                    nc.gpsimd.memset(mask[:, p.strip0, 0:BAND], NEG).then_inc(sem["a_mask_steps"], 1)
                    pool.wait_ge(sem["a_mask_steps"], steps + 1)
                    nc.gpsimd.memset(mask[:, p.strip0 + p.tiles - 1, P - BAND:P], NEG
                                     ).then_inc(sem["a_mask_steps"], 1)
                    steps += 2
            c["a_mask_total"] = steps

            def load_v(p, r, k, half_k, b):
                opening = isinstance(k, int) and k < p.keys
                for h in range(2):
                    pool.wait_ge(sem["a_o"], p.tile(r, 0) * GROUP4 + 2 if opening else
                                 p.tile(r, k - 1) * GROUP4 + 2 * h)
                    cut = slice(h * HEADS // 2 * VW, (h + 1) * HEADS // 2 * VW)
                    for src, dst in p.parts(p.key_rows(scratch["v"][:, cut], HEADS // 2 * VW), r, k, v[b][:, cut]):
                        pool.dma_start(dst, src).then_inc(sem["a_v_in"][2 * h + b], 16)

            def start(p, r):
                for k in range(p.keys):
                    load_v(p, r, k, 0, k)

            def body(p, r, i, u, more, after):
                if more:
                    load_v(p, r, 2 * i + u + p.keys, i + (u + p.keys) // 2, (u + p.keys) % 2)
                if after:
                    start(*after)
                    if after[0] is not p:
                        for _ in range(2):
                            out_weights.load_and_split_next(pool)

            for_tiles(pool, passes, start, body)
            out_weights.finish_first_half(pool)

        @block.sync
        def _(sp):
            def q_free(p, r, t):
                sp.wait_ge(sem["a_q_turned"], p.tile(r, t) * 2 + 2)

            def load_q(p, r, t, u):
                for src, dst in p.parts(p.token_rows(scratch["q"], D_ATTN), r, t, q_raw[u][:, :]):
                    sp.dma_start(dst, src).then_inc(sem["a_q_in"][u], 16)

            def load_k(p, r, k, b, first=False):
                sp.wait_ge(sem["a_k_turned"], p.chunk(r, k) * 2 + (4 if first else 2))
                for src, dst in p.parts(p.key_rows(scratch["k"], D_ATTN), r, k, k_raw[b][:, :]):
                    sp.dma_start(dst, src).then_inc(sem["a_k_in"][b], 16)

            def start(p, r):
                load_k(p, r, 0, 0, first=True)
                q_free(p, r, 0)
                load_q(p, r, 0, 0)
                if p.banded:
                    load_k(p, r, 1, 1)

            def body(p, r, i, u, more, after):
                if more:
                    q_free(p, r, 2 * i + u + 1)
                    load_k(p, r, 2 * i + u + p.keys, (u + p.keys) % 2)
                    load_q(p, r, 2 * i + u + 1, 1 - u)
                if after:
                    start(*after)

            for_tiles(sp, passes, start, body)

        @block.tensor
        def _(pe):
            def turn_q(p, r, i, u, h):
                if h == 0:
                    pe.wait_ge(sem["a_q_in"][u], (p.tile_dmas(r, i) + p.halves) * 16)
                pe.wait_ge(sem["a_k_split"], p.chunk(r, 2 * i + u + p.keys - 1) * 2 + h + 1)
                for j in range(4):
                    last = nc.tensor.transpose(turn[:, j, :], q_raw[u][:, (4 * h + j) * P:(4 * h + j + 1) * P],
                                               c["ident"][:, :])
                last.then_inc(sem["a_q_turned"], 1)

            def turn_k(p, r, k, half_k, b, h, tile_before):
                if h == 0:
                    pe.wait_ge(sem["a_k_in"][b], p.slot_loads(r, half_k, b) * 16)
                if tile_before is not None:
                    pe.wait_ge(sem["a_q_split"], tile_before * 2 + h + 1)
                else:
                    pe.wait_ge(sem["a_k_split"], p.chunk(r, k) * 2 + h + 1)
                for j in range(4):
                    last = nc.tensor.transpose(turn[:, j, :], k_raw[b][:, (4 * h + j) * P:(4 * h + j + 1) * P],
                                               c["ident"][:, :])
                last.then_inc(sem["a_k_turned"], 1)

            def scores(p, r, i, u, jj):
                width = p.keys * P
                t = 2 * i + u
                n = p.tile(r, t) * GROUP4 + jj
                pe.wait_ge(sem["a_p"], n + 1)
                if jj % 2 == 0:
                    pe.wait_ge(sem["a_q_split"], p.tile(r, t) * 2 + jj // 2 + 1)
                    pe.wait_ge(sem["a_k_split"], p.chunk(r, t + p.keys - 1) * 2 + jj // 2 + 2)
                strip = ds(t + p.strip0, 1) if p.banded else slice(p.strip0, p.strip0 + 1)
                m = mask[:, strip, 0:width].to_broadcast([P, 2, width])
                for half in range(2):
                    nc.tensor.matmul(s_ps[jj % 2][:, 2 * half:2 * half + 2, 0:width], ident_b[:, :], m,
                                     start=True, stop=False)
                for a in range(2):
                    pair = 2 * jj + a
                    if p.banded:
                        terms = [(qs[u][:, pair, :], ks[:, pair, :, :].rearrange("p s n -> p (s n)"))
                                 for qs, ks in ((q_hi, k_hi), (q_hi, k_lo), (q_lo, k_hi))]
                    else:
                        terms = [(q_one[u][:, pair, :], k_one[u][:, pair, :])]
                    for x, (qs, ks) in enumerate(terms):
                        for half in range(2):
                            rows = slice(64 * half, 64 * half + 64)
                            last = nc.tensor.matmul(s_ps[jj % 2][:, 2 * half + a, 0:width], qs[rows, :],
                                                    ks[rows, :], start=False, stop=a == 1 and x == len(terms) - 1)
                last.then_inc(sem["a_scores"], 1)

            def turn_p(p, r, i, u, jj):
                n = p.tile(r, 2 * i + u) * GROUP4 + jj
                pe.wait_ge(sem["a_p"], n + 1 + 2)
                pe.wait_ge(sem["a_p_copied"], n + 1)
                for x in range(4):
                    for k in range(p.keys):
                        cut = slice(k * P, (k + 1) * P)
                        last = nc.tensor.transpose(pt_ps[:, x, cut], p_sb[jj % 2][:, x, cut], c["ident"][:, :])
                last.then_inc(sem["a_p_turned"], 1)

            def outputs(p, r, i, u, jj):
                n = p.tile(r, 2 * i + u) * GROUP4 + jj
                if jj % 2 == 0:
                    h, b = jj // 2, (u + p.keys - 1) % 2
                    pe.wait_ge(sem["a_v_in"][2 * h + b], p.slot_loads(r, i + (u + p.keys - 1) // 2, b) * 16)
                    if p.banded:
                        pe.wait_ge(sem["a_v_in"][2 * h + u], p.slot_loads(r, i, u) * 16)
                pe.wait_ge(sem["a_p_copied"], n + 1 + 1)
                pe.wait_ge(sem["a_o_copied"], n + 1)
                for x in range(4):
                    h = head(jj, x)
                    for k in range(p.keys):
                        last = nc.tensor.matmul(o_ps[:, x, :], pt_sb[jj % 2][:, x, k * P:(k + 1) * P],
                                                v[k if p.banded else u][:, h * VW:(h + 1) * VW],
                                                start=k == 0, stop=k == p.keys - 1)
                last.then_inc(sem["a_o"], 1)

            def opening(p, r):
                half_k = [lambda h=h: turn_k(p, r, 0, 0, 0, h, None) for h in range(2)] if p.banded else []
                last_k = p.keys - 1
                return half_k + [turn for h in range(2) for turn in (
                    lambda h=h: turn_q(p, r, 0, 0, h),
                    lambda h=h: turn_k(p, r, last_k, 0, last_k, h, p.tile(r, 0)))]

            def start(p, r):
                for turn_half in opening(p, r):
                    turn_half()
                pe.wait_ge(sem["a_mask_steps"], c["a_mask_total"])
                scores(p, r, 0, 0, 0)
                scores(p, r, 0, 0, 1)

            def body(p, r, i, u, more, after):
                tile = (p, r, i, u)
                nxt = (p, r, i + u, 1 - u)
                turn_p(*tile, 0)
                scores(*tile, 2)
                if more:
                    turn_q(*nxt, 0)
                turn_p(*tile, 1)
                outputs(*tile, 0)
                scores(*tile, 3)
                if more:
                    next_k = (p, r, 2 * i + u + p.keys, i + (u + p.keys) // 2, (u + p.keys) % 2)
                    next_tile = p.tile(r, 2 * i + u + 1)
                    turn_k(*next_k, 0, next_tile)
                    turn_p(*tile, 2)
                    outputs(*tile, 1)
                    turn_q(*nxt, 1)
                    scores(*nxt, 0)
                    turn_k(*next_k, 1, next_tile)
                    turn_p(*tile, 3)
                    outputs(*tile, 2)
                    scores(*nxt, 1)
                    outputs(*tile, 3)
                elif after:
                    first, second, third, fourth, fifth, sixth = padded(opening(*after))
                    first()
                    turn_p(*tile, 2)
                    second()
                    outputs(*tile, 1)
                    third()
                    turn_p(*tile, 3)
                    fourth()
                    outputs(*tile, 2)
                    scores(*after, 0, 0, 0)
                    fifth()
                    outputs(*tile, 3)
                    sixth()
                    scores(*after, 0, 0, 1)
                else:
                    turn_p(*tile, 2)
                    outputs(*tile, 1)
                    turn_p(*tile, 3)
                    outputs(*tile, 2)
                    outputs(*tile, 3)

            for_tiles(pe, passes, start, body)

        @block.scalar
        def _(act):
            def high_q(p, r, i, u, h):
                t = p.tile(r, 2 * i + u)
                act.wait_ge(sem["a_scores"], t * GROUP4 + 4)
                act.wait_ge(sem["a_q_turned"], t * 2 + h + 1 + 4)
                dst, src = ((q_hi[u][:, 4 * h:4 * h + 4, :], turn[:, :, :]) if p.banded else
                            (q_one[u][:, 4 * h:4 * h + 2, :], turn[:, 0:2, :]))
                nc.scalar.activation(dst, src, ACT.Copy, scale=scale).then_inc(sem["a_q_high"], 1)

            def high_k(p, r, k, b, h):
                opening = isinstance(k, int) and k < p.keys
                act.wait_ge(sem["a_scores"], p.tile(r, 0) * GROUP4 + 8 if opening else
                            p.tile(r, k - 1) * GROUP4 + 6 + 2 * h)
                act.wait_ge(sem["a_k_turned"], p.chunk(r, k) * 2 + h + 1 + 4)
                dst, src = ((k_hi[:, 4 * h:4 * h + 4, b, :], turn[:, :, :]) if p.banded else
                            (k_one[b][:, 4 * h:4 * h + 2, :], turn[:, 0:2, :]))
                nc.scalar.copy(dst, src).then_inc(sem["a_k_high"], 1)

            def exponentials(p, r, i, u, jj):
                width = p.keys * P
                n = p.tile(r, 2 * i + u) * GROUP4 + jj
                act.wait_ge(sem["a_max"], n + 1)
                act.wait_ge(sem["a_p_turned"], n + 1)
                for x in range(4):
                    h = head(jj, x)
                    last = nc.scalar.activation(p_sb[jj % 2][:, x, 0:width], s_ps[jj % 2][:, x, 0:width], ACT.Exp,
                                                bias=o_sb[u][:, h, VW:OW])
                last.then_inc(sem["a_p"], 1)

            def copy_o(p, r, i, u, jj):
                n = p.tile(r, 2 * i + u) * GROUP4 + jj
                act.wait_ge(sem["a_o"], n + 1 + 2)
                nc.scalar.copy(heads_of(jj, o_sb[u])[:, :, :, 0:VW],
                               o_ps[:, :, :].rearrange("p (b a) d -> p b a d", a=2)).then_inc(sem["a_o_copied"], 1)

            def store(p, r, i, u):
                o_rows = p.token_rows(scratch["o"][p.pattern], HEADS * OW)
                act.wait_ge(sem["a_o_copied"], (p.tile(r, 2 * i + u) + 1) * GROUP4 + 1)
                for dst, src in p.parts(o_rows, r, 2 * i + u, o_sb[u][:, :, :].rearrange("p h d -> p (h d)")):
                    act.dma_start(dst, src).then_inc(sem["a_stored"][u], 16)

            def opening(p, r):
                last_k = p.keys - 1
                half_k = [lambda h=h: high_k(p, r, 0, 0, h) for h in range(2)] if p.banded else []
                return half_k + [part for h in range(2) for part in (lambda h=h: high_q(p, r, 0, 0, h),
                                                                     lambda h=h: high_k(p, r, last_k, last_k, h))]

            def start(p, r):
                for part in opening(p, r):
                    part()
                exponentials(p, r, 0, 0, 0)
                exponentials(p, r, 0, 0, 1)

            def body(p, r, i, u, more, after):
                tile = (p, r, i, u)
                nxt = (p, r, i + u, 1 - u)
                if more:
                    high_q(*nxt, 0)
                exponentials(*tile, 2)
                copy_o(*tile, 0)
                if more:
                    next_k = (p, r, 2 * i + u + p.keys, (u + p.keys) % 2)
                    high_k(*next_k, 0)
                    exponentials(*tile, 3)
                    copy_o(*tile, 1)
                    high_q(*nxt, 1)
                    high_k(*next_k, 1)
                    exponentials(*nxt, 0)
                    copy_o(*tile, 2)
                    exponentials(*nxt, 1)
                    copy_o(*tile, 3)
                elif after:
                    first, second, third, fourth, fifth, sixth = padded(opening(*after))
                    first()
                    exponentials(*tile, 3)
                    second()
                    copy_o(*tile, 1)
                    third()
                    fourth()
                    copy_o(*tile, 2)
                    exponentials(*after, 0, 0, 0)
                    fifth()
                    copy_o(*tile, 3)
                    sixth()
                    exponentials(*after, 0, 0, 1)
                else:
                    exponentials(*tile, 3)
                    for jj in range(1, GROUP4):
                        copy_o(*tile, jj)
                store(*tile)

            for_tiles(act, passes, start, body)
            for u in range(2):
                p = passes[-1]
                act.wait_ge(sem["a_stored"][u], 16 * (p.tile_dmas(p.subs - 1, p.tiles // 2) + 1))

        @block.vector
        def _(dve):
            give_credit(nc, c, nc.vector).then_inc(sem["a_k_split"], 1)
            give_credit(nc, c, nc.vector).then_inc(sem["a_p_copied"], 1)
            def low_q(p, r, i, u, h):
                dve.wait_ge(sem["a_q_high"], p.tile(r, 2 * i + u) * 2 + h + 1)
                half = slice(4 * h, 4 * h + 4)
                if p.banded:
                    done = nc.vector.scalar_tensor_tensor(q_lo[u][:, half, :], turn[:, :, :], scale,
                                                          q_hi[u][:, half, :].bitcast(F32), ALU.mult,
                                                          ALU.subtract)
                else:
                    done = nc.vector.tensor_scalar(q_one[u][:, 4 * h + 2:4 * h + 4, :], turn[:, 2:4, :], scale,
                                                   None, ALU.mult)
                done.then_inc(sem["a_q_split"], 1)

            def low_k(p, r, k, b, h):
                dve.wait_ge(sem["a_k_high"], p.chunk(r, k) * 2 + h + 1)
                half = slice(4 * h, 4 * h + 4)
                if p.banded:
                    done = nc.vector.tensor_tensor(k_lo[:, half, b, :], turn[:, :, :],
                                                   k_hi[:, half, b, :].bitcast(F32), ALU.subtract)
                else:
                    done = nc.vector.tensor_copy(k_one[b][:, 4 * h + 2:4 * h + 4, :], turn[:, 2:4, :])
                done.then_inc(sem["a_k_split"], 1)

            def maximum(p, r, i, u, jj):
                width = p.keys * P
                n = p.tile(r, 2 * i + u) * GROUP4 + jj
                if jj == 0:
                    dve.wait_ge(sem["a_stored"][u], p.tile_dmas(r, i) * 16 + 16)
                dve.wait_ge(sem["a_scores"], n + 1 + 8)
                nc.vector.tensor_reduce(heads_of(jj, o_sb[u])[:, :, :, VW:OW],
                                        s_ps[jj % 2][:, :, 0:width].rearrange("p (b a) n -> p b a n", a=2),
                                        AX.X, ALU.max, negate=True).then_inc(sem["a_max"], 1)

            def copy_p(p, r, i, u, jj):
                width = p.keys * P
                n = p.tile(r, 2 * i + u) * GROUP4 + jj
                dve.wait_ge(sem["a_p_turned"], n + 1 + 2)
                dve.wait_ge(sem["a_o"], n + 1)
                nc.vector.tensor_copy(pt_sb[jj % 2][:, :, 0:width], pt_ps[:, :, 0:width]
                                      ).then_inc(sem["a_p_copied"], 1)

            def opening(p, r):
                last_k = p.keys - 1
                half_k = [lambda h=h: low_k(p, r, 0, 0, h) for h in range(2)] if p.banded else []
                return half_k + [part for h in range(2) for part in (lambda h=h: low_q(p, r, 0, 0, h),
                                                                     lambda h=h: low_k(p, r, last_k, last_k, h))]

            def start(p, r):
                for part in opening(p, r):
                    part()
                maximum(p, r, 0, 0, 0)
                maximum(p, r, 0, 0, 1)

            def body(p, r, i, u, more, after):
                tile = (p, r, i, u)
                nxt = (p, r, i + u, 1 - u)
                copy_p(*tile, 0)
                maximum(*tile, 2)
                if more:
                    low_q(*nxt, 0)
                copy_p(*tile, 1)
                maximum(*tile, 3)
                if more:
                    next_k = (p, r, 2 * i + u + p.keys, (u + p.keys) % 2)
                    low_k(*next_k, 0)
                    copy_p(*tile, 2)
                    low_q(*nxt, 1)
                    maximum(*nxt, 0)
                    low_k(*next_k, 1)
                    copy_p(*tile, 3)
                    maximum(*nxt, 1)
                elif after:
                    first, second, third, fourth, fifth, sixth = padded(opening(*after))
                    first()
                    copy_p(*tile, 2)
                    second()
                    third()
                    copy_p(*tile, 3)
                    fourth()
                    maximum(*after, 0, 0, 0)
                    fifth()
                    sixth()
                    maximum(*after, 0, 0, 1)
                else:
                    copy_p(*tile, 2)
                    copy_p(*tile, 3)

            for_tiles(dve, passes, start, body)


class OutWeights:

    def __init__(self, nc, stack, sem, c, w_out):
        mem = Core(nc, stack, "out_weights")
        self.nc, self.sem = nc, sem
        self.raw = mem.sbuf("raw", [P, 2, D])
        self.hi = [mem.sbuf("hi0", [P, D_SSD // P, D], F32R)]
        self.lo = [mem.sbuf("lo0", [P, D_SSD // P, D], F32R)]
        self.rows = w_out.rearrange("o (k p) n -> p (o k) n", p=P)
        self.one = c["one"][:, :]
        self.next = 0

    def load_and_split_next(self, pool):
        nc, sem, k = self.nc, self.sem, self.next
        if k == D_SSD // P:
            return
        raw = self.raw[:, k % 2, :]
        if k >= 2:
            pool.wait_ge(sem["first_w_split"], k - 1)
        pool.dma_start(raw, self.rows[:, k, :]).then_inc(sem["first_w_in"][k % 2], 16)
        pool.wait_ge(sem["first_w_in"][k % 2], 16 * (k // 2 + 1))
        nc.gpsimd.tensor_tensor(self.hi[0][:, k, :], raw, self.one.to_broadcast([P, D]), ALU.mult
                                ).then_inc(sem["first_w_hi"], 1)
        pool.wait_ge(sem["first_w_hi"], k + 1)
        nc.gpsimd.tensor_tensor(self.lo[0][:, k, :], raw, self.hi[0][:, k, :].bitcast(F32), ALU.subtract
                                ).then_inc(sem["first_w_split"], 1)
        self.next += 1

    def finish_first_half(self, pool):
        while self.next < D_SSD // P:
            self.load_and_split_next(pool)
        pool.wait_ge(self.sem["first_w_split"], D_SSD // P)


def output_phase(nc, sem, c, x_parts, y_parts, weights, norm_f, scratch):
    half_k = D_SSD // P
    with ExitStack() as stack:
        mem = Core(nc, stack, "output")
        w_hi = weights.hi + [mem.sbuf("w_hi1", [P, half_k, D], F32R)]
        w_lo = weights.lo + [mem.sbuf("w_lo1", [P, half_k, D], F32R)]
        w_ring, w_raw = 2, weights.raw
        mix_hi = [mem.sbuf(f"mix_hi{b}", [P, D], F32R) for b in range(2)]
        mix_lo = [mem.sbuf(f"mix_lo{b}", [P, D], F32R) for b in range(2)]
        parts = mem.sbuf("parts", [P, 3, HEADS, OW])
        gate = mem.sbuf("gate", [P, D])
        y_ssd = mem.sbuf("y_ssd", [P, 2, D])
        y_attn = mem.sbuf("y_attn", [P, 2, D])
        x_t = mem.sbuf("x_t", [P, 2, D])
        gain = mem.sbuf("gain", [P, D])
        square = mem.sbuf("square", [P, D])
        low = mem.sbuf("low", [P, 1, HEADS])
        share = mem.sbuf("share", [P, 3, HEADS])
        weight = mem.sbuf("weight", [P, 3, HEADS])
        over = mem.sbuf("over", [P, HEADS])
        ssum = mem.sbuf("ssum", [P, 2])
        root = mem.sbuf("root", [P, 2])
        rinv = mem.sbuf("rinv", [P, 2])
        tr = [mem.psum(f"tr{b}", [P, D]) for b in range(2)]
        out = [mem.psum(f"out{u}", [P, D]) for u in range(2)]
        block = stack.enter_context(nc.Block())

        def per_head(t, width):
            return t.rearrange("p (h o) -> p h o", o=1).to_broadcast([P, HEADS, width])

        def by_head(t):
            return t.rearrange("p (h d) -> p h d", d=DH)

        @block.gpsimd
        def _(pool):
            for name, n in (("e_turned", 2), ("e_products", 2)):
                give_credit(nc, c).then_inc(sem[name], n)
            for k in range(half_k):
                pool.wait_ge(sem["e_w_hi"], k + 1)
                nc.gpsimd.tensor_tensor(w_lo[1][:, k, :], w_raw[:, k % w_ring, :], w_hi[1][:, k, :].bitcast(F32),
                                        ALU.subtract).then_inc(sem["e_w_split"], 1)
            for y, first, tiles in y_parts:
                rows = y.rearrange("o (t u p) d -> (o t) u p d", u=2, p=P)
                with pool.Fori(0, tiles // 2) as i:
                    for u in range(2):
                        pool.wait_ge(sem["e_normed"], first + 2 * i + u + 1)
                        pool.dma_start(rows[ds(i, 1), u, :, :].rearrange("o p d -> p (o d)"), x_t[:, u, :]
                                       ).then_inc(sem["e_stored"][u], 16)
            for u in range(2):
                pool.wait_ge(sem["e_stored"][u], 16 * (NT // 2))

        @block.sync
        def _(sp):
            sp.dma_start(gain[:, :], norm_f.rearrange("(o d) -> o d", o=1).to_broadcast([P, D])).then_inc(sem["e_gain_in"], 16)
            y_rows = scratch["y_ssd"].rearrange("(c p) n -> c p n", p=P)
            o_rows = scratch["o"].rearrange("a (c p) n -> c p a n", p=P)
            gate_rows = scratch["za"].rearrange("(c p) n -> c p n", p=P)

            def load(rows, first, i, u, peeled=False):
                n = first + 2 * i + u
                at = ds(n, 1)
                if not peeled:
                    sp.wait_ge(sem["e_turned"], 2 * n)
                sp.dma_start(y_ssd[:, u, :], y_rows[at, :, :].rearrange("o p n -> p (o n)")
                             ).then_inc(sem["e_y_in"][u], 16)
                if not (peeled and u == 0):
                    sp.wait_ge(sem["e_merged"], n)
                sp.dma_start(parts[:, :, :, :].rearrange("p a h d -> p a (h d)"),
                             o_rows[at, :, :, :].rearrange("o p a n -> p (o a) n")).then_inc(sem["e_parts_in"], 16)
                sp.dma_start(gate[:, :], gate_rows[at, :, :].rearrange("o p n -> p (o n)")
                             ).then_inc(sem["e_parts_in"], 16)
                if not peeled:
                    sp.wait_ge(sem["e_stored"][u], 16 * (first // 2 + i))
                sp.dma_start(x_t[:, u, :], rows[ds(i, 1), u, :, :].rearrange("o p d -> p (o d)")
                             ).then_inc(sem["e_x_in"][u], 16)

            for x, first, tiles in x_parts:
                rows = x.rearrange("o (t u p) d -> (o t) u p d", u=2, p=P)
                if first == 0:
                    for u in range(2):
                        load(rows, first, 0, u, peeled=True)
                with sp.Fori(1 if first == 0 else 0, tiles // 2) as i:
                    for u in range(2):
                        load(rows, first, i, u)

        def for_tiles_ahead(eng, start, body):
            start()
            with eng.Fori(0, NT // 2 - 1) as i:
                for u in range(2):
                    body(2 * i + u, i, u, True)
            body(NT - 2, NT // 2 - 1, 0, True)
            body(NT - 1, NT // 2 - 1, 1, False)

        @block.tensor
        def _(pe):
            def turn(n, i, u, b):
                if b == 0:
                    pe.wait_ge(sem["e_y_in"][u], 16 * i + 16)
                else:
                    pe.wait_ge(sem["e_merged"], n + 1)
                pe.wait_ge(sem["e_split"], 2 * n + b + 1)
                src = (y_ssd, y_attn)[b]
                for k in range(half_k):
                    last = nc.tensor.transpose(tr[b][:, k * P:(k + 1) * P], src[:, u, k * P:(k + 1) * P],
                                               c["ident"][:, :])
                last.then_inc(sem["e_turned"], 1)

            def product(n, u, b):
                pe.wait_ge(sem["e_split"], 2 * n + b + 3)
                if b == 1:
                    pe.wait_ge(sem["e_w_split"], half_k)
                else:
                    pe.wait_ge(sem["e_added"], n + 1)
                for half in range(2):
                    cols = slice(half * CW, (half + 1) * CW)
                    for j, (lhs, rhs) in enumerate(((mix_hi, w_hi), (mix_hi, w_lo), (mix_lo, w_hi))):
                        for k in range(half_k):
                            last = nc.tensor.matmul(out[u][:, cols], lhs[b][:, k * P:(k + 1) * P],
                                                    rhs[b][:, k, cols], start=b == 0 and j == 0 and k == 0,
                                                    stop=b == 1 and j == 2 and k == half_k - 1)
                last.then_inc(sem["e_products"], 1)

            def start():
                turn(0, 0, 0, 0)

            def body(n, i, u, more):
                turn(n, i, u, 1)
                product(n, u, 0)
                if more:
                    turn(n + 1, i + u, 1 - u, 0)
                product(n, u, 1)

            for_tiles_ahead(pe, start, body)

        @block.scalar
        def _(act):

            def load_w(k):
                if k >= w_ring:
                    act.wait_ge(sem["e_w_split"], k - w_ring + 1)
                act.dma_start(w_raw[:, k % w_ring, :], weights.rows[:, half_k + k, :]).then_inc(sem["e_w_in"][k % w_ring], 16)

            def shares(n):
                act.wait_ge(sem["e_diff"], n + 1)
                act.wait_ge(sem["e_merge_steps"], 3 * n + 1)
                nc.scalar.activation(weight[:, :, :], share[:, :, :], ACT.Exp).then_inc(sem["e_shares"], 1)

            def high(n, b):
                act.wait_ge(sem["e_turned"], 2 * n + b + 1 + 2)
                act.wait_ge(sem["e_products"], 2 * n + b + 1)
                nc.scalar.copy(mix_hi[b][:, :], tr[b][:, :]).then_inc(sem["e_high"], 1)

            def norm(n, u):
                act.wait_ge(sem["e_added"], n + 1 + 2)
                nc.scalar.activation(square[:, :], x_t[:, u, :], ACT.Square, accum_out=ssum[:, u:u + 1]
                                     ).then_inc(sem["e_ssum"], 1)
                act.wait_ge(sem["e_ssum"], n + 1)
                nc.scalar.activation(root[:, u:u + 1], ssum[:, u:u + 1], ACT.Sqrt, scale=1.0 / D,
                                     bias=c["eps"][:, :]).then_inc(sem["e_root"], 1)

            def start():
                for k in range(w_ring - 1):
                    load_w(k)
                shares(0)
                high(0, 0)
                for k in range(half_k):
                    if k + w_ring - 1 < half_k:
                        load_w(k + w_ring - 1)
                    act.wait_ge(sem["e_w_in"][k % w_ring], 16 * (k // w_ring + 1))
                    nc.scalar.copy(w_hi[1][:, k, :], w_raw[:, k % w_ring, :]).then_inc(sem["e_w_hi"], 1)

            def body(n, i, u, more):
                high(n, 1)
                if more:
                    shares(n + 1)
                    high(n + 1, 0)
                norm(n, u)

            for_tiles_ahead(act, start, body)

        @block.vector
        def _(dve):
            give_credit(nc, c, nc.vector).then_inc(sem["e_split"], 2)
            give_credit(nc, c, nc.vector).then_inc(sem["e_added"], 2)
            give_credit(nc, c, nc.vector).then_inc(sem["e_diff_steps"], 1)
            give_credit(nc, c, nc.vector).then_inc(sem["e_merge_steps"], 1)
            dve.wait_ge(sem["e_gain_in"], 16)

            def low_part(n, b):
                dve.wait_ge(sem["e_high"], 2 * n + b + 1)
                nc.vector.tensor_tensor(mix_lo[b][:, :], tr[b][:, :], mix_hi[b][:, :].bitcast(F32), ALU.subtract
                                        ).then_inc(sem["e_split"], 1)

            def merge(n, u):
                dve.wait_ge(sem["e_parts_in"], 32 * n + 32)
                nc.vector.tensor_reduce(low[:, 0, :], parts[:, :, :, VW].rearrange("p a h -> p h a"), AX.X, ALU.min
                                        ).then_inc(sem["e_diff_steps"], 1)
                dve.wait_ge(sem["e_diff_steps"], n + 1 + 1)
                nc.vector.tensor_tensor(share[:, :, :], low[:, :, :].to_broadcast([P, 3, HEADS]),
                                        parts[:, :, :, VW], ALU.subtract).then_inc(sem["e_diff"], 1)
                dve.wait_ge(sem["e_shares"], n + 1)
                weights = weight[:, :, :].rearrange("p a (h o) -> p a h o", o=1)
                nc.vector.tensor_tensor(parts[:, :, :, 0:VW], parts[:, :, :, 0:VW],
                                        weights.to_broadcast([P, 3, HEADS, VW]), ALU.mult
                                        ).then_inc(sem["e_merge_steps"], 1)
                for a in range(2):
                    dve.wait_ge(sem["e_merge_steps"], 3 * n + a + 1 + 1)
                    nc.vector.tensor_tensor(parts[:, 0, :, 0:VW], parts[:, 0, :, 0:VW], parts[:, a + 1, :, 0:VW],
                                            ALU.add).then_inc(sem["e_merge_steps"], 1)
                dve.wait_ge(sem["e_merge_steps"], 3 * n + 3 + 1)
                nc.vector.reciprocal(over[:, :], parts[:, 0, :, DH]).then_inc(sem["e_over"], 1)
                dve.wait_ge(sem["e_turned"], 2 * n if not isinstance(n, int) or n else 2)
                nc.vector.tensor_tensor(by_head(y_attn[:, u, :]), parts[:, 0, :, 0:DH], by_head(gate[:, :]), ALU.mult
                                        ).then_inc(sem["e_gated"], 1)
                dve.wait_ge(sem["e_over"], n + 1)
                dve.wait_ge(sem["e_gated"], n + 1)
                nc.vector.tensor_tensor(by_head(y_attn[:, u, :]), by_head(y_attn[:, u, :]), per_head(over[:, :], DH),
                                        ALU.mult).then_inc(sem["e_merged"], 1)

            def residual(n, i, u):
                dve.wait_ge(sem["e_x_in"][u], 16 * i + 16)
                dve.wait_ge(sem["e_products"], 2 * n + 2 + 2)
                nc.vector.tensor_tensor(x_t[:, u, :], x_t[:, u, :], out[u][:, :], ALU.add
                                        ).then_inc(sem["e_added"], 1)

            def norm(n, u):
                dve.wait_ge(sem["e_root"], n + 1)
                nc.vector.reciprocal(rinv[:, u:u + 1], root[:, u:u + 1]).then_inc(sem["e_rinv"], 1)
                dve.wait_ge(sem["e_rinv"], n + 1)
                nc.vector.scalar_tensor_tensor(x_t[:, u, :], x_t[:, u, :], rinv[:, u:u + 1], gain[:, :],
                                               ALU.mult, ALU.mult).then_inc(sem["e_normed"], 1)

            def start():
                merge(0, 0)
                low_part(0, 0)

            def body(n, i, u, more):
                low_part(n, 1)
                if more:
                    merge(n + 1, 1 - u)
                    low_part(n + 1, 0)
                residual(n, i, u)
                norm(n, u)

            for_tiles_ahead(dve, start, body)


SEMAPHORES = (
    "ident_zeroed", "w_split", "out_ready", "w_hi_ready", "gain_in", "h_ready", "zero_set", "pads_stored",
    "tr_copied", "ssum_ready", "root_ready", "tr_ready", "rinv_ready", "turned", "ones_set", "rotated",
    "staged", "h_hi_ready", "h_split", "rope_in", "halo_set", "conv_turned", "conv_copied", "conv_done",
    "silu_done", "back_turned", "back_copied", "rows_in", "consts_turned", "consts_ready", "tap_done",
    "stats_in", "masks_set", "stats_act", "stats_dve", "sums_ready", "a_ready", "b_added", "b_state",
    "b_weighted", "b_kept", "f_consts", "f_off", "f_gated", "f_out", "f_spread_used", "f_seg_used",
    "f_m_ready", "f_off_used", "f_cb_masked", "f_added_used", "f_diag", "f_spread", "f_m_summed", "f_m_back",
    "f_scaled", "f_rest", "f_cb", "f_zeroed", "f_added", "f_norm_steps", "f_root", "f_m_part", "f_kept",
    "f_y_steps", "a_q_turned", "a_k_turned", "a_scores", "a_p", "a_p_turned", "a_o", "a_o_copied",
    "a_mask_steps", "a_k_split", "a_q_split", "a_p_copied", "a_q_high", "a_k_high", "a_max", "first_w_split",
    "first_w_hi", "e_turned", "e_products", "e_w_hi", "e_w_split", "e_normed", "e_gain_in", "e_merged",
    "e_parts_in", "e_split", "e_added", "e_diff", "e_merge_steps", "e_shares", "e_high", "e_ssum", "e_root",
    "e_diff_steps", "e_over", "e_gated", "e_rinv",
)
SLOT_SEMAPHORES = (
    "w_in", "x_in", "stored", "toks_stored", "raw_in", "chans_stored", "b_in", "b_stored", "f_bc_in", "f_in",
    "f_stored", "a_stored", "a_v_in", "a_q_in", "a_k_in", "first_w_in", "e_stored", "e_y_in", "e_x_in",
    "e_w_in",
)
RING_SIZES = {"a_v_in": 4, "b_in": 4}


def build(nc, t_in, y_parts):
    tokens = sum(SEQS)
    widths = {"q": D_ATTN, "k": D_ATTN, "v": HEADS * VW, "za": D_ATTN, "zs": D_SSD, "xbc": D_XBC, "dt": 2 * HEADS,
              "xb": D_SSD + GROUPS * NST, "y_ssd": D_SSD}
    scratch = {name: nc.dram_tensor(f"s_{name}", [KV_ROWS if name in ("k", "v") else tokens, width], F32).ap()
               for name, width in widths.items()}
    scratch["bct"] = nc.dram_tensor("s_bct", [2 * GROUPS * NST, tokens], F32).ap()
    scratch["states"] = nc.dram_tensor("s_states", [NT, P, D_SSD], F32).ap()
    scratch["o"] = nc.dram_tensor("s_o", [len(DILATIONS), tokens, HEADS * OW], F32).ap()
    params = {"dt_bias": (t_in["dt_bias_fwd"], t_in["dt_bias_bwd"]), "a_log": (t_in["a_log_fwd"], t_in["a_log_bwd"]),
              "d_skip": t_in["d_skip"], "norm_ssd": t_in["norm_ssd"]}
    x_parts = (t_in["x_prompt"], t_in["x_sample"])

    def with_tiles(arrays):
        return [(a, TOK_BASE[s] // P, TILES[s]) for s, a in enumerate(arrays)]

    with ExitStack() as stack:
        sem = {name: stack.enter_context(nc.semaphore(name)) for name in SEMAPHORES}
        for name in SLOT_SEMAPHORES:
            sem[name] = [stack.enter_context(nc.semaphore(f"{name}{u}"))
                         for u in range(RING_SIZES.get(name, 2))]
        c = {name: stack.enter_context(nc.sbuf_tensor(name, [P, width], F32))
             for name, width in (("ident", P), ("credit", 64), ("one", 1), ("eps", 1))}
        c["credit_column"] = itertools.count()
        make_constants(nc, sem, c)
        with ExitStack() as projection:
            hT = projection.enter_context(nc.sbuf_tensor("hT", [P, NT, KT, P], F32))
            weights = Weights(nc, projection, sem, c, t_in["w_in"])
            norm_phase(nc, sem, c, x_parts, t_in["norm_in"], hT, weights, scratch)
            project_phase(nc, sem, c, weights, t_in["rope"], hT, scratch)
        conv_phase(nc, sem, c, t_in["conv_w"], t_in["conv_b"], scratch)
        with ExitStack() as ssd:
            st = {name: ssd.enter_context(nc.sbuf_tensor(f"st_{name}", [P, NT, 2 * HEADS], F32))
                  for name in ("a", "dt", "decay", "entry", "total", "weight")}
            st["masks"] = ssd.enter_context(nc.sbuf_tensor("masks", [P, 4, P], F32))
            st["ones"] = ssd.enter_context(nc.sbuf_tensor("ones", [P, P], F32))
            ssd_stats_phase(nc, sem, c, params, scratch, st)
            backward_states_phase(nc, sem, c, scratch, st)
            ssd_phase(nc, sem, c, params, scratch, st)
        out_weights = OutWeights(nc, stack, sem, c, t_in["w_out"])
        attention_phase(nc, sem, c, out_weights, scratch)
        output_phase(nc, sem, c, with_tiles(x_parts), with_tiles(y_parts), out_weights, t_in["norm_f"], scratch)


def rope_table():
    half = DH // 2
    inv = np.float32(10000.0) ** (-np.arange(half, dtype=np.float32) * np.float32(2.0) / np.float32(DH))
    table = np.zeros((P, NT, 3, half), np.float32)
    for s in range(len(SEQS)):
        angles = np.arange(SEQS[s], dtype=np.float32)[:, None] * inv[None, :]
        first = TOK_BASE[s] // P
        for a, values in enumerate((np.cos(angles), -np.sin(angles), np.sin(angles))):
            table[:, first:first + TILES[s], a, :] = values.reshape(TILES[s], P, half).transpose(1, 0, 2)
    return table


def kernel(x_prompt, x_sample, w_in, conv_w, conv_b, dt_bias_fwd, dt_bias_bwd, a_log_fwd, a_log_bwd,
           d_skip, norm_ssd, norm_in, w_out, norm_f):
    import concourse.bacc as _bacc
    from concourse.bass_utils import run_bass_kernel_spmd as _run

    arrays = {"x_prompt": x_prompt, "x_sample": x_sample, "w_in": w_in, "conv_w": conv_w, "conv_b": conv_b,
              "dt_bias_fwd": dt_bias_fwd, "dt_bias_bwd": dt_bias_bwd, "a_log_fwd": a_log_fwd,
              "a_log_bwd": a_log_bwd, "d_skip": d_skip, "norm_ssd": norm_ssd, "norm_in": norm_in,
              "w_out": w_out, "norm_f": norm_f}
    arrays = {name: np.ascontiguousarray(a) for name, a in arrays.items()}
    arrays["rope"] = rope_table()
    nc = _bacc.Bacc("TRN2", target_bir_lowering=False, num_devices=1)
    t_in = {name: nc.dram_tensor(name, list(a.shape), F32, kind="ExternalInput").ap() for name, a in arrays.items()}
    y_parts = [nc.dram_tensor(name, [1, SEQS[s], D], F32, kind="ExternalOutput").ap()
               for s, name in enumerate(("y_prompt", "y_sample"))]
    build(nc, t_in, y_parts)
    r = _run(nc, [arrays], core_ids=[0])
    return r.results[0]["y_prompt"], r.results[0]["y_sample"]
```
